# Optimizing a Trainium2 kernel written in Bass

```python
import functools
import jax, jax.numpy as jnp
from jax import lax
import numpy as np

D_MODEL = 1024
BATCH = 1
SEQ = 512
DEPTH = 1
DEC_BATCH = 8
DEC_SEQ = 1
PAST_LEN = 4096
PAGE_SIZE = 128

MIX_WIDTH = D_MODEL
LRU_WIDTH = MIX_WIDTH // 2
LRU_HEADS = 8
LRU_HEAD_DIM = LRU_WIDTH // LRU_HEADS
CONV_WIDTH = 4
LRU_C = 8.0
MLA_WIDTH = MIX_WIDTH - LRU_WIDTH
MLA_HEADS = 8
QK_NOPE_DIM = 64
QK_ROPE_DIM = 32
QK_HEAD_DIM = QK_NOPE_DIM + QK_ROPE_DIM
V_HEAD_DIM = MLA_WIDTH // MLA_HEADS
Q_LORA_RANK = 256
KV_LORA_RANK = 128
ROPE_THETA = 10000.0
ATTN_SCALE = QK_HEAD_DIM ** -0.5
D_FF = 2816
FFN_CONV_WIDTH = 3
Q_BLOCK = 128
EPS = 1e-6
IN_COLS = 2 * LRU_WIDTH + Q_LORA_RANK + KV_LORA_RANK + QK_ROPE_DIM
IN_SPLITS = (LRU_WIDTH, 2 * LRU_WIDTH, 2 * LRU_WIDTH + Q_LORA_RANK,
             2 * LRU_WIDTH + Q_LORA_RANK + KV_LORA_RANK)

kernel_name = 'hymba_rglru_mla_convffn_adaln_step'

def rms_norm(x, g):
    xf = x.astype(jnp.float32)
    y = xf * lax.rsqrt(jnp.mean(xf * xf, axis=-1, keepdims=True) + EPS)
    return (y * g.astype(jnp.float32)).astype(x.dtype)

def rope_cos_sin(pos):
    inv = ROPE_THETA ** (-jnp.arange(0, QK_ROPE_DIM, 2, dtype=jnp.float32) / QK_ROPE_DIM)
    ang = pos.astype(jnp.float32)[:, None] * inv[None, :]
    return jnp.cos(ang), jnp.sin(ang)

def apply_rope(x, cos, sin):
    xf = x.astype(jnp.float32)
    half = QK_ROPE_DIM // 2
    x1, x2 = xf[..., :half], xf[..., half:]
    return jnp.concatenate([x1 * cos - x2 * sin, x2 * cos + x1 * sin], axis=-1).astype(x.dtype)

def causal_dwconv(x, buf, w, b):
    k = w.shape[0]
    s = x.shape[1]
    xx = jnp.concatenate([buf.astype(x.dtype), x], axis=1)
    out = b + xx[:, 0:s] * w[0]
    for j in range(1, k):
        out = out + xx[:, j:j + s] * w[j]
    return out, xx[:, xx.shape[1] - (k - 1):]

def rg_lru(x, pos, h0, w_a, b_a, w_x, b_x, lam):
    bsz, s, w = x.shape
    xh = x.reshape(bsz, s, LRU_HEADS, LRU_HEAD_DIM)
    r = jax.nn.sigmoid((jnp.einsum('bshi,hij->bshj', xh, w_a).reshape(bsz, s, w) + b_a).astype(jnp.float32))
    i = jax.nn.sigmoid((jnp.einsum('bshi,hij->bshj', xh, w_x).reshape(bsz, s, w) + b_x).astype(jnp.float32))
    log_a = -LRU_C * r * jax.nn.softplus(-lam.astype(jnp.float32))
    a = jnp.exp(log_a)
    mult = jnp.sqrt(-jnp.expm1(2.0 * log_a))
    mult = jnp.where((pos == 0)[None, :, None], 1.0, mult)
    u = mult * i * x.astype(jnp.float32)

    def step(h, au):
        a_t, u_t = au
        h = a_t * h + u_t
        return h, h

    h_last, hs = lax.scan(step, h0.astype(jnp.float32), (jnp.swapaxes(a, 0, 1), jnp.swapaxes(u, 0, 1)))
    return jnp.swapaxes(hs, 0, 1).astype(x.dtype), h_last.astype(h0.dtype)

def mla_prompt_attention(q_nope, q_rope, kv_lat, k_rope, w_ukv, k_nope_g):
    bsz, s = q_nope.shape[:2]
    kv = (kv_lat @ w_ukv).reshape(bsz, s, MLA_HEADS, QK_NOPE_DIM + V_HEAD_DIM)
    k_nope = rms_norm(kv[..., :QK_NOPE_DIM], k_nope_g)
    v = kv[..., QK_NOPE_DIM:]
    nb = s // Q_BLOCK
    key_pos = jnp.arange(s)
    neg = jnp.finfo(jnp.float32).min

    def to_blocks(t):
        return jnp.moveaxis(t.reshape(bsz, nb, Q_BLOCK, *t.shape[2:]), 1, 0)

    def one_block(args):
        qn, qr, blk = args
        q_pos = blk * Q_BLOCK + jnp.arange(Q_BLOCK)
        sc = (jnp.einsum('bqhd,bkhd->bhqk', qn, k_nope)
              + jnp.einsum('bqhd,bkd->bhqk', qr, k_rope)).astype(jnp.float32) * ATTN_SCALE
        sc = jnp.where(key_pos[None, :] <= q_pos[:, None], sc, neg)
        p = jax.nn.softmax(sc, axis=-1).astype(v.dtype)
        return jnp.einsum('bhqk,bkhd->bqhd', p, v)

    out = lax.map(one_block, (to_blocks(q_nope), to_blocks(q_rope), jnp.arange(nb)))
    return jnp.moveaxis(out, 0, 1).reshape(bsz, s, MLA_HEADS, V_HEAD_DIM)

def mla_sample_attention(q_nope, q_rope, kv_lat, k_rope, cache_lat, cache_kr, page_table, w_ukv, k_nope_g):
    n_past = page_table.shape[1] * PAGE_SIZE
    ds = q_nope.shape[1]
    key_pos = jnp.arange(n_past + ds)
    q_pos = n_past + jnp.arange(ds)
    mask = key_pos[None, :] <= q_pos[:, None]
    neg = jnp.finfo(jnp.float32).min

    def one_seq(args):
        qn, qr, lat_new, kr_new, pages = args
        lat = jnp.concatenate([cache_lat[pages].reshape(n_past, KV_LORA_RANK).astype(lat_new.dtype), lat_new], axis=0)
        kr = jnp.concatenate([cache_kr[pages].reshape(n_past, QK_ROPE_DIM).astype(kr_new.dtype), kr_new], axis=0)
        kv = (lat @ w_ukv).reshape(n_past + ds, MLA_HEADS, QK_NOPE_DIM + V_HEAD_DIM)
        k_nope = rms_norm(kv[..., :QK_NOPE_DIM], k_nope_g)
        v = kv[..., QK_NOPE_DIM:]
        sc = (jnp.einsum('qhd,khd->hqk', qn, k_nope)
              + jnp.einsum('qhd,kd->hqk', qr, kr)).astype(jnp.float32) * ATTN_SCALE
        sc = jnp.where(mask, sc, neg)
        p = jax.nn.softmax(sc, axis=-1).astype(v.dtype)
        return jnp.einsum('hqk,khd->qhd', p, v)

    return lax.map(one_seq, (q_nope, q_rope, kv_lat, k_rope, page_table))

def hybrid_layer(x, c, pos, lru_h0, lru_buf, ffn_buf, attend, lp):
    bsz, s, _ = x.shape
    mod = jnp.dot(jax.nn.silu(c), lp['w_ada']) + lp['b_ada']
    shift1, scale1, gate1, shift2, scale2, gate2 = jnp.split(mod[:, None, :], 6, axis=-1)

    h = rms_norm(x, lp['norm1_g']) * (1.0 + scale1) + shift1
    z = h @ lp['w_in']
    x_lru, g_lru, q_lat, kv_lat, k_rope = jnp.split(z, IN_SPLITS, axis=-1)

    x_conv, lru_buf_new = causal_dwconv(x_lru, lru_buf, lp['lru_conv_w'], lp['lru_conv_b'])
    hs, h_last = rg_lru(x_conv, pos, lru_h0, lp['lru_w_a'], lp['lru_b_a'], lp['lru_w_x'], lp['lru_b_x'], lp['lru_lambda'])
    lru_out = hs * jax.nn.gelu(g_lru)

    cos, sin = rope_cos_sin(pos)
    q = (rms_norm(q_lat, lp['q_lora_norm_g']) @ lp['w_uq']).reshape(bsz, s, MLA_HEADS, QK_HEAD_DIM)
    q_nope = rms_norm(q[..., :QK_NOPE_DIM], lp['q_nope_norm_g'])
    q_rope = apply_rope(rms_norm(q[..., QK_NOPE_DIM:], lp['q_rope_norm_g']), cos[:, None, :], sin[:, None, :])
    kv_lat = rms_norm(kv_lat, lp['kv_lora_norm_g'])
    k_rope = apply_rope(rms_norm(k_rope, lp['k_rope_norm_g']), cos, sin)
    attn = attend(q_nope, q_rope, kv_lat, k_rope).reshape(bsz, s, MLA_WIDTH)

    mixed = jnp.concatenate([rms_norm(lru_out, lp['lru_out_norm_g']),
                             rms_norm(attn, lp['mla_out_norm_g'])], axis=-1) @ lp['w_o']
    x = x + gate1 * mixed

    h2 = rms_norm(x, lp['norm2_g']) * (1.0 + scale2) + shift2
    up, ffn_buf_new = causal_dwconv(h2 @ lp['w_up'], ffn_buf, lp['ffn_conv_w'], lp['ffn_conv_b'])
    val, gt = jnp.split(up, 2, axis=-1)
    x = x + gate2 * ((jax.nn.gelu(gt) * val) @ lp['w_down'])
    return x, kv_lat, k_rope, h_last, lru_buf_new, ffn_buf_new

def setup_inputs(seed: int = 0) -> dict:
    key = jax.random.key(seed)
    ks = iter(jax.random.split(key, 48))
    f32 = jnp.float32

    def nrm(shape, scale=1.0):
        return jax.random.normal(next(ks), shape, f32) * scale

    def gain(shape):
        return 1.0 + 0.02 * nrm(shape)

    L = DEPTH
    n_pages = PAST_LEN // PAGE_SIZE
    n_pool = (DEC_BATCH * n_pages * 5) // 4

    x_prompt = nrm((BATCH, SEQ, D_MODEL))
    x_sample = nrm((DEC_BATCH, DEC_SEQ, D_MODEL))
    cache_kv_latent = nrm((L, n_pool, PAGE_SIZE, KV_LORA_RANK))
    cache_k_rope = nrm((L, n_pool, PAGE_SIZE, QK_ROPE_DIM))
    state_lru_h = nrm((L, DEC_BATCH, LRU_WIDTH), 0.5)
    state_lru_conv = nrm((L, DEC_BATCH, CONV_WIDTH - 1, LRU_WIDTH))
    state_ffn_conv = nrm((L, DEC_BATCH, FFN_CONV_WIDTH - 1, 2 * D_FF))
    perm = jax.random.permutation(next(ks), n_pool)
    page_table = perm[:DEC_BATCH * n_pages].reshape(DEC_BATCH, n_pages).astype(jnp.int32)
    c_prompt = nrm((BATCH, D_MODEL))
    c_sample = nrm((DEC_BATCH, D_MODEL))

    a0 = jax.random.uniform(next(ks), (L, LRU_WIDTH), f32, 0.9, 0.999)
    sg = a0 ** (1.0 / LRU_C)
    lru_lambda = jnp.log(sg) - jnp.log1p(-sg)

    return {
        'x_prompt': x_prompt,
        'x_sample': x_sample,
        'cache_kv_latent': cache_kv_latent,
        'cache_k_rope': cache_k_rope,
        'state_lru_h': state_lru_h,
        'state_lru_conv': state_lru_conv,
        'state_ffn_conv': state_ffn_conv,
        'page_table': page_table,
        'c_prompt': c_prompt,
        'c_sample': c_sample,
        'w_ada': nrm((L, D_MODEL, 6 * D_MODEL), 0.5 * D_MODEL ** -0.5),
        'b_ada': nrm((L, 6 * D_MODEL), 0.01),
        'norm1_g': gain((L, D_MODEL)),
        'w_in': nrm((L, D_MODEL, IN_COLS), D_MODEL ** -0.5),
        'lru_conv_w': nrm((L, CONV_WIDTH, LRU_WIDTH), CONV_WIDTH ** -0.5),
        'lru_conv_b': nrm((L, LRU_WIDTH), 0.01),
        'lru_w_a': nrm((L, LRU_HEADS, LRU_HEAD_DIM, LRU_HEAD_DIM), LRU_HEAD_DIM ** -0.5),
        'lru_b_a': nrm((L, LRU_WIDTH), 0.01),
        'lru_w_x': nrm((L, LRU_HEADS, LRU_HEAD_DIM, LRU_HEAD_DIM), LRU_HEAD_DIM ** -0.5),
        'lru_b_x': nrm((L, LRU_WIDTH), 0.01),
        'lru_lambda': lru_lambda,
        'q_lora_norm_g': gain((L, Q_LORA_RANK)),
        'w_uq': nrm((L, Q_LORA_RANK, MLA_HEADS * QK_HEAD_DIM), Q_LORA_RANK ** -0.5),
        'q_nope_norm_g': gain((L, QK_NOPE_DIM)),
        'q_rope_norm_g': gain((L, QK_ROPE_DIM)),
        'kv_lora_norm_g': gain((L, KV_LORA_RANK)),
        'k_rope_norm_g': gain((L, QK_ROPE_DIM)),
        'w_ukv': nrm((L, KV_LORA_RANK, MLA_HEADS * (QK_NOPE_DIM + V_HEAD_DIM)), KV_LORA_RANK ** -0.5),
        'k_nope_norm_g': gain((L, QK_NOPE_DIM)),
        'lru_out_norm_g': gain((L, LRU_WIDTH)),
        'mla_out_norm_g': gain((L, MLA_WIDTH)),
        'w_o': nrm((L, MIX_WIDTH, D_MODEL), MIX_WIDTH ** -0.5),
        'norm2_g': gain((L, D_MODEL)),
        'w_up': nrm((L, D_MODEL, 2 * D_FF), D_MODEL ** -0.5),
        'ffn_conv_w': nrm((L, FFN_CONV_WIDTH, 2 * D_FF), FFN_CONV_WIDTH ** -0.5),
        'ffn_conv_b': nrm((L, 2 * D_FF), 0.01),
        'w_down': nrm((L, D_FF, D_MODEL), D_FF ** -0.5),
    }

def reference(x_prompt, x_sample, cache_kv_latent, cache_k_rope, state_lru_h, state_lru_conv,
              state_ffn_conv, page_table, c_prompt, c_sample, w_ada, b_ada, norm1_g, w_in,
              lru_conv_w, lru_conv_b, lru_w_a, lru_b_a, lru_w_x, lru_b_x, lru_lambda,
              q_lora_norm_g, w_uq, q_nope_norm_g, q_rope_norm_g, kv_lora_norm_g, k_rope_norm_g,
              w_ukv, k_nope_norm_g, lru_out_norm_g, mla_out_norm_g, w_o, norm2_g, w_up,
              ffn_conv_w, ffn_conv_b, w_down):
    bsz, s = x_prompt.shape[:2]
    dbsz, ds = x_sample.shape[:2]
    pos_prompt = jnp.arange(s)
    pos_sample = PAST_LEN + jnp.arange(ds)
    dt = x_prompt.dtype

    y_p, y_s = x_prompt, x_sample
    outs_p = ([], [], [], [], [])
    outs_s = ([], [], [], [], [])
    for l in range(DEPTH):
        lp = dict(w_ada=w_ada[l], b_ada=b_ada[l], norm1_g=norm1_g[l], w_in=w_in[l],
                  lru_conv_w=lru_conv_w[l], lru_conv_b=lru_conv_b[l], lru_w_a=lru_w_a[l],
                  lru_b_a=lru_b_a[l], lru_w_x=lru_w_x[l], lru_b_x=lru_b_x[l], lru_lambda=lru_lambda[l],
                  q_lora_norm_g=q_lora_norm_g[l], w_uq=w_uq[l], q_nope_norm_g=q_nope_norm_g[l],
                  q_rope_norm_g=q_rope_norm_g[l], kv_lora_norm_g=kv_lora_norm_g[l],
                  k_rope_norm_g=k_rope_norm_g[l], lru_out_norm_g=lru_out_norm_g[l],
                  mla_out_norm_g=mla_out_norm_g[l], w_o=w_o[l], norm2_g=norm2_g[l], w_up=w_up[l],
                  ffn_conv_w=ffn_conv_w[l], ffn_conv_b=ffn_conv_b[l], w_down=w_down[l])
        attend_prompt = functools.partial(mla_prompt_attention, w_ukv=w_ukv[l], k_nope_g=k_nope_norm_g[l])
        attend_sample = functools.partial(mla_sample_attention, cache_lat=cache_kv_latent[l],
                                          cache_kr=cache_k_rope[l], page_table=page_table,
                                          w_ukv=w_ukv[l], k_nope_g=k_nope_norm_g[l])
        res_p = hybrid_layer(y_p, c_prompt, pos_prompt,
                             jnp.zeros((bsz, LRU_WIDTH), dt),
                             jnp.zeros((bsz, CONV_WIDTH - 1, LRU_WIDTH), dt),
                             jnp.zeros((bsz, FFN_CONV_WIDTH - 1, 2 * D_FF), dt),
                             attend_prompt, lp)
        res_s = hybrid_layer(y_s, c_sample, pos_sample, state_lru_h[l], state_lru_conv[l],
                             state_ffn_conv[l], attend_sample, lp)
        y_p, y_s = res_p[0], res_s[0]
        for j in range(5):
            outs_p[j].append(res_p[j + 1])
            outs_s[j].append(res_s[j + 1])

    kv_latent_prompt = jnp.stack(outs_p[0])
    k_rope_prompt = jnp.stack(outs_p[1])
    lru_h_prompt = jnp.stack(outs_p[2])
    lru_conv_prompt = jnp.stack(outs_p[3])
    ffn_conv_prompt = jnp.stack(outs_p[4])
    kv_latent_sample = jnp.stack(outs_s[0])
    k_rope_sample = jnp.stack(outs_s[1])
    lru_h_sample = jnp.stack(outs_s[2])
    lru_conv_sample = jnp.stack(outs_s[3])
    ffn_conv_sample = jnp.stack(outs_s[4])
    return (y_p, y_s, kv_latent_prompt, k_rope_prompt, lru_h_prompt, lru_conv_prompt, ffn_conv_prompt,
            kv_latent_sample, k_rope_sample, lru_h_sample, lru_conv_sample, ffn_conv_sample)


_drawn_inputs = setup_inputs


def setup_inputs(seed=0):
    import zlib

    import numpy as np

    out = dict(_drawn_inputs(seed))
    spreads = {}
    factors = {'lru_b_a': 36.325,
     'lru_b_x': 8.0,
     'q_lora_norm_g': 8.0,
     'q_nope_norm_g': 8.0,
     'q_rope_norm_g': 8.0,
     'kv_lora_norm_g': 3.033,
     'k_rope_norm_g': 3.117,
     'k_nope_norm_g': 8.0,
     'lru_out_norm_g': 33.547,
     'mla_out_norm_g': 29.414,
     'norm2_g': 7.508,
     'ffn_conv_b': 21.96}
    for name, (base, spread) in spreads.items():
        noise = np.random.default_rng([zlib.crc32(name.encode()), seed]).standard_normal(out[name].shape)
        drawn = base * np.exp(spread * noise) if base else spread * noise
        out[name] = __import__('jax').numpy.asarray(drawn.astype(out[name].dtype))
    for name, factor in factors.items():
        out[name] = (out[name] * factor).astype(out[name].dtype)
    return out
```

```python
from contextlib import ExitStack

import concourse.bass as bass
from concourse import mybir

F32 = mybir.dt.float32
I32 = mybir.dt.int32
ALU = mybir.AluOpType
ACT = mybir.ActivationFunctionType
AX = mybir.AxisListType
RMAX = bass.bass_isa.ReduceOp.max

P = 128
D = 1024
KT = D // P
NP, NS = 512, 8
T = NP + NS
H = T // 2
LT = 4
LW = LT * P
HEADS = 8
NOPE, ROPE, VD = 64, 32, 64
QK = NOPE + ROPE
KV = 128
QL = 256
IN = 2 * LW + QL + KV + ROPE
FF = 2816
FT = FF // P
PAGE = 128
PAGES = 32
POOL = 320
KTILES = PAGES + 1
EPS = 1e-6
SCALE = float(QK) ** -0.5
NEG = -1e30
LN2 = 0.6931471805599453

ROWS = {}
_r = 0
for _name, _n in (("b_ada", 48), ("norm1_g", 8), ("lru_conv_w", 16), ("lru_conv_b", 4), ("lru_b_a", 4), ("lru_b_x", 4),
                  ("lru_lambda", 4), ("q_lora_norm_g", 2), ("kv_lora_norm_g", 1), ("lru_out_norm_g", 4),
                  ("mla_out_norm_g", 4), ("norm2_g", 8), ("gq", 1), ("gk", 1)):
    ROWS[_name] = _r
    _r += _n
NROWS = _r

CC = {}
_c = 0
for _name, _n in (("ident", P), ("ones", P), ("blk", P), ("perm", QK), ("mask", P), ("spread", P), ("cos", T),
                  ("sin", T), ("tail", 1)):
    CC[_name] = _c
    _c += _n
NCONST = _c


def constants():
    import numpy as np
    c = np.zeros((P, NCONST), np.float32)
    c[:, CC["ident"]:CC["ident"] + P] = np.eye(P)
    c[:, CC["ones"]:CC["ones"] + P] = 1.0
    blk = np.zeros((QK, QK), np.float32)
    blk[:NOPE, :NOPE] = 1.0 / NOPE
    blk[NOPE:, NOPE:] = 1.0 / ROPE
    c[:QK, CC["blk"]:CC["blk"] + QK] = blk
    half = ROPE // 2
    for m in range(half):
        c[NOPE + half + m, CC["perm"] + NOPE + m] = -1.0
        c[NOPE + m, CC["perm"] + NOPE + half + m] = 1.0
    q = np.arange(P)
    c[:, CC["mask"]:CC["mask"] + P] = np.where(q[None, :] <= q[:, None], 0.0, NEG)
    for j in range(4):
        for d in range(ROPE):
            c[NOPE + d, CC["spread"] + ROPE * j + d] = 1.0
    inv = (np.float32(10000.0) ** (-np.arange(0, ROPE, 2, dtype=np.float32) / np.float32(ROPE))).astype(np.float32)
    pos = np.concatenate([np.arange(NP), np.full(NS, PAGES * PAGE)]).astype(np.float32)
    ang = (pos[None, :] * inv[:, None]).astype(np.float32)
    c[NOPE:NOPE + half, CC["cos"]:CC["cos"] + T] = np.cos(ang)
    c[NOPE + half:QK, CC["cos"]:CC["cos"] + T] = np.cos(ang)
    c[NOPE:NOPE + half, CC["sin"]:CC["sin"] + T] = np.sin(ang)
    c[NOPE + half:QK, CC["sin"]:CC["sin"] + T] = np.sin(ang)
    c[1:, CC["tail"]] = NEG
    return c


class Steps:

    def __init__(self, eng, sem):
        self.eng, self.sem, self.n, self.base = eng, sem, 0, 0

    def did(self, ins):
        ins.then_inc(self.sem, 1)
        self.n += 1
        return self.base + self.n

    def need(self, v):
        self.eng.wait_ge(self.sem, v)

    def seq(self, ins):
        self.need(self.did(ins))

    def enter(self, i, per):
        self.start, self.base, self.n, self.per = self.n, self.n + i * per, 0, per

    def leave(self, laps):
        assert self.n == self.per, (self.n, self.per)
        self.n, self.base = self.start + laps * self.per, 0


J_PAR = 0
J_XT = J_PAR + 4
J_ADA1 = J_XT + KT
J_N1 = J_ADA1 + 8
J_WIN = J_N1 + 1
J_GATE = J_WIN + 12
J_NQ = J_GATE + 8
J_NKV = J_NQ + 1
J_KR = J_NKV + 1
J_NLRU = J_KR + 2
J_LOUT = J_NLRU + 1
J_ADA2 = J_LOUT + 7
J_HEAD = J_ADA2 + 16


POFF = [0, P, 3 * P, 6 * P]
TOFF = [0, 4 * P, 7 * P, 9 * P]


class HeadJobs:

    def __init__(self, e):
        b = J_HEAD + 7 * e
        self.q, self.qms, self.qrot, self.kn, self.kms, self.vw, self.qa = range(b, b + 7)
        self.s = [J_HEAD + 14 + 4 * e + n for n in range(4)]
        self.p = [J_HEAD + 22 + 4 * e + n for n in range(4)]
        self.pv = J_HEAD + 30 + e


HEAD_LAP = 32
J_SPREAD = J_HEAD + HEAD_LAP * (HEADS // 2)
J_DEC = J_SPREAD + 1
NG = 9
UNIT = 36
PV_AT = 5


def unit_jobs():
    order = [("t", 0)]
    for g in range(NG):
        if g + 1 < NG:
            order.append(("t", g + 1))
        order.append(("k0", g))
        if g < NG - 1:
            order.append(("k1", g))
        order.append(("s", g))
        if g == PV_AT:
            order.append(("pv", 0))
    assert len(order) == UNIT
    return {x: n for n, x in enumerate(order)}


UJ = unit_jobs()
J_UNIT1 = J_DEC + UNIT - 1
J_PVLAST = J_UNIT1 + UNIT * (NS - 1)
J_VP = J_PVLAST + 1
J_NMLA = J_VP + 1
J_WO = J_NMLA + 1
J_N2 = J_WO + KT
J_FST = J_N2 + 1
J_UP = J_FST + 1
J_DOWN = J_UP + 2 * FT
J_Y = J_DOWN + KT
J_FT = J_Y + 5


def build(nc, t):
    with ExitStack() as ctx:
        def sb(name, shape, dt=F32):
            return ctx.enter_context(nc.sbuf_tensor(name, shape, dt))

        def sem(name):
            return ctx.enter_context(nc.semaphore(name))

        cst = sb("cst", [P, NCONST])
        par_rows = sb("par_rows", [P, 3, P])
        par = sb("par", [P, NROWS])
        fpar = sb("fpar", [P, 4 * 2 * FT])
        xT = sb("xT", [P, KT, T])
        hT = sb("hT", [P, KT, T])
        sq = sb("sq", [P, KT, T])
        rs = sb("rs", [P, T])
        modT = sb("modT", [P, 48, 9])
        gmod = sb("gmod", [P, KT, 9])
        cT = sb("cT", [P, KT, 9])
        small = sb("small", [P, 64])
        RW = sb("RW", [P, 12288])
        RB = sb("RB", [P, 13200])
        ring = RW[:, 0:8192].rearrange("p (c k n) -> p c k n", c=4, k=KT)
        RA = RW[:, 8192:12288].rearrange("p (c k n) -> p c k n", c=4, k=KT)

        def sq_flat(a, n):
            return sq[:, :, :].rearrange("p k n -> p (k n)")[:, a:a + n]

        def C(name, w=P, rows=(0, P)):
            return cst[rows[0]:rows[1], CC[name]:CC[name] + w]

        ident, ones = C("ident"), C("ones")

        def pr(name, k=0, n=1, rows=(0, P)):
            return par[rows[0]:rows[1], ROWS[name] + k:ROWS[name] + k + n]

        x_tok = RB[:, 0:4 * D].rearrange("p (a d) -> p a d", a=4)
        xs_tok = RB[0:NS, 4 * D:5 * D]
        c_tok = RB[0:9, 5 * D:6 * D]
        c_th = RB[0:9, 6 * D:7 * D]
        st_tok = RB[0:24, 7 * D:7 * D + LW]
        h0_tok = RB[0:NS, 7 * D + LW:8 * D]
        o = 0

        def take(n):
            nonlocal o
            o += n
            assert o <= 13200, o
            return RB[:, o - n:o]

        XX = take(LT * (3 + T)).rearrange("p (t n) -> p t n", t=LT)
        GG = take(LT * T).rearrange("p (t n) -> p t n", t=LT)
        XC = take(LT * T).rearrange("p (t n) -> p t n", t=LT)
        TA = take(LT * T).rearrange("p (t n) -> p t n", t=LT)
        TI = take(LT * T).rearrange("p (t n) -> p t n", t=LT)
        AA = take(LT * T).rearrange("p (t n) -> p t n", t=LT)
        stT = sb("stT", [P, LT * 24])
        h0T = sb("h0T", [P, LT * NS])
        st4 = stT[:, :].rearrange("p (t b r) -> p t b r", t=LT, b=NS)
        h04 = h0T[:, :].rearrange("p (t b) -> p t b", t=LT)
        BD = sb("BD", [P, 2, LT, P])
        qlT = sb("qlT", [P, 2, T])
        kvT = sb("kvT", [P, T])
        krT = sb("krT", [P, T])
        qrot = sb("qrot", [P, T])
        otok = sb("otok", [P, 5, 160])
        lout = sb("lout", [16, 2, LW])

        o = 0
        hb = []
        for e in range(2):
            hb.append(dict(q=take(T), k=take(NP), p=take(10 * P), pt=take(10 * P), v=take(4 * VD), wt=take(P),
                           nm=take(4), l=take(4), rl=take(4), gq=take(NS)))
        wuq = sb("wuq", [P, 2, 2, QK])
        wukv = sb("wukv", [P, 2, P])
        QA = sb("QA", [P, NS, HEADS])
        QRS = sb("QRS", [P, NS, HEADS])
        QBD = sb("QBD", [P, NS, 4, HEADS])
        OL = sb("OL", [P, NS, HEADS])
        rden = sb("rden", [P, HEADS])[:, :]
        d8 = sb("d8", [P, KT, NS])
        wkn = sb("wkn", [P, HEADS * NOPE])
        ptab = sb("ptab", [1, NS * PAGES], I32)
        newrow = sb("newrow", [1, NS, KV + ROPE])
        o = 0
        latT = [take(4 * P) for _ in range(2)]
        krTt = [take(P) for _ in range(2)]
        sqd = [take(1024) for _ in range(2)]
        ssd = [take(KTILES * HEADS) for _ in range(2)]
        snd = [take(KTILES * HEADS) for _ in range(2)]
        srd = [take(KTILES * HEADS) for _ in range(2)]
        mx = [take(HEADS) for _ in range(2)]
        pd = [take(HEADS) for _ in range(2)]
        wv = take(HEADS * VD).rearrange("p (h d) -> p h d", h=HEADS)
        woR = RB[:, 13200 - 4096:13200].rearrange("p (c k n) -> p c k n", c=4, k=KT)
        assert o <= 13200 - 4096
        n_lat = KTILES * P
        n_kr = 36 * ROPE
        lat = [RW[:, e * n_lat:(e + 1) * n_lat].rearrange("p (c d) -> p c d", c=KTILES) for e in range(2)]
        kr_ = [RW[:, 2 * n_lat + e * n_kr:2 * n_lat + (e + 1) * n_kr].rearrange("p (c d) -> p c d", c=36) for e in range(2)]
        actT = RB[:, 0:FT * T].rearrange("p (m n) -> p m n", m=FT)
        wup = RW[:, 0:6144].rearrange("p (c k n) -> p c k n", c=3, k=2 * KT)
        wdn = RW[:, 6144:6144 + 2 * FT * P].rearrange("p (c k n) -> p c k n", c=2, k=FT)
        UW = 2 + T
        UU = [sq_flat(2 * UW * e, 2 * UW).rearrange("p (g n) -> p g n", g=2) for e in range(2)]
        CV = [sq_flat(4 * UW + T * g, T) for g in range(2)]
        GE = sq_flat(4 * UW + 2 * T, T)
        UT = sb("UT", [P, 2 * FT, 10])
        FS = sb("FS", [P, 2 * FT, 2 * NS])
        fs_tok = RB[0:2 * NS, 0:2 * FF]
        y_tok = [RB[:, D * n:D * n + D] for n in range(5)]
        ft_tok = RB[0:10, 6 * D:6 * D + 2 * FF]

        ps = [ctx.enter_context(nc.psum_tensor(f"ps{i}", [P, 2, 512], F32)) for i in range(4)]
        psum_full = [sem(f"psum_full{i}") for i in range(4)]
        psum_free = [sem(f"psum_free{i}") for i in range(4)]

        def halves(j, rows=(0, P)):
            return ps[j % 4][rows[0]:rows[1], :, 0:H]

        def flat(j):
            return ps[j % 4][:, :, :].rearrange("p a b -> p (a b)")

        def two(ap):
            return ap.rearrange("p (a n) -> p a n", a=2)

        s_cst = sem("consts_in")
        s_par = sem("params_in")
        s_x = sem("x_in")
        s_ada = [sem(f"w_ada_in{i}") for i in range(4)]
        s_hp = sem("h_scaled")
        s_hd = sem("h_decode_done")
        s_tiny = sem("mult_argument_done")
        s_win = [sem(f"w_in_in{i}") for i in range(4)]
        s_bd = sem("gate_weights_in")
        s_bdz = sem("gate_weights_cleared")
        s_parz = sem("param_rows_cleared")
        s_out = sem("outputs_stored")
        s_cT = sem("c_transposed_done")
        s_silu = sem("silu_c_done")
        s_sq = sem("squares_done")
        s_rs = sem("rstd_done")
        s_h = sem("normed_done")
        s_dve = sem("dve_steps")
        s_act2 = sem("key_ln_done")
        s_cvfree = sem("up_buffers_free")
        s_act = sem("act_steps")
        s_xt = sem("xT_done")
        s_mod = sem("modT_done")
        s_xc = sem("x_conv_done")
        s_ta = sem("tanh_a_done")
        s_ti = sem("tanh_x_done")
        s_lru = sem("lru_act_done")
        s_lrud = sem("lru_dve_done")
        s_sp = sem("softplus_done")
        s_ev = sem("act_evacuated")
        s_g = sem("gelu_done")
        s_kr = sem("k_rope_done")
        s_ql = sem("q_latent_normed")
        s_kvn = sem("kv_latent_normed")
        s_mix = sem("mixed_done")
        s_hw = [sem(f"head_weights_in{e}") for e in range(2)]
        s_wo = [sem(f"w_o_in{e}") for e in range(4)]
        s_qsq = sem("q_squares_done")
        s_qrs = sem("q_rstd_done")
        s_qn = sem("q_normed")
        s_qr = sem("q_rotated")
        s_ksq = sem("k_squares_done")
        s_krs = sem("k_rstd_done")
        s_kn = sem("k_head_done")
        s_gq = sem("q_times_k_gain_done")
        s_nm = sem("row_max_done")
        s_p = sem("exp_done")
        s_pn = sem("probs_normed")
        s_pt = sem("page_table_in")
        s_lat = [sem(f"cache_in{e}") for e in range(2)]
        s_new = sem("new_token_rows_in")
        s_newc = sem("new_token_tile_done")
        s_clr = sem("new_token_tiles_cleared")
        s_tT = sem("latents_transposed_copied")
        s_sqd = sem("key_squares_done")
        s_sqr = sem("key_squares_summed")
        s_drs = sem("key_rstd_done")
        s_mx = sem("partition_max_done")
        s_am = sem("all_max_done")
        s_sh = sem("scores_shifted")
        s_dp = sem("decode_probs_done")
        s_pd = sem("decode_prob_sums_done")
        s_wkn = sem("key_weights_in")
        s_krk = sem("rope_key_rows_set")
        s_msk = sem("scores_masked")
        s_ptc = sem("prob_blocks_copied")
        s_snc = sem("decode_scores_copied")
        s_sm = sem("decode_score_steps")
        s_rd = sem("decode_sum_inverted")
        s_d8 = sem("decode_residual_scaled")
        s_pads = sem("conv_pads_cleared")
        s_ut = sem("last_rows_kept")
        s_wv = sem("value_weights_in")
        s_qbd = sem("decode_rope_queries_done")
        s_x1 = sem("x1_done")
        s_wup = [sem(f"w_up_in{e}") for e in range(3)]
        s_wdn = [sem(f"w_down_in{e}") for e in range(2)]
        s_fst = sem("ffn_state_in")
        s_u = sem("up_evacuated")
        s_cv = sem("conv_done")
        s_ge = sem("gelu_gate_done")
        s_hid = sem("hidden_done")
        s_x2 = sem("x2_done")
        s_tok = sem("token_rows_done")

        def full(eng, j, lap=0):
            eng.wait_ge(psum_full[j % 4], j // 4 + 1 + lap)

        def claim(eng, j, lap=0):
            if j // 4 >= 1 or not isinstance(lap, int):
                eng.wait_ge(psum_free[j % 4], j // 4 + lap)

        def free_value(j, lap=0):
            return j // 4 + 1 + lap

        block = ctx.enter_context(nc.Block())

        @block.sync
        def _(sp):
            sp.dma_start(cst[:, :], t["consts"]).then_inc(s_cst, 16)
            x3 = t["x_prompt"].rearrange("b (a p) d -> p (b a) d", p=P)
            sp.dma_start(c_tok[0:1, :], t["c_prompt"]).then_inc(s_x, 16)
            sp.dma_start(c_tok[1:9, :], t["c_sample"]).then_inc(s_x, 16)
            sp.wait_ge(s_parz, 1)

            def rows(name, src, part=0):
                n = src.shape[0]
                sp.dma_start(par_rows[ROWS[name]:ROWS[name] + n, part, 0:src.shape[1]], src).then_inc(s_par, 16)

            for name in ("b_ada", "norm1_g", "lru_conv_b", "lru_b_a", "lru_b_x", "lru_lambda",
                         "q_lora_norm_g", "kv_lora_norm_g", "lru_out_norm_g", "mla_out_norm_g", "norm2_g"):
                rows(name, t[name].rearrange("l (r p) -> (l r) p", p=P))
            rows("lru_conv_w", t["lru_conv_w"].rearrange("l w (r p) -> (l w r) p", p=P))
            for name, a, b in (("gq", "q_nope_norm_g", "q_rope_norm_g"), ("gk", "k_nope_norm_g", "k_rope_norm_g")):
                r = ROWS[name]
                sp.dma_start(par_rows[r:r + 1, 0, 0:NOPE], t[a]).then_inc(s_par, 16)
                sp.dma_start(par_rows[r:r + 1, 0, NOPE:QK], t[b]).then_inc(s_par, 16)
            fw = t["ffn_conv_w"].rearrange("l w (r p) -> (l w r) p", p=P)
            sp.dma_start(par_rows[0:4 * FT, 1, :], fw[0:4 * FT, :]).then_inc(s_par, 16)
            sp.dma_start(par_rows[0:2 * FT, 2, :], fw[4 * FT:6 * FT, :]).then_inc(s_par, 16)
            sp.dma_start(par_rows[2 * FT:4 * FT, 2, :],
                         t["ffn_conv_b"].rearrange("l (r p) -> (l r) p", p=P)).then_inc(s_par, 16)
            sp.dma_start(st_tok, t["state_lru_conv"].rearrange("l b r w -> (l b r) w")).then_inc(s_par, 16)
            sp.dma_start(h0_tok, t["state_lru_h"].rearrange("l b w -> (l b) w")).then_inc(s_par, 16)
            sp.dma_start(xs_tok, t["x_sample"].rearrange("b s d -> (b s) d")).then_inc(s_x, 16)
            sp.dma_start(x_tok, x3).then_inc(s_x, 16)

            wa = t["w_ada"].rearrange("l (k p) (c n) -> p (l k) c n", p=P, n=256)
            for c in range(4):
                sp.dma_start(ring[:, c, :, :], wa[:, :, c, :]).then_inc(s_ada[c], 16)
            for c in range(4):
                full(sp, J_ADA1 + c)
                sp.dma_start(ring[:, c, :, :], wa[:, :, 4 + c, :]).then_inc(s_ada[c], 16)
            wi = t["w_in"].rearrange("l (k p) n -> p (l k) n", p=P)
            for m in range(12):
                w = P if m < 11 else ROPE
                if m >= 4:
                    full(sp, J_WIN + m - 4)
                sp.dma_start(RA[:, m % 4, :, 0:w], wi[:, :, P * m:P * m + w]).then_inc(s_win[m % 4], 16)
            sp.wait_ge(s_bdz, 1)
            for g, name in enumerate(("lru_w_a", "lru_w_x")):
                w = t[name].rearrange("l (t e) i j -> (l e) i t j", e=2)
                for e in range(2):
                    sp.dma_start(BD[64 * e:64 * e + 64, g, :, 64 * e:64 * e + 64], w[e]).then_inc(s_bd, 16)
            sp.dma_start(t["o_lru_conv_s"][0, :, 0:2, :], t["state_lru_conv"][0, :, 1:3, :]).then_inc(s_out, 16)
            sp.dma_start(t["o_ffn_conv_s"][0, :, 0:1, :], t["state_ffn_conv"][0, :, 1:2, :]).then_inc(s_out, 16)

            for a in range(5):
                sp.wait_ge(psum_free[(J_LOUT + a) % 4], free_value(J_LOUT + a))
            sp.dma_start(t["o_kv_p"].rearrange("l b (a p) d -> p (l b a) d", p=P), otok[:, 0:4, 0:KV]).then_inc(s_out, 16)
            sp.dma_start(t["o_kr_p"].rearrange("l b (a p) d -> p (l b a) d", p=P), otok[:, 0:4, KV:KV + ROPE]).then_inc(s_out, 16)
            sp.dma_start(t["o_kv_s"].rearrange("l b s d -> (l b s) d"), otok[0:NS, 4, 0:KV]).then_inc(s_out, 16)
            sp.dma_start(t["o_kr_s"].rearrange("l b s d -> (l b s) d"), otok[0:NS, 4, KV:KV + ROPE]).then_inc(s_out, 16)
            for a in range(5, 7):
                sp.wait_ge(psum_free[(J_LOUT + a) % 4], free_value(J_LOUT + a))
            sp.dma_start(t["o_lru_h_p"].rearrange("l b w -> (l b) w"), lout[0:1, 0, :]).then_inc(s_out, 16)
            sp.dma_start(t["o_lru_h_s"].rearrange("l b w -> (l b) w"), lout[1:9, 0, :]).then_inc(s_out, 16)
            sp.dma_start(t["o_lru_conv_p"].rearrange("l b r w -> (l b r) w"), lout[0:3, 1, :]).then_inc(s_out, 16)
            sp.dma_start(t["o_lru_conv_s"][0, :, 2, :], lout[3:11, 1, :]).then_inc(s_out, 16)
            for c in range(4):
                sp.dma_start(ring[:, c, :, :], wa[:, :, 8 + c, :]).then_inc(s_ada[c], 16)
            with sp.Fori(1, 4) as i:
                for c in range(4):
                    full(sp, J_ADA2 + c, i - 1)
                    sp.dma_start(ring[:, c, :, :], wa[:, :, bass.ds(8 + c + 4 * i, 1), :]).then_inc(s_ada[c], 16)
            sp.dma_start(ptab[:, :], t["page_table"].rearrange("b (o n) -> o (b n)", o=1)).then_inc(s_pt, 16)
            sp.dma_start(newrow[0:1, :, :], otok[0:NS, 4, :]).then_inc(s_new, 16)
            wq = t["w_uq"].rearrange("l (k p) (h n) -> p (l k) h n", p=P, h=HEADS)
            wk = t["w_ukv"].rearrange("l p (h n) -> p (l h) n", h=HEADS)

            def head_weights(e, h):
                sp.dma_start(wuq[:, e, :, :], wq[:, :, h, :]).then_inc(s_hw[e], 16)
                sp.dma_start(wukv[:, e, :], wk[:, h, :]).then_inc(s_hw[e], 16)

            sp.dma_start(wkn[:, :].rearrange("p (h n) -> p h n", h=HEADS),
                         t["w_ukv"][0].rearrange("p (h n) -> p h n", h=HEADS)[:, :, 0:NOPE]).then_inc(s_wkn, 16)
            for e in range(2):
                head_weights(e, bass.ds(e, 1))
            with sp.Fori(1, HEADS // 2) as i:
                for e in range(2):
                    full(sp, HeadJobs(e).qa, HEAD_LAP // 4 * (i - 1))
                    head_weights(e, bass.ds(2 * i + e, 1))
            cl = t["cache_kv_latent"].rearrange("l n p d -> p (l n) d")
            ck = t["cache_k_rope"].rearrange("l n p d -> p (l n) d")
            sp.wait_ge(s_pt, 16)

            def pages(e, s):
                with sp.Fori(0, PAGES) as n:
                    page = sp.value_load(ptab[0:1, bass.ds(PAGES * s + n, 1)], min_val=0, max_val=POOL - 1)
                    sp.dma_start(lat[e][:, bass.ds(n, 1), :], cl[:, bass.ds(page, 1), :]).then_inc(s_lat[e], 16)
                    sp.dma_start(kr_[e][:, bass.ds(n, 1), :], ck[:, bass.ds(page, 1), :]).then_inc(s_lat[e], 16)

            full(sp, J_ADA2 + 15)
            pages(0, 0)
            pages(1, 1)
            for n in range(2, NS):
                full(sp, J_UNIT1 + UNIT * (n - 2) + UJ["pv", 0])
                pages(n % 2, n)
            sp.dma_start(wv, t["w_ukv"][0].rearrange("p (h n) -> p h n", h=HEADS)[:, :, NOPE:]).then_inc(s_wv, 16)
            wo = t["w_o"].rearrange("l (k p) n -> p (l k) n", p=P)
            full(sp, J_SPREAD)
            for m in range(KT):
                if m >= 4:
                    full(sp, J_WO + m - 4)
                sp.dma_start(woR[:, m % 4, :, :], wo[:, :, P * m:P * m + P]).then_inc(s_wo[m % 4], 16)
            full(sp, J_PVLAST)
            wu = t["w_up"].rearrange("l (k p) (g n) -> p (l k) g n", p=P, g=2)

            def up_weights(c, m):
                for g in range(2):
                    sp.dma_start(wup[:, c, KT * g:KT * g + KT, :], wu[:, :, g, m]).then_inc(s_wup[c], 16)

            for m in range(2):
                up_weights(m, bass.ds(P * m, P))
            full(sp, J_WO + 7)
            sp.dma_start(fs_tok, t["state_ffn_conv"].rearrange("l b r w -> (l b r) w")).then_inc(s_fst, 16)
            wd = t["w_down"].rearrange("l (k p) n -> p (l k) n", p=P)
            for m in range(2):
                sp.dma_start(wdn[:, m, :, :], wd[:, :, P * m:P * m + P]).then_inc(s_wdn[m], 16)
            with sp.Fori(1, FT // 2) as i:
                for e in range(2):
                    full(sp, J_UP + 2 * e + 1, i - 1)
                    up_weights(e, bass.ds(2 * P * i + P * e, P))
            for m in range(2, KT):
                full(sp, J_DOWN + m - 2)
                sp.dma_start(wdn[:, m % 2, :, :], wd[:, :, P * m:P * m + P]).then_inc(s_wdn[m % 2], 16)
            for n in range(5):
                sp.wait_ge(psum_free[(J_Y + n) % 4], free_value(J_Y + n))
                if n < 4:
                    sp.dma_start(t["o_y_p"][0, P * n:P * n + P, :], y_tok[n]).then_inc(s_out, 16)
                else:
                    sp.dma_start(t["o_y_s"].rearrange("b s d -> (b s) d"), y_tok[n][0:NS, :]).then_inc(s_out, 16)
            for n in range(6):
                sp.wait_ge(psum_free[(J_FT + n) % 4], free_value(J_FT + n))
            sp.dma_start(t["o_ffn_conv_p"][0, 0, :, :], ft_tok[0:2, :]).then_inc(s_out, 16)
            sp.dma_start(t["o_ffn_conv_s"][0, :, 1, :], ft_tok[2:10, :]).then_inc(s_out, 16)
            sp.wait_ge(s_out, 16 * 17)

        @block.gpsimd
        def _(pool):
            nc.gpsimd.memset(par_rows[:, :, :], 0.0).then_inc(s_parz, 1)
            nc.gpsimd.memset(BD[:, :, :, :], 0.0).then_inc(s_bdz, 1)
            nc.gpsimd.memset(QBD[:, :, :, :], 0.0).then_inc(s_bdz, 1)
            full(pool, J_ADA2 + 15)
            for e in range(2):
                nc.gpsimd.memset(lat[e][:, PAGES, :], 0.0).then_inc(s_clr, 1)
                nc.gpsimd.memset(kr_[e][:, PAGES:36, :], 0.0).then_inc(s_clr, 1)
            pool.wait_ge(s_clr, 4)
            pool.wait_ge(s_new, 16)

            def new_tile(e, s):
                nc.gpsimd.tensor_copy(lat[e][0:1, PAGES, :], newrow[0:1, s, 0:KV]).then_inc(s_newc, 1)
                nc.gpsimd.tensor_copy(kr_[e][0:1, PAGES, :], newrow[0:1, s, KV:KV + ROPE]).then_inc(s_newc, 1)

            def all_max(e, v):
                pool.wait_ge(s_mx, v)
                nc.gpsimd.partition_all_reduce(mx[e], mx[e], P, RMAX).then_inc(s_am, 1)

            new_tile(0, 0)
            new_tile(1, 1)
            for n in range(2, NS):
                all_max(n % 2, n - 1)
                full(pool, J_UNIT1 + UNIT * (n - 2) + UJ["pv", 0])
                new_tile(n % 2, n)
            all_max(0, NS - 1)
            all_max(1, NS)
            with pool.Fori(0, FT // 2) as i:
                for e in range(2):
                    for g in range(2):
                        pool.wait_ge(psum_free[(J_UP + 2 * e + g) % 4], free_value(J_UP + 2 * e + g, i))
                        nc.gpsimd.tensor_copy(UT[:, bass.ds(FT * g + 2 * i + e, 1), :], UU[e][:, g, NP:UW]).then_inc(s_ut, 1)

        @block.tensor
        def _(pe):
            mm = nc.tensor.matmul

            def tr(out, in_, n):
                return nc.tensor.transpose(out, in_, ident[0:n, 0:n])

            def both(j, lhsT, src, start, stop, rows=(0, P), lap=0):
                for h in range(2):
                    last = mm(ps[j % 4][rows[0]:rows[1], h, 0:H], lhsT, src[:, h * H:(h + 1) * H], start=start, stop=stop)
                return last

            pe.wait_ge(s_cst, 16)
            pe.wait_ge(s_par, 16 * 21)
            tr(flat(0)[:, 0:NROWS], par_rows[0:NROWS, 0, :], NROWS).then_inc(psum_full[0], 1)
            tr(flat(1)[:, 0:88], par_rows[0:88, 1, :], 88)
            tr(flat(1)[:, 88:176], par_rows[0:88, 2, :], 88).then_inc(psum_full[1], 1)
            for k in range(LT):
                tr(flat(2)[:, 24 * k:24 * k + 24], st_tok[:, P * k:P * k + P], 24)
            for k in range(LT):
                last = tr(flat(2)[:, 96 + NS * k:96 + NS * k + NS], h0_tok[:, P * k:P * k + P], NS)
            last.then_inc(psum_full[2], 1)
            pe.wait_ge(s_silu, 2)
            for k in range(KT):
                last = tr(flat(3)[:, 9 * k:9 * k + 9], c_tok[:, P * k:P * k + P], 9)
            last.then_inc(psum_full[3], 1)
            pe.wait_ge(s_x, 64)
            for k in range(KT):
                j = J_XT + k
                claim(pe, j)
                for a in range(4):
                    tr(flat(j)[:, P * a:P * a + P], x_tok[:, a, P * k:P * k + P], P)
                tr(flat(j)[:, NP:T], xs_tok[:, P * k:P * k + P], NS).then_inc(psum_full[j % 4], 1)

            pe.wait_ge(psum_free[3], 1)
            for c in range(8):
                j = J_ADA1 + c
                claim(pe, j)
                pe.wait_ge(s_ada[c % 4], 16 * (c // 4 + 1))
                for m in range(2):
                    for k in range(KT):
                        last = mm(flat(j)[:, 9 * m:9 * m + 9], ring[:, c % 4, k, P * m:P * m + P], cT[:, k, :],
                                  start=(k == 0), stop=(k == KT - 1))
                last.then_inc(psum_full[j % 4], 1)

            def norm_sum(j, n, base, first=0):
                claim(pe, j)
                for k in range(n):
                    pe.wait_ge(s_sq, base + k + 1)
                    last = both(j, ones, sq[:, first + k, :], k == 0, k == n - 1)
                last.then_inc(psum_full[j % 4], 1)

            norm_sum(J_N1, KT, 0)
            for m in range(12):
                j = J_WIN + m
                rows = (0, P) if m < 11 else (NOPE, QK)
                w = P if m < 11 else ROPE
                claim(pe, j)
                pe.wait_ge(s_win[m % 4], 16 * (m // 4 + 1))
                for k in range(KT):
                    if m == 0:
                        pe.wait_ge(s_h, k + 1)
                        pe.wait_ge(s_hd, 1)
                    last = both(j, RA[:, m % 4, k, 0:w], hT[:, k, :], k == 0, k == KT - 1, rows)
                last.then_inc(psum_full[j % 4], 1)
            pe.wait_ge(s_bd, 64)
            for g in range(2):
                for k in range(LT):
                    j = J_GATE + g * LT + k
                    claim(pe, j)
                    pe.wait_ge(s_xc, k + 1)
                    both(j, BD[:, g, k, :], XC[:, k, :], True, True).then_inc(psum_full[j % 4], 1)
            norm_sum(J_NQ, 2, KT)
            norm_sum(J_NKV, 1, KT + 2, 2)
            R = (NOPE, QK)
            j = J_KR
            claim(pe, j)
            pe.wait_ge(s_sq, KT + 4)
            both(j, C("blk", QK, R)[:, NOPE:QK], sq[NOPE:QK, 3, :], True, True, R).then_inc(psum_full[j % 4], 1)
            j = J_KR + 1
            claim(pe, j)
            pe.wait_ge(s_kr, 1)
            both(j, C("perm", QK, R)[:, NOPE:QK], krT[NOPE:QK, :], True, True, R).then_inc(psum_full[j % 4], 1)
            norm_sum(J_NLRU, LT, KT + 4, 4)
            pe.wait_ge(s_kr, 2)
            pe.wait_ge(s_kvn, 1)
            for a in range(5):
                j = J_LOUT + a
                n = P if a < 4 else NS
                claim(pe, j)
                tr(flat(j)[0:n, 0:KV], kvT[:, P * a:P * a + n], P)
                mm(flat(j)[0:n, KV:KV + ROPE], krT[NOPE:QK, P * a:P * a + n], C("ident", QK, R)[:, NOPE:QK],
                   start=True, stop=True).then_inc(psum_full[j % 4], 1)
            pe.wait_ge(s_lrud, 1)
            for n, (src, c0, w) in enumerate(((TA, NP - 1, 9), (XX, NP, 11))):
                j = J_LOUT + 5 + n
                claim(pe, j)
                for k in range(LT):
                    last = tr(flat(j)[0:w, P * k:P * k + P], src[:, k, c0:c0 + w], P)
                last.then_inc(psum_full[j % 4], 1)

            with pe.Fori(0, 4) as i:
                for c in range(4):
                    j = J_ADA2 + c
                    claim(pe, j, i)
                    pe.wait_ge(s_ada[c], 48 + 16 * i)
                    for m in range(2):
                        for k in range(KT):
                            last = mm(flat(j)[:, 9 * m:9 * m + 9], ring[:, c, k, P * m:P * m + P], cT[:, k, :],
                                      start=(k == 0), stop=(k == KT - 1))
                    last.then_inc(psum_full[j % 4], 1)

            pe.wait_ge(s_ql, 2)
            with pe.Fori(0, HEADS // 2) as i:
                lap = HEAD_LAP // 4 * i
                for e in range(2):
                    J, b = HeadJobs(e), hb[e]
                    nth = 2 * i + e + 1
                    pe.wait_ge(s_hw[e], 32 * (i + 1))
                    claim(pe, J.q, lap)
                    for k in range(2):
                        last = both(J.q, wuq[:, e, k, :], qlT[:, k, :], k == 0, k == 1, (0, QK))
                    last.then_inc(psum_full[J.q % 4], 1)
                    claim(pe, J.qms, lap)
                    pe.wait_ge(s_qsq, nth)
                    both(J.qms, C("blk", QK, (0, QK)), sq[0:QK, 2 * e, :], True, True, (0, QK)).then_inc(psum_full[J.qms % 4], 1)
                    pe.wait_ge(s_cst, 16)
                    claim(pe, J.qrot, lap)
                    pe.wait_ge(s_qn, nth)
                    both(J.qrot, C("perm", QK, R)[:, NOPE:QK], b["q"][NOPE:QK, :], True, True, R).then_inc(psum_full[J.qrot % 4], 1)
                    claim(pe, J.kn, lap)
                    mm(flat(J.kn)[0:NOPE, 0:NP], wukv[:, e, 0:NOPE], kvT[:, 0:NP], start=True, stop=True).then_inc(psum_full[J.kn % 4], 1)
                    claim(pe, J.kms, lap)
                    pe.wait_ge(s_ksq, nth)
                    mm(flat(J.kms)[:, 0:NP], C("blk", P, (0, NOPE)), sq[0:NOPE, 4 + 2 * e, 0:NP], start=True,
                       stop=True).then_inc(psum_full[J.kms % 4], 1)
                    claim(pe, J.vw, lap)
                    for a in range(4):
                        mm(flat(J.vw)[:, VD * a:VD * a + VD], kvT[:, P * a:P * a + P], wukv[:, e, NOPE:P], start=True, stop=True)
                    tr(flat(J.vw)[0:NOPE, 512:512 + P], wukv[:, e, 0:NOPE], P).then_inc(psum_full[J.vw % 4], 1)
                    claim(pe, J.qa, lap)
                    pe.wait_ge(s_gq, nth)
                    pe.wait_ge(psum_free[J.vw % 4], free_value(J.vw, lap))
                    mm(flat(J.qa)[:, 0:NS], b["wt"][0:NOPE, :], b["gq"][0:NOPE, :], start=True, stop=True).then_inc(psum_full[J.qa % 4], 1)
                for e in range(2):
                    J, b = HeadJobs(e), hb[e]
                    nth = 2 * i + e + 1
                    pe.wait_ge(s_qr, nth)
                    pe.wait_ge(s_kn, nth)
                    for n in range(4):
                        claim(pe, J.s[n], lap)
                        mm(flat(J.s[n])[:, 0:P * (n + 1)], b["q"][0:QK, P * n:P * n + P], b["k"][0:QK, 0:P * (n + 1)],
                           start=True, stop=True).then_inc(psum_full[J.s[n] % 4], 1)
                for e in range(2):
                    J, b = HeadJobs(e), hb[e]
                    for n in range(4):
                        claim(pe, J.p[n], lap)
                        pe.wait_ge(s_pn, 8 * i + 4 * e + n + 1)
                        for a in range(n + 1):
                            last = tr(flat(J.p[n])[:, P * a:P * a + P], b["p"][:, POFF[n] + P * a:POFF[n] + P * a + P], P)
                        last.then_inc(psum_full[J.p[n] % 4], 1)
                for e in range(2):
                    J, b = HeadJobs(e), hb[e]
                    claim(pe, J.pv, lap)
                    for n in range(4):
                        pe.wait_ge(psum_free[J.p[n] % 4], free_value(J.p[n], lap))
                    for a in range(4):
                        last = mm(flat(J.pv)[VD * e:VD * e + VD, P * a:NP], b["v"][:, VD * a:VD * a + VD],
                                  b["pt"][:, TOFF[a]:TOFF[a] + NP - P * a], start=(a == 0), stop=(a == 3))
                    last.then_inc(psum_full[J.pv % 4], 1)

            j = J_SPREAD
            claim(pe, j)
            pe.wait_ge(s_qr, HEADS)
            mm(flat(j)[:, 0:NS * HEADS], C("spread", P, R), QRS[NOPE:QK, :, :], start=True, stop=True).then_inc(psum_full[j % 4], 1)
            pe.wait_ge(s_qbd, 1)
            pe.wait_ge(s_wkn, 16)

            def jobs_of(base, lap):
                return (lambda kind, g: base + UJ[kind, g] - (1 if base == J_DEC and UJ[kind, g] > UJ["pv", 0] else 0)), lap

            def pv(j, lap, e, v):
                claim(pe, j, lap)
                pe.wait_ge(s_pd, v)
                for n in range(KTILES):
                    mm(flat(j)[:, 0:HEADS], lat[e][:, n, :], snd[e][:, HEADS * n:HEADS * n + HEADS], start=(n == 0), stop=(n == KTILES - 1))
                mm(flat(j)[:, 512:512 + HEADS], ones, pd[e], start=True, stop=True).then_inc(psum_full[j % 4], 1)

            def unit(base, lap, e, s, v):
                jj, _ = jobs_of(base, lap)
                s_ = s if isinstance(s, int) else bass.ds(s, 1)

                def transposes(g):
                    j = jj("t", g)
                    claim(pe, j, lap)
                    if g == 0:
                        pe.wait_ge(s_lat[e], 512 * (v + 1 - e))
                    if g == NG - 1:
                        pe.wait_ge(s_newc, 2 * v)
                    for n in range(4 if g < NG - 1 else 1):
                        tr(flat(j)[:, P * n:P * n + P], lat[e][:, 4 * g + n, :], P)
                    tr(flat(j)[:, 512:512 + P], kr_[e][:, 4 * g:4 * g + 4, :].rearrange("p c d -> p (c d)"), P).then_inc(psum_full[j % 4], 1)

                transposes(0)
                for g in range(NG):
                    tiles = 4 if g < NG - 1 else 1
                    if g + 1 < NG:
                        transposes(g + 1)
                    pe.wait_ge(psum_free[jj("t", g) % 4], free_value(jj("t", g), lap))
                    for half in range(2 if tiles == 4 else 1):
                        j = jj(f"k{half}", g)
                        claim(pe, j, lap)
                        for n in range(min(2, tiles)):
                            c = 2 * half + n
                            last = mm(ps[j % 4][:, n, :], latT[g % 2][:, P * c:P * c + P], wkn[:, :], start=True, stop=True)
                        last.then_inc(psum_full[j % 4], 1)
                    j = jj("s", g)
                    claim(pe, j, lap)
                    for n in range(tiles):
                        mm(flat(j)[:, HEADS * n:HEADS * n + HEADS], latT[g % 2][:, P * n:P * n + P], QA[:, s_, :], start=True, stop=True)
                    mm(flat(j)[:, 512:512 + 4 * HEADS], krTt[g % 2], QBD[:, s_, :, :], start=True, stop=True).then_inc(psum_full[j % 4], 1)
                    if g == PV_AT and base != J_DEC:
                        pv(jj("pv", 0), lap, 1 - e, v - 1)

            unit(J_DEC, 0, 0, 0, 1)
            with pe.Fori(0, 3) as i:
                unit(J_UNIT1, 2 * UNIT // 4 * i, 1, 2 * i + 1, 2 * i + 2)
                unit(J_UNIT1 + UNIT, 2 * UNIT // 4 * i, 0, 2 * i + 2, 2 * i + 3)
            unit(J_UNIT1 + 6 * UNIT, 0, 1, 7, 8)
            pv(J_PVLAST, 0, 1, NS)
            j = J_VP
            claim(pe, j)
            pe.wait_ge(s_wv, 16)
            pe.wait_ge(psum_free[J_PVLAST % 4], free_value(J_PVLAST))
            for h in range(HEADS):
                last = mm(flat(j)[VD * (h % 2):VD * (h % 2) + VD, NS * (h // 2):NS * (h // 2) + NS], wv[:, h, :], OL[:, :, h], start=True, stop=True)
            last.then_inc(psum_full[j % 4], 1)
            norm_sum(J_NMLA, LT, KT + 8)
            for m in range(KT):
                j = J_WO + m
                claim(pe, j)
                pe.wait_ge(s_wo[m % 4], 16 * (m // 4 + 1))
                if m == 0:
                    pe.wait_ge(s_mix, 2 * LT)
                for k in range(KT):
                    last = both(j, woR[:, m % 4, k, :], hT[:, k, :], k == 0, k == KT - 1)
                last.then_inc(psum_full[j % 4], 1)
            norm_sum(J_N2, KT, KT + 12)
            j = J_FST
            claim(pe, j)
            pe.wait_ge(s_fst, 16)
            for m in range(2 * FT):
                last = tr(flat(j)[:, 2 * NS * m:2 * NS * m + 2 * NS], fs_tok[:, P * m:P * m + P], 2 * NS)
            last.then_inc(psum_full[j % 4], 1)
            pe.wait_ge(s_h, 2 * KT)
            pe.wait_ge(s_hd, 2)
            with pe.Fori(0, FT // 2) as i:
                for e in range(2):
                    pe.wait_ge(s_wup[e], 32 * (i + 1))
                    for g in range(2):
                        j = J_UP + 2 * e + g
                        claim(pe, j, i)
                        for k in range(KT):
                            last = both(j, wup[:, e, KT * g + k, :], hT[:, k, :], k == 0, k == KT - 1)
                        last.then_inc(psum_full[j % 4], 1)
            for m in range(KT):
                j = J_DOWN + m
                claim(pe, j)
                pe.wait_ge(s_wdn[m % 2], 16 * (m // 2 + 1))
                if m == 0:
                    pe.wait_ge(s_hid, FT)
                for k in range(FT):
                    last = both(j, wdn[:, m % 2, k, :], actT[:, k, :], k == 0, k == FT - 1)
                last.then_inc(psum_full[j % 4], 1)
            pe.wait_ge(s_x2, KT)
            for n in range(5):
                j = J_Y + n
                w = P if n < 4 else NS
                claim(pe, j)
                for k in range(KT):
                    last = tr(flat(j)[0:w, P * k:P * k + P], xT[:, k, P * n:P * n + w], P)
                last.then_inc(psum_full[j % 4], 1)
            for n in range(6):
                j = J_FT + n
                claim(pe, j)
                for m in range(8 * n, min(8 * n + 8, 2 * FT)):
                    last = tr(flat(j)[0:10, P * (m - 8 * n):P * (m - 8 * n) + P], UT[:, m, :], P)
                last.then_inc(psum_full[j % 4], 1)

        @block.scalar
        def _(act):
            A = nc.scalar.activation
            st = Steps(act, s_act)

            def rstd(j, width, rows=(0, P), lap=0, dst=None):
                full(act, j, lap)
                dst = rs[rows[0]:rows[1], :] if dst is None else dst
                A(two(dst), halves(j, rows), ACT.Ln, bias=epsc[rows[0]:rows[1], :], scale=1.0 / width).then_inc(psum_free[j % 4], 1)
                act.wait_ge(psum_free[j % 4], free_value(j, lap))
                return A(dst, dst, ACT.Exp, scale=-0.5)

            epsc = small[:, 0:1]
            act.wait_ge(s_x, 64)
            A(c_th, c_tok, ACT.Tanh, scale=0.5).then_inc(s_silu, 1)
            act.wait_ge(s_sp, 1)
            A(small[:, 8:12], small[:, 4:8], ACT.Exp, scale=-1.0).then_inc(s_sp, 1)
            for k in range(KT):
                j = J_XT + k
                full(act, j)
                A(xT[:, k, :], flat(j)[:, 0:T], ACT.Copy).then_inc(psum_free[j % 4], 1)
                act.wait_ge(psum_free[j % 4], free_value(j))
                A(sq[:, k, :], xT[:, k, :], ACT.Square).then_inc(s_sq, 1)
            rstd(J_N1, D).then_inc(s_rs, 1)
            for k in range(KT):
                act.wait_ge(s_hp, k + 1)
                A(hT[:, k, 0:NP], hT[:, k, 0:NP], ACT.Identity, bias=modT[:, k, 0:1], scale=gmod[:, k, 0:1]).then_inc(s_h, 1)
            for k in range(LT):
                j = J_WIN + LT + k
                full(act, j)
                A(two(GG[:, k, :]), halves(j), ACT.Gelu_apprx_tanh).then_inc(psum_free[j % 4], 1)
            for m, dst in ((8, qlT[:, 0, :]), (9, qlT[:, 1, :]), (10, kvT[:, :]), (11, krT[NOPE:QK, :])):
                j = J_WIN + m
                rows = (0, P) if m < 11 else (NOPE, QK)
                full(act, j)
                A(two(dst), halves(j, rows), ACT.Copy).then_inc(psum_free[j % 4], 1)
                act.wait_ge(psum_free[j % 4], free_value(j))
                A(sq[rows[0]:rows[1], m - 8, :], dst, ACT.Square).then_inc(s_sq, 1)
            act.wait_ge(s_sp, 3)
            for g, dst in ((0, TA), (1, TI)):
                for k in range(LT):
                    j = J_GATE + g * LT + k
                    full(act, j)
                    A(two(dst[:, k, :]), halves(j), ACT.Tanh, bias=small[:, 20 + 4 * g + k:21 + 4 * g + k],
                      scale=0.5).then_inc(psum_free[j % 4], 1)
            for k in range(LT):
                act.wait_ge(psum_free[(J_GATE + k) % 4], free_value(J_GATE + k))
            for k in range(LT):
                v = st.did(A(AA[:, k, :], TA[:, k, :], ACT.Exp, bias=small[:, 32 + k:33 + k], scale=small[:, 32 + k:33 + k]))
            st.need(v)
            for k in range(LT):
                A(TA[:, k, :], TA[:, k, :], ACT.Tanh, bias=small[:, 28 + k:29 + k], scale=small[:, 28 + k:29 + k]).then_inc(s_ta, 1)
            act.wait_ge(s_tiny, 1)
            st.did(A(sq[:, 4:8, :], TA[:, :, :], ACT.Ln, bias=1.0))
            st.seq(A(TA[:, :, :], TA[:, :, :], ACT.Ln)) 
            act.sem_inc(s_lru, 1)
            rstd(J_NQ, QL, dst=sq[:, 0, :]).then_inc(s_rs, 1)
            rstd(J_NKV, KV, dst=sq[:, 1, :]).then_inc(s_rs, 1)
            rstd(J_KR, 1, (NOPE, QK), dst=sq[NOPE:QK, 2, :]).then_inc(s_rs, 1)
            act.wait_ge(s_tiny, 2)
            A(TA[:, :, :], TA[:, :, :], ACT.Exp, scale=0.5).then_inc(s_lru, 1)
            act.wait_ge(s_lrud, 2)
            for k in range(LT):
                A(sq[:, 4 + k, :], XC[:, k, :], ACT.Square).then_inc(s_sq, 1)
            rstd(J_NLRU, LW).then_inc(s_rs, 1)

            def copy_out(j, dst, src, lap=0):
                full(act, j, lap)
                A(dst, src, ACT.Copy).then_inc(psum_free[j % 4], 1)
                act.wait_ge(psum_free[j % 4], free_value(j, lap))

            with act.Fori(0, HEADS // 2) as i:
                lap = HEAD_LAP // 4 * i
                for e in range(2):
                    J, b = HeadJobs(e), hb[e]
                    q, r = b["q"][0:QK, :], sq[0:QK, 2 * e + 1, :]
                    copy_out(J.q, two(q), halves(J.q, (0, QK)), lap)
                    A(sq[0:QK, 2 * e, :], q, ACT.Square).then_inc(s_qsq, 1)
                    rstd(J.qms, 1, (0, QK), lap, r).then_inc(s_qrs, 1)
                    k, r = b["k"][0:NOPE, :], sq[0:NOPE, 5 + 2 * e, 0:NP]
                    copy_out(J.kn, k, flat(J.kn)[0:NOPE, 0:NP], lap)
                    A(sq[0:NOPE, 4 + 2 * e, 0:NP], k, ACT.Square).then_inc(s_ksq, 1)
                    full(act, J.kms, lap)
                    A(r, flat(J.kms)[0:NOPE, 0:NP], ACT.Ln, bias=epsc[0:NOPE, :]).then_inc(psum_free[J.kms % 4], 1)
                    act.wait_ge(psum_free[J.kms % 4], free_value(J.kms, lap))
                    A(r, r, ACT.Exp, scale=-0.5).then_inc(s_krs, 1)
                for e in range(2):
                    J, b = HeadJobs(e), hb[e]
                    for n in range(4):
                        j = J.s[n]
                        act.wait_ge(s_nm, 8 * i + 4 * e + n + 1)
                        A(b["p"][:, POFF[n]:POFF[n] + P * (n + 1)], flat(j)[:, 0:P * (n + 1)], ACT.Exp,
                          bias=b["nm"][:, n:n + 1], scale=SCALE, accum_out=b["l"][:, n:n + 1]).then_inc(psum_free[j % 4], 1)

            def rstd_keys(e, v):
                act.wait_ge(s_sqr, 17 * v)
                A(ssd[e], ssd[e], ACT.Ln, bias=epsc, scale=1.0 / NOPE).then_inc(s_act2, 1)
                act.wait_ge(s_act2, v)
                A(ssd[e], ssd[e], ACT.Exp, scale=-0.5).then_inc(s_drs, 1)

            def probs(e, v):
                act.wait_ge(s_sh, v)
                A(snd[e], snd[e], ACT.Exp, scale=SCALE).then_inc(s_dp, 1)

            def unit(base, lap, e, v):
                jj = lambda kind, g: base + UJ[kind, g] - (1 if base == J_DEC and UJ[kind, g] > UJ["pv", 0] else 0)

                def latents(g):
                    j = jj("t", g)
                    full(act, j, lap)
                    n = 4 * P if g < NG - 1 else P
                    A(latT[g % 2][:, 0:n], flat(j)[:, 0:n], ACT.Copy).then_inc(s_tT, 1)
                    A(krTt[g % 2], flat(j)[:, 512:512 + P], ACT.Copy).then_inc(psum_free[j % 4], 1)

                latents(0)
                nth = 0
                for g in range(NG):
                    if g + 1 < NG:
                        latents(g + 1)
                    for half in range(2 if g < NG - 1 else 1):
                        j = jj(f"k{half}", g)
                        n = 2 if g < NG - 1 else 1
                        nth += 1
                        if base != J_DEC or nth > 2:
                            act.wait_ge(s_sqr, 17 * (v - 1) + nth - 2)
                        full(act, j, lap)
                        A(sqd[(nth + e) % 2][:, 0:512 * n], flat(j)[:, 0:512 * n], ACT.Square).then_inc(psum_free[j % 4], 1)
                    if base != J_DEC and g == 0:
                        rstd_keys(1 - e, v - 1)
                    if base != J_DEC and g == 3:
                        probs(1 - e, v - 1)

            unit(J_DEC, 0, 0, 1)
            with act.Fori(0, 3) as i:
                unit(J_UNIT1, 2 * UNIT // 4 * i, 1, 2 * i + 2)
                unit(J_UNIT1 + UNIT, 2 * UNIT // 4 * i, 0, 2 * i + 3)
            unit(J_UNIT1 + 6 * UNIT, 0, 1, 8)
            rstd_keys(1, NS)
            probs(1, NS)

            act.wait_ge(psum_free[J_VP % 4], free_value(J_VP))
            for k in range(LT):
                A(sq[:, k, :], hT[:, LT + k, :], ACT.Square).then_inc(s_sq, 1)
            act.wait_ge(s_mix, LT)
            rstd(J_NMLA, LW).then_inc(s_rs, 1)
            for k in range(KT):
                act.wait_ge(s_x1, k + 1)
                A(sq[:, k, :], xT[:, k, :], ACT.Square).then_inc(s_sq, 1)
            act.wait_ge(s_mix, 2 * LT)
            rstd(J_N2, D).then_inc(s_rs, 1)
            for k in range(KT):
                act.wait_ge(s_hp, KT + k + 1)
                A(hT[:, k, 0:NP], hT[:, k, 0:NP], ACT.Identity, bias=modT[:, 3 * KT + k, 0:1], scale=gmod[:, k, 0:1]).then_inc(s_h, 1)
            act.wait_ge(s_pads, 2)
            with act.Fori(0, FT // 2) as i:
                for e in range(2):
                    m = 2 * i + e
                    act.wait_ge(s_cvfree, m + 1)
                    for g in range(2):
                        j = J_UP + 2 * e + g
                        full(act, j, i)
                        A(two(UU[e][:, g, 2:UW]), halves(j), ACT.Copy).then_inc(psum_free[j % 4], 1)
                    act.wait_ge(s_cv, m + 1)
                    A(GE, CV[1], ACT.Gelu_apprx_tanh).then_inc(s_ge, 1)
            for n in (0, 2, 4):
                j = J_Y + n
                w = P if n < 4 else NS
                full(act, j)
                A(y_tok[n][0:w, :], flat(j)[0:w, :], ACT.Copy).then_inc(psum_free[j % 4], 1)

        @block.vector
        def _(dve):
            V = nc.vector
            st = Steps(dve, s_dve)
            MUL, ADD, SUB = ALU.mult, ALU.add, ALU.subtract

            def copy_out(j, dst, src, ready=None):
                full(dve, j)
                V.tensor_copy(dst, src).then_inc(psum_free[j % 4], 1)
                dve.wait_ge(psum_free[j % 4], free_value(j))

            st.did(V.memset(small[:, 0:1], EPS))
            st.did(V.memset(small[:, 1:2], 0.0))
            dve.wait_ge(s_silu, 1)
            V.scalar_tensor_tensor(c_tok, c_th, 1.0, c_tok, ADD, MUL).then_inc(s_silu, 1)
            copy_out(0, par[:, :], flat(0)[:, 0:NROWS])
            copy_out(1, fpar[:, :], flat(1)[:, 0:8 * FT])
            full(dve, 2)
            st.did(V.tensor_copy(stT[:, :], flat(2)[:, 0:96]))
            V.tensor_copy(h0T[:, :], flat(2)[:, 96:128]).then_inc(psum_free[2], 1)
            full(dve, 3)
            V.tensor_scalar(cT[:, :, :], flat(3)[:, 0:72].rearrange("p (k n) -> p k n", n=9), 0.5, None, MUL).then_inc(psum_free[3], 1)
            lam = pr("lru_lambda", 0, 4)
            st.seq(V.tensor_scalar(small[:, 36:40], lam, -1.0, None, MUL))
            V.tensor_tensor(small[:, 4:8], small[:, 36:40], lam, ALU.max).then_inc(s_sp, 1)
            dve.wait_ge(s_sp, 2)
            u, z, acc, z2 = small[:, 8:12], small[:, 12:16], small[:, 16:20], small[:, 40:44]
            st.seq(V.tensor_scalar(acc, u, 2.0, None, ADD))
            st.seq(V.reciprocal(acc, acc))
            st.seq(V.tensor_tensor(z, u, acc, MUL))
            st.seq(V.tensor_tensor(z2, z, z, MUL))
            st.seq(V.tensor_scalar(acc, z2, 2.0 / 17, 2.0 / 15, MUL, ADD))
            for n in range(6, -1, -1):
                st.seq(V.tensor_tensor(acc, acc, z2, MUL))
                st.seq(V.tensor_scalar(acc, acc, 2.0 / (2 * n + 1), None, ADD))
            st.seq(V.tensor_tensor(acc, acc, z, MUL))
            st.seq(V.tensor_scalar(small[:, 36:40], small[:, 36:40], 0.0, None, ALU.max))
            st.seq(V.tensor_tensor(acc, acc, small[:, 36:40], ADD))
            st.did(V.tensor_scalar(small[:, 28:32], acc, 4.0, None, MUL))
            st.did(V.tensor_scalar(small[:, 32:36], acc, -4.0, None, MUL))
            v = st.did(V.tensor_scalar(small[:, 20:24], pr("lru_b_a", 0, 4), 0.5, None, MUL))
            st.need(v)
            V.tensor_scalar(small[:, 24:28], pr("lru_b_x", 0, 4), 0.5, None, MUL).then_inc(s_sp, 1)
            for c in range(8):
                j = J_ADA1 + c
                full(dve, j)
                V.tensor_tensor(modT[:, 2 * c:2 * c + 2, :], flat(j)[:, 0:18].rearrange("p (m n) -> p m n", n=9),
                                pr("b_ada", 2 * c, 2).unsqueeze(2).to_broadcast([P, 2, 9]), ADD).then_inc(psum_free[j % 4], 1)
            for c in range(4, 8):
                dve.wait_ge(psum_free[(J_ADA1 + c) % 4], free_value(J_ADA1 + c))
            st.seq(V.tensor_scalar(gmod[:, :, :], modT[:, KT:2 * KT, :], 1.0, None, ADD))
            st.seq(V.tensor_tensor(gmod[:, :, :], gmod[:, :, :], pr("norm1_g", 0, KT).unsqueeze(2).to_broadcast([P, KT, 9]), MUL))
            dve.wait_ge(s_rs, 1)
            for k in range(KT):
                V.tensor_tensor(hT[:, k, :], xT[:, k, :], rs[:, :], MUL).then_inc(s_hp, 1)
            dve.wait_ge(s_hp, KT)
            st.seq(V.tensor_tensor(hT[:, :, NP:T], hT[:, :, NP:T], gmod[:, :, 1:9], MUL))
            V.tensor_tensor(hT[:, :, NP:T], hT[:, :, NP:T], modT[:, 0:KT, 1:9], ADD).then_inc(s_hd, 1)

            full(dve, J_WIN)
            v = st.did(V.memset(XX[:, :, 0:3], 0.0))
            for k in range(LT):
                j = J_WIN + k
                full(dve, j)
                V.tensor_copy(two(XX[:, k, 3:3 + T]), halves(j)).then_inc(psum_free[j % 4], 1)
            st.need(v)
            for tap in range(4):
                for k in range(LT):
                    w = pr("lru_conv_w", 4 * tap + k)
                    x = XX[:, k, tap:tap + NP]
                    if tap == 0:
                        dve.wait_ge(psum_free[(J_WIN + k) % 4], free_value(J_WIN + k))
                        v = st.did(V.tensor_scalar(XC[:, k, 0:NP], x, w, pr("lru_conv_b", k), MUL, ADD))
                    else:
                        v = st.did(V.scalar_tensor_tensor(XC[:, k, 0:NP], x, w, XC[:, k, 0:NP], MUL, ADD))
                st.need(v)
            dec, tmp = XC[:, :, NP:T], AA[:, :, 0:NS]
            for tap in range(4):
                w = pr("lru_conv_w", 4 * tap, 4).unsqueeze(2).to_broadcast([P, LT, NS])
                x = st4[:, :, :, tap] if tap < 3 else XX[:, :, 3 + NP:3 + T]
                st.seq(V.tensor_tensor(tmp, x, w, MUL))
                other = pr("lru_conv_b", 0, 4).unsqueeze(2).to_broadcast([P, LT, NS]) if tap == 0 else dec
                ins = V.tensor_tensor(dec, tmp, other, ADD)
                if tap < 3:
                    st.seq(ins)
                else:
                    ins.then_inc(s_xc, 4)
            for k in range(LT):
                j = J_GATE + LT + k
                dve.wait_ge(psum_free[j % 4], free_value(j))
            dve.wait_ge(s_xc, 4)
            v = st.did(V.scalar_tensor_tensor(TI[:, :, :], TI[:, :, :], 1.0, XC[:, :, :], ADD, MUL))
            dve.wait_ge(s_ta, 4)
            V.tensor_scalar(TA[:, :, :], TA[:, :, :], 1e-18, None, ALU.max).then_inc(s_tiny, 1)
            dve.wait_ge(s_lru, 1)
            V.scalar_tensor_tensor(TA[:, :, :], TA[:, :, :], LN2, sq[:, 4:8, :], ADD, SUB).then_inc(s_tiny, 1)
            dve.wait_ge(s_lru, 2)
            st.seq(V.memset(TA[:, :, 0:1], 1.0))
            st.seq(V.scalar_tensor_tensor(TI[:, :, :], TI[:, :, :], 0.5, TA[:, :, :], MUL, MUL))
            for k in range(LT):
                v = st.did(V.tensor_tensor_scan(TA[:, k, 0:NP], AA[:, k, 0:NP], TI[:, k, 0:NP], 0.0, MUL, ADD))
            v = st.did(V.tensor_tensor(TA[:, :, NP:T], AA[:, :, NP:T], h04, MUL))
            st.need(v)
            V.tensor_tensor(TA[:, :, NP:T], TA[:, :, NP:T], TI[:, :, NP:T], ADD).then_inc(s_lrud, 1)
            dve.wait_ge(s_lrud, 1)
            for k in range(LT):
                dve.wait_ge(psum_free[(J_WIN + LT + k) % 4], free_value(J_WIN + LT + k))
            V.tensor_tensor(XC[:, :, :], TA[:, :, :], GG[:, :, :], MUL).then_inc(s_lrud, 1)

            dve.wait_ge(s_rs, 2)
            for k in range(2):
                V.scalar_tensor_tensor(qlT[:, k, :], qlT[:, k, :], pr("q_lora_norm_g", k), sq[:, 0, :], MUL, MUL).then_inc(s_ql, 1)
            dve.wait_ge(s_rs, 3)
            V.scalar_tensor_tensor(kvT[:, :], kvT[:, :], pr("kv_lora_norm_g"), sq[:, 1, :], MUL, MUL).then_inc(s_kvn, 1)
            dve.wait_ge(s_rs, 4)
            R = (NOPE, QK)
            kr = krT[NOPE:QK, :]
            V.scalar_tensor_tensor(kr, kr, pr("gk", 0, 1, R), sq[NOPE:QK, 2, :], MUL, MUL).then_inc(s_kr, 1)
            dve.wait_ge(s_kr, 1)
            j = J_KR + 1
            full(dve, j)
            V.tensor_tensor(two(qrot[NOPE:QK, :]), halves(j, R), two(C("sin", T, R)), MUL).then_inc(psum_free[j % 4], 1)
            st.seq(V.tensor_tensor(kr, kr, C("cos", T, R), MUL))
            dve.wait_ge(psum_free[j % 4], free_value(j))
            V.tensor_tensor(kr, kr, qrot[NOPE:QK, :], ADD).then_inc(s_kr, 1)
            dve.wait_ge(s_rs, 5)
            for k in range(LT):
                V.scalar_tensor_tensor(hT[:, k, :], XC[:, k, :], pr("lru_out_norm_g", k), rs[:, :], MUL, MUL).then_inc(s_mix, 1)
            for a in range(5):
                j = J_LOUT + a
                n = P if a < 4 else NS
                full(dve, j)
                V.tensor_copy(otok[0:n, a, :], flat(j)[0:n, 0:KV + ROPE]).then_inc(psum_free[j % 4], 1)
            for n, w in enumerate((9, 11)):
                j = J_LOUT + 5 + n
                full(dve, j)
                V.tensor_copy(lout[0:w, n, :], flat(j)[0:w, 0:LW]).then_inc(psum_free[j % 4], 1)

            with dve.Fori(0, 4) as i:
                for c in range(4):
                    j = J_ADA2 + c
                    full(dve, j, i)
                    m = 16 + 2 * c + 8 * i
                    V.tensor_tensor(modT[:, bass.ds(m, 2), :], flat(j)[:, 0:18].rearrange("p (m n) -> p m n", n=9),
                                    par[:, bass.ds(ROWS["b_ada"] + m, 2)].unsqueeze(2).to_broadcast([P, 2, 9]), ADD).then_inc(psum_free[j % 4], 1)

            for e in range(2):
                V.tensor_copy(hb[e]["k"][NOPE:QK, :], krT[NOPE:QK, 0:NP]).then_inc(s_krk, 1)
            N0 = (0, NOPE)
            with dve.Fori(0, HEADS // 2) as i:
                lap = HEAD_LAP // 4 * i
                st.enter(i, 16)
                for e in range(2):
                    J, b = HeadJobs(e), hb[e]
                    nth = 2 * i + e + 1
                    q, qr = b["q"][0:QK, :], b["q"][NOPE:QK, :]
                    dve.wait_ge(s_qrs, nth)
                    V.scalar_tensor_tensor(q, q, pr("gq", 0, 1, (0, QK)), sq[0:QK, 2 * e + 1, :], MUL, MUL).then_inc(s_qn, 1)
                    dve.wait_ge(s_qn, nth)
                    V.tensor_scalar(b["gq"][0:NOPE, :], b["q"][0:NOPE, NP:T], pr("gk", 0, 1, N0), None, MUL).then_inc(s_gq, 1)
                    full(dve, J.qrot, lap)
                    V.tensor_tensor(two(qrot[NOPE:QK, :]), halves(J.qrot, R), two(C("sin", T, R)), MUL).then_inc(psum_free[J.qrot % 4], 1)
                    st.seq(V.tensor_tensor(qr, qr, C("cos", T, R), MUL))
                    dve.wait_ge(psum_free[J.qrot % 4], free_value(J.qrot, lap))
                    st.seq(V.tensor_tensor(qr, qr, qrot[NOPE:QK, :], ADD))
                    V.tensor_copy(QRS[NOPE:QK, :, bass.ds(2 * i + e, 1)], b["q"][NOPE:QK, NP:T].unsqueeze(2)).then_inc(s_qr, 1)
                    dve.wait_ge(s_krs, nth)
                    k = b["k"][0:NOPE, :]
                    V.scalar_tensor_tensor(k, k, pr("gk", 0, 1, N0), sq[0:NOPE, 5 + 2 * e, 0:NP], MUL, MUL).then_inc(s_kn, 1)
                    full(dve, J.vw, lap)
                    v = st.did(V.tensor_copy(b["v"], flat(J.vw)[:, 0:4 * VD]))
                    st.need(v)
                    V.tensor_copy(b["wt"][0:NOPE, :], flat(J.vw)[0:NOPE, 512:512 + P]).then_inc(psum_free[J.vw % 4], 1)
                    full(dve, J.qa, lap)
                    V.tensor_copy(QA[:, :, bass.ds(2 * i + e, 1)], flat(J.qa)[:, 0:NS].unsqueeze(2)).then_inc(psum_free[J.qa % 4], 1)
                for e in range(2):
                    J, b = HeadJobs(e), hb[e]
                    for n in range(4):
                        j = J.s[n]
                        full(dve, j, lap)
                        d = flat(j)[:, P * n:P * n + P]
                        V.tensor_tensor(d, d, C("mask"), ADD).then_inc(s_msk, 1)
                        dve.wait_ge(s_msk, 8 * i + 4 * e + n + 1)
                        st.seq(V.tensor_reduce(b["rl"][:, n:n + 1], flat(j)[:, 0:P * (n + 1)], AX.X, ALU.max))
                        V.tensor_scalar(b["nm"][:, n:n + 1], b["rl"][:, n:n + 1], -SCALE, None, MUL).then_inc(s_nm, 1)
                for e in range(2):
                    J, b = HeadJobs(e), hb[e]
                    for n in range(4):
                        dve.wait_ge(psum_free[J.s[n] % 4], free_value(J.s[n], lap))
                    st.seq(V.reciprocal(b["rl"], b["l"]))
                    for n in range(4):
                        p = b["p"][:, POFF[n]:POFF[n] + P * (n + 1)]
                        V.tensor_scalar(p, p, b["rl"][:, n:n + 1], None, MUL).then_inc(s_pn, 1)
                for e in range(2):
                    J, b = HeadJobs(e), hb[e]
                    for n in range(4):
                        j = J.p[n]
                        full(dve, j, lap)
                        for a in range(n + 1):
                            dst = b["pt"][:, TOFF[a] + P * (n - a):TOFF[a] + P * (n - a) + P]
                            ins = V.tensor_copy(dst, flat(j)[:, P * a:P * a + P])
                            if a == n:
                                ins.then_inc(psum_free[j % 4], 1)
                            else:
                                ins.then_inc(s_ptc, 1)
                for e in range(2):
                    J, b = HeadJobs(e), hb[e]
                    full(dve, J.pv, lap)
                    V.tensor_copy(hT[VD * e:VD * e + VD, bass.ds(LT + i, 1), 0:NP], flat(J.pv)[VD * e:VD * e + VD, 0:NP]).then_inc(psum_free[J.pv % 4], 1)
            st.leave(HEADS // 2)

            full(dve, J_SPREAD)
            dve.wait_ge(s_bdz, 2)
            src = flat(J_SPREAD)[:, 0:NS * HEADS].rearrange("p (b h) -> p b h", b=NS)
            for n in range(4):
                rows = slice(ROPE * n, ROPE * n + ROPE)
                ins = V.tensor_copy(QBD[rows, :, n, :], src[rows, :, :])
                st.did(ins) if n < 3 else ins.then_inc(psum_free[J_SPREAD % 4], 1)
            st.need(st.n)
            dve.wait_ge(psum_free[J_SPREAD % 4], free_value(J_SPREAD))
            dve.sem_inc(s_qbd, 1)

            def by_key(x):
                return x.rearrange("p (c h) -> p c h", h=HEADS)

            def scores_max(e, v):
                dve.wait_ge(s_drs, v)
                dve.wait_ge(s_snc, 9 * v)
                V.tensor_tensor(snd[e], snd[e], ssd[e], MUL).then_inc(s_sm, 1)
                dve.wait_ge(s_sm, 3 * v - 2)
                V.tensor_tensor(snd[e], snd[e], srd[e], ADD).then_inc(s_sm, 1)
                dve.wait_ge(s_sm, 3 * v - 1)
                last = snd[e][:, HEADS * PAGES:HEADS * KTILES]
                V.tensor_scalar(last, last, C("tail", 1), None, ADD).then_inc(s_sm, 1)
                dve.wait_ge(s_sm, 3 * v)
                V.tensor_reduce(mx[e], snd[e].rearrange("p (c h) -> p h c", h=HEADS), AX.X, ALU.max).then_inc(s_mx, 1)

            def shift(e, v):
                dve.wait_ge(s_am, v)
                V.tensor_tensor(by_key(snd[e]), by_key(snd[e]), mx[e].unsqueeze(1).to_broadcast([P, KTILES, HEADS]), SUB).then_inc(s_sh, 1)

            def prob_sums(e, v):
                dve.wait_ge(s_dp, v)
                V.tensor_reduce(pd[e], snd[e].rearrange("p (c h) -> p h c", h=HEADS), AX.X, ADD).then_inc(s_pd, 1)

            def finish(j, lap, s, v):
                full(dve, j, lap)
                V.reciprocal(rden, flat(j)[:, 512:512 + HEADS]).then_inc(s_rd, 1)
                dve.wait_ge(s_rd, v)
                V.tensor_tensor(OL[:, s, :], flat(j)[:, 0:HEADS], rden, MUL).then_inc(psum_free[j % 4], 1)

            def unit(base, lap, e, s_before, v):
                jj = lambda kind, g: base + UJ[kind, g] - (1 if base == J_DEC and UJ[kind, g] > UJ["pv", 0] else 0)
                nth = 0
                for g in range(NG):
                    tiles = 4 if g < NG - 1 else 1
                    for half in range(2 if g < NG - 1 else 1):
                        j = jj(f"k{half}", g)
                        n = min(2, tiles)
                        nth += 1
                        dve.wait_ge(psum_free[j % 4], free_value(j, lap))
                        c = HEADS * (4 * g + 2 * half)
                        V.tensor_reduce(ssd[e][:, c:c + HEADS * n], sqd[(nth + e) % 2][:, 0:512 * n].rearrange("p (m d) -> p m d", d=NOPE),
                                        AX.X, ADD).then_inc(s_sqr, 1)
                    j = jj("s", g)
                    full(dve, j, lap)
                    c = HEADS * 4 * g
                    V.tensor_copy(snd[e][:, c:c + HEADS * tiles], flat(j)[:, 0:HEADS * tiles]).then_inc(s_snc, 1)
                    V.tensor_copy(srd[e][:, c:c + HEADS * tiles], flat(j)[:, 512:512 + HEADS * tiles]).then_inc(psum_free[j % 4], 1)
                    if base != J_DEC:
                        if g == 1:
                            scores_max(1 - e, v - 1)
                        if g == 2:
                            shift(1 - e, v - 1)
                        if g == 4:
                            prob_sums(1 - e, v - 1)
                        if g == PV_AT:
                            finish(jj("pv", 0), lap, s_before, v - 1)

            unit(J_DEC, 0, 0, None, 1)
            with dve.Fori(0, 3) as i:
                unit(J_UNIT1, 2 * UNIT // 4 * i, 1, bass.ds(2 * i, 1), 2 * i + 2)
                unit(J_UNIT1 + UNIT, 2 * UNIT // 4 * i, 0, bass.ds(2 * i + 1, 1), 2 * i + 3)
            unit(J_UNIT1 + 6 * UNIT, 0, 1, 6, 8)
            dve.wait_ge(psum_free[(J_PVLAST - 1) % 4], free_value(J_PVLAST - 1))
            scores_max(1, NS)
            shift(1, NS)
            prob_sums(1, NS)
            finish(J_PVLAST, 0, NS - 1, NS)
            full(dve, J_VP)
            V.tensor_copy(hT[:, LT:KT, NP:T], flat(J_VP)[:, 0:LT * NS].rearrange("p (k n) -> p k n", n=NS)).then_inc(psum_free[J_VP % 4], 1)
            dve.wait_ge(s_rs, 6)
            for k in range(LT):
                V.scalar_tensor_tensor(hT[:, LT + k, :], hT[:, LT + k, :], pr("mla_out_norm_g", k), rs[:, :], MUL, MUL).then_inc(s_mix, 1)

            def residual(j, m, gate, done, nth):
                g = modT[:, gate + m, 0:1]
                full(dve, j)
                b0, b1 = ps[j % 4][:, 0, 0:H], ps[j % 4][:, 1, 0:NP - H]
                V.tensor_tensor(d8[:, m, :], ps[j % 4][:, 1, NP - H:H], modT[:, gate + m, 1:9], MUL).then_inc(s_d8, 1)
                v = st.did(V.scalar_tensor_tensor(xT[:, m, 0:H], b0, g, xT[:, m, 0:H], MUL, ADD))
                V.scalar_tensor_tensor(xT[:, m, H:NP], b1, g, xT[:, m, H:NP], MUL, ADD).then_inc(psum_free[j % 4], 1)
                dve.wait_ge(s_d8, nth)
                st.need(v)
                dve.wait_ge(psum_free[j % 4], free_value(j))
                V.tensor_tensor(xT[:, m, NP:T], xT[:, m, NP:T], d8[:, m, :], ADD).then_inc(done, 1)

            for m in range(KT):
                residual(J_WO + m, m, 2 * KT, s_x1, m + 1)
            st.seq(V.tensor_scalar(gmod[:, :, :], modT[:, 4 * KT:5 * KT, :], 1.0, None, ADD))
            st.seq(V.tensor_tensor(gmod[:, :, :], gmod[:, :, :], pr("norm2_g", 0, KT).unsqueeze(2).to_broadcast([P, KT, 9]), MUL))
            dve.wait_ge(s_rs, 7)
            for k in range(KT):
                V.tensor_tensor(hT[:, k, :], xT[:, k, :], rs[:, :], MUL).then_inc(s_hp, 1)
            dve.wait_ge(s_hp, 2 * KT)
            st.seq(V.tensor_tensor(hT[:, :, NP:T], hT[:, :, NP:T], gmod[:, :, 1:9], MUL))
            V.tensor_tensor(hT[:, :, NP:T], hT[:, :, NP:T], modT[:, 3 * KT:4 * KT, 1:9], ADD).then_inc(s_hd, 1)
            full(dve, J_FST)
            V.tensor_copy(FS[:, :, :].rearrange("p m n -> p (m n)"), flat(J_FST)[:, 0:4 * FT * NS]).then_inc(psum_free[J_FST % 4], 1)
            dve.wait_ge(psum_free[J_FST % 4], free_value(J_FST))
            for e in range(2):
                V.memset(UU[e][:, :, 0:2], 0.0).then_inc(s_pads, 1)
            dve.sem_inc(s_cvfree, 2)

            with dve.Fori(0, FT // 2) as i:
                st.enter(i, 20)
                for e in range(2):
                    m = 2 * i + e
                    for g in range(2):
                        j = J_UP + 2 * e + g
                        dve.wait_ge(psum_free[j % 4], free_value(j, i))
                        u, cv = UU[e][:, g, :], CV[g]
                        w = [fpar[:, bass.ds(2 * FT * n + FT * g + m, 1)] for n in range(4)]
                        fs = FS[:, bass.ds(FT * g + m, 1), :].rearrange("p o (b r) -> p (o b) r", r=2)
                        st.did(V.tensor_scalar(cv[:, 0:NP], u[:, 0:NP], w[0], w[3], MUL, ADD))
                        st.seq(V.tensor_scalar(cv[:, NP:T], fs[:, :, 0], w[0], w[3], MUL, ADD))
                        st.did(V.scalar_tensor_tensor(cv[:, 0:NP], u[:, 1:1 + NP], w[1], cv[:, 0:NP], MUL, ADD))
                        st.seq(V.scalar_tensor_tensor(cv[:, NP:T], fs[:, :, 1], w[1], cv[:, NP:T], MUL, ADD))
                        st.seq(V.scalar_tensor_tensor(cv[:, :], u[:, 2:2 + T], w[2], cv[:, :], MUL, ADD))
                    V.memset(small[:, 50:51], 0.0).then_inc(s_cv, 1)
                    dve.wait_ge(s_ge, m + 1)
                    V.tensor_tensor(actT[:, bass.ds(m, 1), :].rearrange("p o n -> p (o n)"), CV[0], GE, MUL).then_inc(s_hid, 1)
                    dve.wait_ge(s_hid, m + 1)
                    dve.wait_ge(s_ut, 2 * m + 2)
                    dve.sem_inc(s_cvfree, 1)
            st.leave(FT // 2)
            for m in range(KT):
                residual(J_DOWN + m, m, 5 * KT, s_x2, KT + m + 1)
            for n in (1, 3):
                j = J_Y + n
                full(dve, j)
                V.tensor_copy(y_tok[n], flat(j)[:, :]).then_inc(psum_free[j % 4], 1)
            for n in range(6):
                j = J_FT + n
                w = P * (min(8 * n + 8, 2 * FT) - 8 * n)
                full(dve, j)
                V.tensor_copy(ft_tok[:, D * n:D * n + w], flat(j)[0:10, 0:w]).then_inc(psum_free[j % 4], 1)


_INS = ["x_prompt", "x_sample", "cache_kv_latent", "cache_k_rope", "state_lru_h", "state_lru_conv", "state_ffn_conv",
        "page_table", "c_prompt", "c_sample", "w_ada", "b_ada", "norm1_g", "w_in", "lru_conv_w", "lru_conv_b", "lru_w_a",
        "lru_b_a", "lru_w_x", "lru_b_x", "lru_lambda", "q_lora_norm_g", "w_uq", "q_nope_norm_g", "q_rope_norm_g",
        "kv_lora_norm_g", "k_rope_norm_g", "w_ukv", "k_nope_norm_g", "lru_out_norm_g", "mla_out_norm_g", "w_o", "norm2_g",
        "w_up", "ffn_conv_w", "ffn_conv_b", "w_down"]
_OUTS = [("o_y_p", (1, NP, D)), ("o_y_s", (NS, 1, D)), ("o_kv_p", (1, 1, NP, KV)), ("o_kr_p", (1, 1, NP, ROPE)),
         ("o_lru_h_p", (1, 1, LW)), ("o_lru_conv_p", (1, 1, 3, LW)), ("o_ffn_conv_p", (1, 1, 2, 2 * FF)),
         ("o_kv_s", (1, NS, 1, KV)), ("o_kr_s", (1, NS, 1, ROPE)), ("o_lru_h_s", (1, NS, LW)),
         ("o_lru_conv_s", (1, NS, 3, LW)), ("o_ffn_conv_s", (1, NS, 2, 2 * FF))]


def kernel(**inputs):
    import numpy as np
    import concourse.bacc as bacc
    from concourse.bass_utils import run_bass_kernel_spmd as run

    nc = bacc.Bacc("TRN2", target_bir_lowering=False, num_devices=1)
    arrays, t = {}, {}
    for name in _INS:
        arrays[name] = np.ascontiguousarray(inputs[name])
    arrays["consts"] = constants()
    for name, a in arrays.items():
        t[name] = nc.dram_tensor(name, a.shape, mybir.dt.from_np(a.dtype), kind="ExternalInput").ap()
    for name, shape in _OUTS:
        t[name] = nc.dram_tensor(name, shape, F32, kind="ExternalOutput").ap()
    build(nc, t)
    r = run(nc, [arrays], core_ids=[0])
    return tuple(r.results[0][name] for name, _ in _OUTS)
```

```python
import math
from contextlib import ExitStack

import concourse.bass as bass
from concourse import mybir

F32 = mybir.dt.float32
FR = mybir.dt.float32r
I32 = mybir.dt.int32
ALU = mybir.AluOpType
ACT = mybir.ActivationFunctionType
AX = mybir.AxisListType
RMAX = bass.bass_isa.ReduceOp.max

P = 128
D = 1024
KT = D // P
NP, NS = 512, 8
T = NP + NS
H = T // 2
LT = 4
LW = LT * P
HEADS = 8
NOPE, ROPE, VD = 64, 32, 64
QK = NOPE + ROPE
KV = 128
QL = 256
IN = 2 * LW + QL + KV + ROPE
FF = 2816
FT = FF // P
PAGE = 128
PAGES = 32
POOL = 320
KTILES = PAGES + 1
EPS = 1e-6
SCALE = float(QK) ** -0.5
NEG = -1e30
LN2 = 0.6931471805599453

ROWS = {}
_r = 0
for _name, _n in (("b_ada", 48), ("norm1_g", 8), ("lru_conv_w", 16), ("lru_conv_b", 4), ("lru_b_a", 4), ("lru_b_x", 4),
                  ("lru_lambda", 4), ("q_lora_norm_g", 2), ("kv_lora_norm_g", 1), ("lru_out_norm_g", 4),
                  ("mla_out_norm_g", 4), ("norm2_g", 8), ("gq", 1), ("gk", 1)):
    ROWS[_name] = _r
    _r += _n
NROWS = _r

CC = {}
_c = 0
for _name, _n in (("ident", P), ("ones", P), ("blk", P), ("perm", QK), ("mask", P), ("spread", P), ("cos", T),
                  ("sin", T), ("tail", 1), ("quarter", 1)):
    CC[_name] = _c
    _c += _n
NCONST = _c


def constants():
    import numpy as np
    c = np.zeros((P, NCONST), np.float32)
    c[:, CC["ident"]:CC["ident"] + P] = np.eye(P)
    c[:, CC["ones"]:CC["ones"] + P] = 1.0
    blk = np.zeros((QK, QK), np.float32)
    blk[:NOPE, :NOPE] = 1.0 / NOPE
    blk[NOPE:, NOPE:] = 1.0 / ROPE
    c[:QK, CC["blk"]:CC["blk"] + QK] = blk
    half = ROPE // 2
    for m in range(half):
        c[NOPE + half + m, CC["perm"] + NOPE + m] = -1.0
        c[NOPE + m, CC["perm"] + NOPE + half + m] = 1.0
    q = np.arange(P)
    c[:, CC["mask"]:CC["mask"] + P] = np.where(q[None, :] <= q[:, None], 0.0, NEG)
    for j in range(4):
        for d in range(ROPE):
            c[NOPE + d, CC["spread"] + ROPE * j + d] = 1.0
    inv = (np.float32(10000.0) ** (-np.arange(0, ROPE, 2, dtype=np.float32) / np.float32(ROPE))).astype(np.float32)
    pos = np.concatenate([np.arange(NP), np.full(NS, PAGES * PAGE)]).astype(np.float32)
    ang = (pos[None, :] * inv[:, None]).astype(np.float32)
    c[NOPE:NOPE + half, CC["cos"]:CC["cos"] + T] = np.cos(ang)
    c[NOPE + half:QK, CC["cos"]:CC["cos"] + T] = np.cos(ang)
    c[NOPE:NOPE + half, CC["sin"]:CC["sin"] + T] = np.sin(ang)
    c[NOPE + half:QK, CC["sin"]:CC["sin"] + T] = np.sin(ang)
    c[1:, CC["tail"]] = NEG
    c[:, CC["quarter"]] = q % 4
    return c


class Steps:

    def __init__(self, eng, sem):
        self.eng, self.sem, self.n, self.base = eng, sem, 0, 0

    def did(self, ins):
        ins.then_inc(self.sem, 1)
        self.n += 1
        return self.base + self.n

    def need(self, v):
        self.eng.wait_ge(self.sem, v)

    def seq(self, ins):
        self.need(self.did(ins))

    def enter(self, i, per):
        self.start, self.base, self.n, self.per = self.n, self.n + i * per, 0, per

    def leave(self, laps):
        assert self.n == self.per, (self.n, self.per)
        self.n, self.base = self.start + laps * self.per, 0


J_PAR = 0
J_XT = J_PAR + 4
J_ROW = [J_XT + KT, J_XT + KT + 1]
J_COL = [J_XT + KT + 2, J_XT + KT + 3]
J_N1 = J_COL[1] + 1
WIN_ORDER = [0, 1, 2, 3, 8, 9, 10, 11, 4, 5, 6, 7]
J_GATE = J_N1 + 1 + 8
J_WIN = {m: J_N1 + 1 + n + (8 if n >= 8 else 0) + (3 if n >= 10 else 0) for n, m in enumerate(WIN_ORDER)}
J_NQ = J_WIN[5] + 1
J_NKV = J_NQ + 1
J_KR = [J_NKV + 1, J_WIN[7] + 1]
J_ROW.append(J_KR[1] + 1)
J_ROW.append(J_ROW[2] + 1)
J_COL.append(J_ROW[3] + 1)
J_NLRU = J_COL[2] + 1
J_ROW.append(J_NLRU + 1)
J_COL.append(J_ROW[4] + 1)
J_LOUT = J_COL[3] + 1
J_ROW.append(J_LOUT + 7)
J_COL.append(J_ROW[5] + 1)
J_COL.append(J_COL[4] + 1)
J_HEAD = J_COL[5] + 1


POFF = [0, P, 3 * P, 6 * P]


class HeadJobs:

    def __init__(self, first, order):
        self.count = len(order)
        self.q, self.qms, self.qrot, self.kn, self.kms, self.vw, self.qa, self.pv = ({} for _ in range(8))
        self.s, self.p = [{}, {}], [{}, {}]
        whole = dict(q=self.q, qms=self.qms, qrot=self.qrot, kn=self.kn, kms=self.kms, vw=self.vw, qa=self.qa, pv=self.pv)
        blocks = dict(s=self.s, p=self.p)
        for n, (kind, e, *block) in enumerate(order):
            if block:
                blocks[kind][e][block[0]] = first + n
            else:
                whole[kind][e] = first + n


def _each(*kinds):
    return [(kind, e) for e in range(2) for kind in kinds]


_S = [("s", e, n) for e in range(2) for n in range(4)]
_P0, _P1 = [[("p", e, n) for n in range(4)] for e in range(2)]
HEAD_FIRST = HeadJobs(J_HEAD, _each("q", "kn") + _each("qms", "kms") + _each("qrot") + _each("vw") + _each("qa"))
HEAD_LAP = HeadJobs(J_HEAD + HEAD_FIRST.count, _S + _each("q", "kn") + _P0 + _each("qms", "kms") + _P1 + _each("qrot")
                    + _each("pv") + _each("vw") + _each("qa"))
HEAD_LAPS = HEADS // 2 - 1
assert HEAD_LAP.count % 4 == 0
HEAD_LAST = HeadJobs(J_HEAD + HEAD_FIRST.count + HEAD_LAPS * HEAD_LAP.count, _S + _P0 + _P1 + _each("pv"))
J_SPREAD = J_HEAD + HEAD_FIRST.count + HEAD_LAPS * HEAD_LAP.count + HEAD_LAST.count
J_FIRST_T = J_SPREAD + 1
J_DEC = J_FIRST_T + 2
NG = 9
GT = [4] * (NG - 1) + [1]
UNIT = NG + KTILES + 2
PV_AT = 4


def unit_jobs():
    order = []
    for g in range(NG):
        order.append(("t", g + 2) if g + 2 < NG else ("tn", g + 2 - NG))
        order += [("k", 4 * g + n) for n in range(GT[g])]
        if g == PV_AT:
            order += [("pv", 0), ("den", 0)]
    assert len(order) == UNIT
    return {x: n for n, x in enumerate(order)}


UJ = unit_jobs()
J_UNIT1 = J_DEC + UNIT - 2
J_LAST = J_UNIT1 + UNIT * (NS - 2)


def unit_job(base, kind, n):
    if kind == "t" and n < 2:
        return J_FIRST_T + n if base == J_DEC else base - UNIT + UJ["tn", n]
    u = UJ[kind, n]
    if base == J_DEC and u > UJ["pv", 0]:
        return base + u - 2
    if base == J_LAST:
        return base + u - (u > UJ["tn", 0]) - (u > UJ["tn", 1])
    return base + u


J_PVLAST = J_LAST + UNIT - 2
J_OL = J_PVLAST + 2
J_VP = J_OL + 1
J_NMLA = J_VP + 1
J_WO = J_NMLA + 1
J_N2 = J_WO + KT
J_FST = J_N2 + 1
J_UP = J_FST + 1
J_DOWN = J_UP + 2 * FT
J_Y = J_DOWN + KT
J_FT = J_Y + 5


def build(nc, t):
    with ExitStack() as ctx:
        def sb(name, shape, dt=F32):
            return ctx.enter_context(nc.sbuf_tensor(name, shape, dt))

        def sb_parts(name, shape):
            return [ctx.enter_context(nc.sbuf_tensor(f"{name}_{part}", shape, FR)) for part in ("high", "low")]

        def parts_at(name, shape, at):
            size = 4 * math.prod(shape[1:])
            return [nc.alloc_sbuf_tensor_at(f"{name}_{part}", shape, FR, offset=at + n * size) for n, part in enumerate(("high", "low"))]

        def sem(name):
            return ctx.enter_context(nc.semaphore(name))

        cst = sb("cst", [P, NCONST])
        par_rows = sb("par_rows", [P, 3, P])
        par = sb("par", [P, NROWS])
        fpar = sb("fpar", [P, 4 * 2 * FT])
        xT = sb("xT", [P, KT, T])
        h_at = -(-nc.sbuf_base // 32) * 32
        hT = sb("hT", [P, KT, T])
        sq = sb("sq", [P, KT, T])
        rs = sb("rs", [P, T])
        modT = sb("modT", [P, 48, 9])
        gmod = sb("gmod", [P, KT, 9])
        cT = sb("cT", [P, KT, 9])
        small = sb("small", [P, 64])
        d8 = sb("d8", [P, KT, NS])
        UT = sb("UT", [P, 2 * FT, 10])
        FS = sb("FS", [P, 2 * FT, 2 * NS])
        rw_at = -(-nc.sbuf_base // 32) * 32
        RW = sb("RW", [P, 12288])
        rb_at = -(-nc.sbuf_base // 32) * 32
        RB = sb("RB", [P, 13200])
        ring = RW[:, 0:8192].rearrange("p (c k n) -> p c k n", c=4, k=KT)
        RA = RW[:, 8192:12288].rearrange("p (c k n) -> p c k n", c=4, k=KT)

        def sq_flat(a, n):
            return sq[:, :, :].rearrange("p k n -> p (k n)")[:, a:a + n]

        def C(name, w=P, rows=(0, P)):
            return cst[rows[0]:rows[1], CC[name]:CC[name] + w]

        ident, ones = C("ident"), C("ones")

        def pr(name, k=0, n=1, rows=(0, P)):
            return par[rows[0]:rows[1], ROWS[name] + k:ROWS[name] + k + n]

        x_tok = RB[:, 0:4 * D].rearrange("p (a d) -> p a d", a=4)
        xs_tok = RB[0:NS, 4 * D:5 * D]
        c_tok = RB[0:9, 5 * D:6 * D]
        c_th = RB[0:9, 6 * D:7 * D]
        st_tok = RB[0:24, 7 * D:7 * D + LW]
        h0_tok = RB[0:NS, 7 * D + LW:8 * D]
        o = 0

        def take(n):
            nonlocal o
            o += n
            assert o <= 13200, o
            return RB[:, o - n:o]

        XX = take(LT * (3 + T)).rearrange("p (t n) -> p t n", t=LT)
        GG = take(LT * T).rearrange("p (t n) -> p t n", t=LT)
        XC = take(LT * T).rearrange("p (t n) -> p t n", t=LT)
        TA = take(LT * T).rearrange("p (t n) -> p t n", t=LT)
        TI = take(LT * T).rearrange("p (t n) -> p t n", t=LT)
        AA = take(LT * T).rearrange("p (t n) -> p t n", t=LT)
        stT = sb("stT", [P, LT * 24])
        h0T = sb("h0T", [P, LT * NS])
        st4 = stT[:, :].rearrange("p (t b r) -> p t b r", t=LT, b=NS)
        h04 = h0T[:, :].rearrange("p (t b) -> p t b", t=LT)
        BD = sb("BD", [P, 2, LT, P])
        qlT = sb("qlT", [P, 2, T])
        kvT = sb("kvT", [P, T])
        krT = sb("krT", [P, T])
        qrot = sb("qrot", [P, T])
        otok = sb("otok", [P, 5, 160])
        lout = sb("lout", [16, 2, LW])

        o = 0
        hb = []
        for e in range(2):
            hb.append(dict(q=take(T), k=take(NP), p=take(10 * P),
                           pt=take(4 * NP).rearrange("p (a n) -> p a n", a=4),
                            v=take(4 * VD), wt=take(P),
                           nm=take(4), l=take(4), rl=take(4), gq=take(NS)))
        wuq = sb("wuq", [P, 2, 2, QK])
        wukv = sb("wukv", [P, 2, P])
        QA = sb("QA", [P, NS, HEADS])
        QRS = sb("QRS", [P, NS, HEADS])
        OLR = sb("OLR", [HEADS, NS, KV])
        QBD = sb("QBD", [P, NS, 4, HEADS])
        OL = sb("OL", [P, NS, HEADS])
        rden = sb("rden", [P, HEADS])[:, :]
        wkn = sb("wkn", [P, HEADS * NOPE])
        page_of = sb("page_of", [P, NS], I32)
        row_of = sb("row_of", [P, NS], I32)
        half_of = sb("half_of", [P, 2, NS], I32)
        newrow = sb("newrow", [1, NS, KV + ROPE])
        o = 0
        sqd = [take(512), qrot[:, 0:512], krT[:, 0:512]]
        ssd = [take(KTILES * HEADS) for _ in range(2)]
        snd = [take(KTILES * HEADS) for _ in range(2)]
        srd = [take(KTILES * HEADS) for _ in range(2)]
        mx = [take(HEADS) for _ in range(2)]
        pd = [take(HEADS) for _ in range(2)]
        wv = take(HEADS * VD).rearrange("p (h d) -> p h d", h=HEADS)
        KWW = 4 * NOPE + 4
        turned = take(3 * 5 * P).rearrange("p (g n) -> p g n", g=3)
        latH, latL = parts_at("latents", [P, 3, 4 * P], rb_at + 4 * o)
        o += 2 * 3 * 4 * P
        kwH, kwL = parts_at("key_weights", [P, 2, 2, KWW], rb_at + 4 * o)
        o += 2 * 2 * 2 * KWW
        mxH, mxL = parts_at("mixed", [P, KT, T], rb_at)
        woH, woL = parts_at("output_weights", [P, 2, KT, P], rw_at + 4 * 8192)
        woR = RB[:, 13200 - 3072:13200].rearrange("p (c k n) -> p c k n", c=3, k=KT)
        assert o <= 13200 - 3072
        n_lat = KTILES * P
        n_kr = 36 * ROPE
        lat = [RW[:, e * n_lat:(e + 1) * n_lat].rearrange("p (c d) -> p c d", c=KTILES) for e in range(2)]
        kr_ = [RW[:, 2 * n_lat + e * n_kr:2 * n_lat + (e + 1) * n_kr].rearrange("p (c d) -> p c d", c=36) for e in range(2)]
        sb("hidden_tail", [P, (rb_at + 4 * 2 * FT * T - nc.sbuf_base) // 4])
        hH, hL = parts_at("normed", [P, KT, T], h_at)
        actH, actL = parts_at("hidden", [P, FT, T], rb_at)
        h2 = RB[:, 2 * FF:2 * FF + KT * T].rearrange("p (k n) -> p k n", k=KT)
        wup = RW[:, 0:4096].rearrange("p (c k n) -> p c k n", c=2, k=2 * KT)
        wuH, wuL = parts_at("up_weights", [P, 2 * KT, P], rw_at + 4 * 4096)
        wdn = RW[:, 0:2 * FT * P].rearrange("p (c k n) -> p c k n", c=2, k=FT)
        wdH, wdL = zip(parts_at("down_weights0", [P, FT, P], h_at), parts_at("down_weights1", [P, FT, P], rw_at + 4 * 2 * FT * P))
        UW = 2 + T
        UU = [RW[:, 8192 + 2 * UW * e:8192 + 2 * UW * (e + 1)].rearrange("p (g n) -> p g n", g=2) for e in range(2)]
        CV = [RW[:, 8192 + 4 * UW + T * g:8192 + 4 * UW + T * (g + 1)] for g in range(2)]
        GE = RW[:, 8192 + 4 * UW + 2 * T:8192 + 4 * UW + 3 * T]
        fs_tok = RB[0:2 * NS, 0:2 * FF]
        y_tok = [RB[:, D * n:D * n + D] for n in range(5)]
        ft_tok = RB[0:10, 6 * D:6 * D + 2 * FF]

        ps = [ctx.enter_context(nc.psum_tensor(f"ps{i}", [P, 2, 512], F32)) for i in range(4)]
        psum_full = [sem(f"psum_full{i}") for i in range(4)]
        psum_free = [sem(f"psum_free{i}") for i in range(4)]

        def halves(j, rows=(0, P)):
            return ps[j % 4][rows[0]:rows[1], :, 0:H]

        def flat(j):
            return ps[j % 4][:, :, :].rearrange("p a b -> p (a b)")

        def two(ap):
            return ap.rearrange("p (a n) -> p a n", a=2)

        s_cst = sem("consts_in")
        s_par = sem("params_in")
        s_x = sem("x_in")
        s_ada = [sem(f"w_ada_in{i}") for i in range(4)]
        s_ada2 = [sem(f"w_ada_second_in{i}") for i in range(4)]
        s_hp = sem("h_scaled")
        s_hd = sem("h_decode_done")
        s_tiny = sem("mult_argument_done")
        s_win = [sem(f"w_in_in{i}") for i in range(4)]
        s_bd = sem("gate_weights_in")
        s_bdz = sem("gate_weights_cleared")
        s_parz = sem("param_rows_cleared")
        s_out = sem("outputs_stored")
        s_cT = sem("c_transposed_done")
        s_silu = sem("silu_c_done")
        s_sq = sem("squares_done")
        s_rs = sem("rstd_done")
        s_h = sem("normed_done")
        s_dve = sem("dve_steps")
        s_act2 = sem("key_ln_done")
        s_cvfree = sem("up_buffers_free")
        s_act = sem("act_steps")
        s_xt = sem("xT_done")
        s_mod = sem("modT_done")
        s_xc = sem("x_conv_done")
        s_ta = sem("tanh_a_done")
        s_ti = sem("tanh_x_done")
        s_lru = sem("lru_act_done")
        s_lrud = sem("lru_dve_done")
        s_sp = sem("softplus_done")
        s_ev = sem("act_evacuated")
        s_g = sem("gelu_done")
        s_kr = sem("k_rope_done")
        s_ql = sem("q_latent_normed")
        s_kvn = sem("kv_latent_normed")
        s_mix = sem("mixed_done")
        s_hw = [sem(f"head_weights_in{e}") for e in range(2)]
        s_wo = [sem(f"w_o_in{e}") for e in range(3)]
        s_qsq = sem("q_squares_done")
        s_qrs = sem("q_rstd_done")
        s_qn = sem("q_normed")
        s_qr = sem("q_rotated")
        s_ksq = sem("k_squares_done")
        s_krs = sem("k_rstd_done")
        s_kn = sem("k_head_done")
        s_gq = sem("q_times_k_gain_done")
        s_nm = sem("row_max_done")
        s_p = sem("exp_done")
        s_pn = sem("probs_normed")
        s_pt = sem("page_table_in")
        s_row = sem("cache_rows_known")
        s_ada_used = sem("w_ada_chunks_used")
        s_lat = [[sem(f"cached_latents{n}_in{e}") for e in range(2)] for n in range(2)]
        s_krc = [sem(f"cached_keys_in{e}") for e in range(2)]
        s_new = sem("new_token_rows_in")
        s_newc = sem("new_token_tile_done")
        s_clr = sem("new_token_tiles_cleared")
        s_tT = sem("latents_transposed_copied")
        s_lo = sem("latents_low_done")
        s_kw = sem("key_weights_split")
        s_kwq = sem("queries_split")
        s_sqd = sem("key_squares_done")
        s_sqr = sem("key_squares_summed")
        s_drs = sem("key_rstd_done")
        s_mx = sem("partition_max_done")
        s_am = sem("all_max_done")
        s_sh = sem("scores_shifted")
        s_dp = sem("decode_probs_done")
        s_pd = sem("decode_prob_sums_done")
        s_wkn = sem("key_weights_in")
        s_krk = sem("rope_key_rows_set")
        s_msk = sem("scores_masked")
        s_ptc = sem("prob_blocks_copied")
        s_snc = sem("decode_scores_copied")
        s_sm = sem("decode_score_steps")
        s_rd = sem("decode_sum_inverted")
        s_d8 = sem("decode_residual_scaled")
        s_pads = sem("conv_pads_cleared")
        s_ut = sem("last_rows_kept")
        s_wv = sem("value_weights_in")
        s_qbd = sem("decode_rope_queries_done")
        s_x1 = sem("x1_done")
        s_wup = [sem(f"w_up_in{e}") for e in range(2)]
        s_whi = sem("mlp_weights_high")
        s_wlo = sem("mlp_weights_low")
        s_mhi = sem("mixed_high")
        s_mlo = sem("mixed_low")
        s_wohi = sem("output_weights_high")
        s_wolo = sem("output_weights_low")
        s_hhi = sem("h2_high")
        s_hlo = sem("h2_low")
        s_wdn = [sem(f"w_down_in{e}") for e in range(2)]
        s_fst = sem("ffn_state_in")
        s_u = sem("up_evacuated")
        s_cv = sem("conv_done")
        s_ge = sem("gelu_gate_done")
        s_hid = sem("hidden_done")
        s_x2 = sem("x2_done")
        s_tok = sem("token_rows_done")

        def full(eng, j, lap=0):
            eng.wait_ge(psum_full[j % 4], j // 4 + 1 + lap)

        def claim(eng, j, lap=0):
            if j // 4 >= 1 or not isinstance(lap, int):
                eng.wait_ge(psum_free[j % 4], j // 4 + lap)

        def free_value(j, lap=0):
            return j // 4 + 1 + lap

        def chunk_used(eng, c):
            if c % 4 == 3:
                full(eng, J_ROW[c // 4])
            else:
                eng.wait_ge(s_ada_used, 3 * (c // 4) + c % 4 + 1)

        hflat = hT[:, :, :].rearrange("p k n -> p (k n)")

        def rows9(n):
            return hflat[0:9, 2080 + D * (n % 2):2080 + D * (n % 2) + D]

        block = ctx.enter_context(nc.Block())

        @block.sync
        def _(sp):
            sp.dma_start(cst[:, :], t["consts"]).then_inc(s_cst, 16)
            for r in range(4):
                sp.dma_start(page_of[r:P:4, :], t["page_table"].rearrange("b n -> n b"), allow_slow_non_contiguous=True).then_inc(s_pt, 16)
            x3 = t["x_prompt"].rearrange("b (a p) d -> p (b a) d", p=P)
            sp.dma_start(c_tok[0:1, :], t["c_prompt"]).then_inc(s_x, 16)
            sp.dma_start(c_tok[1:9, :], t["c_sample"]).then_inc(s_x, 16)
            wa = t["w_ada"].rearrange("l (k p) (c n) -> p (l k) c n", p=P, n=256)
            for c in range(4):
                sp.dma_start(ring[:, c, :, :], wa[:, :, c, :]).then_inc(s_ada[c], 16)
            sp.wait_ge(s_parz, 1)

            def rows(name, src, part=0):
                n = src.shape[0]
                sp.dma_start(par_rows[ROWS[name]:ROWS[name] + n, part, 0:src.shape[1]], src).then_inc(s_par, 16)

            for name in ("b_ada", "norm1_g", "lru_conv_b", "lru_b_a", "lru_b_x", "lru_lambda",
                         "q_lora_norm_g", "kv_lora_norm_g", "lru_out_norm_g", "mla_out_norm_g", "norm2_g"):
                rows(name, t[name].rearrange("l (r p) -> (l r) p", p=P))
            rows("lru_conv_w", t["lru_conv_w"].rearrange("l w (r p) -> (l w r) p", p=P))
            for name, a, b in (("gq", "q_nope_norm_g", "q_rope_norm_g"), ("gk", "k_nope_norm_g", "k_rope_norm_g")):
                r = ROWS[name]
                sp.dma_start(par_rows[r:r + 1, 0, 0:NOPE], t[a]).then_inc(s_par, 16)
                sp.dma_start(par_rows[r:r + 1, 0, NOPE:QK], t[b]).then_inc(s_par, 16)
            fw = t["ffn_conv_w"].rearrange("l w (r p) -> (l w r) p", p=P)
            sp.dma_start(par_rows[0:4 * FT, 1, :], fw[0:4 * FT, :]).then_inc(s_par, 16)
            sp.dma_start(par_rows[0:2 * FT, 2, :], fw[4 * FT:6 * FT, :]).then_inc(s_par, 16)
            sp.dma_start(par_rows[2 * FT:4 * FT, 2, :],
                         t["ffn_conv_b"].rearrange("l (r p) -> (l r) p", p=P)).then_inc(s_par, 16)
            sp.dma_start(st_tok, t["state_lru_conv"].rearrange("l b r w -> (l b r) w")).then_inc(s_par, 16)
            sp.dma_start(h0_tok, t["state_lru_h"].rearrange("l b w -> (l b) w")).then_inc(s_par, 16)
            sp.dma_start(xs_tok, t["x_sample"].rearrange("b s d -> (b s) d")).then_inc(s_x, 16)
            sp.dma_start(x_tok, x3).then_inc(s_x, 16)

            for c in range(4):
                chunk_used(sp, c)
                sp.dma_start(ring[:, c, :, :], wa[:, :, 4 + c, :]).then_inc(s_ada[c], 16)
            wi = t["w_in"].rearrange("l (k p) n -> p (l k) n", p=P)

            def w_in(n):
                m = WIN_ORDER[n]
                w = P if m < 11 else ROPE
                if n >= 4:
                    full(sp, J_WIN[WIN_ORDER[n - 4]])
                sp.dma_start(RA[:, n % 4, :, 0:w], wi[:, :, P * m:P * m + w]).then_inc(s_win[n % 4], 16)

            for n in range(4):
                w_in(n)
            sp.wait_ge(s_bdz, 1)
            for g, name in enumerate(("lru_w_a", "lru_w_x")):
                w = t[name].rearrange("l (t e) i j -> (l e) i t j", e=2)
                for e in range(2):
                    sp.dma_start(BD[64 * e:64 * e + 64, g, :, 64 * e:64 * e + 64], w[e]).then_inc(s_bd, 16)
            for n in range(4, 12):
                w_in(n)
            wq = t["w_uq"].rearrange("l (k p) (h n) -> p (l k) h n", p=P, h=HEADS)
            wk = t["w_ukv"].rearrange("l p (h n) -> p (l h) n", h=HEADS)

            def head_weights(e, h):
                sp.dma_start(wuq[:, e, :, :], wq[:, :, h, :]).then_inc(s_hw[e], 16)
                sp.dma_start(wukv[:, e, :], wk[:, h, :]).then_inc(s_hw[e], 16)

            sp.dma_start(wkn[:, :].rearrange("p (h n) -> p h n", h=HEADS),
                         t["w_ukv"][0].rearrange("p (h n) -> p h n", h=HEADS)[:, :, 0:NOPE]).then_inc(s_wkn, 16)
            for e in range(2):
                head_weights(e, bass.ds(e, 1))
            sp.dma_start(t["o_lru_conv_s"][0, :, 0:2, :], t["state_lru_conv"][0, :, 1:3, :]).then_inc(s_out, 16)
            sp.dma_start(t["o_ffn_conv_s"][0, :, 0:1, :], t["state_ffn_conv"][0, :, 1:2, :]).then_inc(s_out, 16)

            for a in range(5):
                sp.wait_ge(psum_free[(J_LOUT + a) % 4], free_value(J_LOUT + a))
            sp.dma_start(t["o_kv_p"].rearrange("l b (a p) d -> p (l b a) d", p=P), otok[:, 0:4, 0:KV]).then_inc(s_out, 16)
            sp.dma_start(t["o_kr_p"].rearrange("l b (a p) d -> p (l b a) d", p=P), otok[:, 0:4, KV:KV + ROPE]).then_inc(s_out, 16)
            sp.dma_start(t["o_kv_s"].rearrange("l b s d -> (l b s) d"), otok[0:NS, 4, 0:KV]).then_inc(s_out, 16)
            sp.dma_start(t["o_kr_s"].rearrange("l b s d -> (l b s) d"), otok[0:NS, 4, KV:KV + ROPE]).then_inc(s_out, 16)
            for a in range(5, 7):
                sp.wait_ge(psum_free[(J_LOUT + a) % 4], free_value(J_LOUT + a))
            sp.dma_start(t["o_lru_h_p"].rearrange("l b w -> (l b) w"), lout[0:1, 0, :]).then_inc(s_out, 16)
            sp.dma_start(t["o_lru_h_s"].rearrange("l b w -> (l b) w"), lout[1:9, 0, :]).then_inc(s_out, 16)
            sp.dma_start(t["o_lru_conv_p"].rearrange("l b r w -> (l b r) w"), lout[0:3, 1, :]).then_inc(s_out, 16)
            sp.dma_start(t["o_lru_conv_s"][0, :, 2, :], lout[3:11, 1, :]).then_inc(s_out, 16)
            sp.dma_start(newrow[0:1, :, :], otok[0:NS, 4, :]).then_inc(s_new, 16)
            for e in range(2):
                full(sp, HEAD_FIRST.qa[e])
                head_weights(e, bass.ds(2 + e, 1))
            with sp.Fori(0, HEAD_LAPS - 1) as i:
                for e in range(2):
                    full(sp, HEAD_LAP.qa[e], HEAD_LAP.count // 4 * i)
                    head_weights(e, bass.ds(2 * i + 4 + e, 1))
            full(sp, J_SPREAD)
            sp.dma_start(wv, t["w_ukv"][0].rearrange("p (h n) -> p h n", h=HEADS)[:, :, NOPE:]).then_inc(s_wv, 16)
            wo = t["w_o"].rearrange("l (k p) n -> p (l k) n", p=P)
            for m in range(KT):
                if m >= 3:
                    full(sp, J_WO + m - 3)
                sp.dma_start(woR[:, m % 3, :, :], wo[:, :, P * m:P * m + P]).then_inc(s_wo[m % 3], 16)
            full(sp, J_PVLAST)
            wu = t["w_up"].rearrange("l (k p) (g n) -> p (l k) g n", p=P, g=2)

            def up_weights(c, m):
                for g in range(2):
                    sp.dma_start(wup[:, c, KT * g:KT * g + KT, :], wu[:, :, g, m]).then_inc(s_wup[c], 16)

            for m in range(2):
                up_weights(m, bass.ds(P * m, P))
            full(sp, J_WO + 7)
            sp.dma_start(fs_tok, t["state_ffn_conv"].rearrange("l b r w -> (l b r) w")).then_inc(s_fst, 16)
            wd = t["w_down"].rearrange("l (k p) n -> p (l k) n", p=P)
            with sp.Fori(1, FT // 2) as i:
                for e in range(2):
                    sp.wait_ge(s_wlo, 4 * i + 2 * e - 2)
                    up_weights(e, bass.ds(2 * P * i + P * e, P))
            for m in range(KT):
                if m == 1:
                    full(sp, J_UP + 2 * FT - 1)
                else:
                    sp.wait_ge(s_wlo, 2 * FT + 2 * max(m - 1, 0))
                sp.dma_start(wdn[:, m % 2, :, :], wd[:, :, P * m:P * m + P]).then_inc(s_wdn[m % 2], 16)
            for n in range(5):
                sp.wait_ge(psum_free[(J_Y + n) % 4], free_value(J_Y + n))
                if n < 4:
                    sp.dma_start(t["o_y_p"][0, P * n:P * n + P, :], y_tok[n]).then_inc(s_out, 16)
                else:
                    sp.dma_start(t["o_y_s"].rearrange("b s d -> (b s) d"), y_tok[n][0:NS, :]).then_inc(s_out, 16)
            for n in range(6):
                sp.wait_ge(psum_free[(J_FT + n) % 4], free_value(J_FT + n))
            sp.dma_start(t["o_ffn_conv_p"][0, 0, :, :], ft_tok[0:2, :]).then_inc(s_out, 16)
            sp.dma_start(t["o_ffn_conv_s"][0, :, 1, :], ft_tok[2:10, :]).then_inc(s_out, 16)
            sp.wait_ge(s_out, 16 * 17)

        @block.gpsimd
        def _(pool):
            nc.gpsimd.memset(par_rows[:, :, :], 0.0).then_inc(s_parz, 1)
            nc.gpsimd.memset(BD[:, :, :, :], 0.0).then_inc(s_bdz, 1)
            nc.gpsimd.memset(QBD[:, :, :, :], 0.0).then_inc(s_bdz, 1)
            wa = t["w_ada"].rearrange("l (k p) (c n) -> p (l k) c n", p=P, n=256)
            for c in range(16):
                chunk_used(pool, 4 + c)
                nc.gpsimd.dma_start(ring[:, c % 4, :, :], wa[:, :, 8 + c, :]).then_inc(s_ada2[c % 4], 16)
            cl = t["cache_kv_latent"].rearrange("l n (r k) d -> (l n r) (k d)", r=8)
            ck = t["cache_k_rope"].rearrange("l n (r k) d -> (l n r) (k d)", r=4)

            def fetch(dst, src, rows, done):
                nc.gpsimd.indirect_dma_start(dst.rearrange("p c d -> p (c d)"), None, src, bass.IndirectOffsetOnAxis(ap=rows, axis=0)).then_inc(done, 16)

            def cached_keys(e, s):
                fetch(kr_[e][:, 0:PAGES, :], ck, row_of[:, s:s + 1], s_krc[e])

            def cached_latents(e, s):
                for n in range(2):
                    fetch(lat[e][:, n * PAGES // 2:(n + 1) * PAGES // 2, :], cl, half_of[:, n, s:s + 1], s_lat[n][e])

            full(pool, J_ROW[5])
            pool.wait_ge(s_row, 3)
            for n in range(2):
                cached_keys(n, n)
                cached_latents(n, n)
            for e in range(2):
                nc.gpsimd.memset(lat[e][:, PAGES, :], 0.0).then_inc(s_clr, 1)
                nc.gpsimd.memset(kr_[e][:, PAGES:36, :], 0.0).then_inc(s_clr, 1)
            pool.wait_ge(s_clr, 4)
            pool.wait_ge(s_new, 16)

            def new_key(e, s):
                nc.gpsimd.tensor_copy(kr_[e][0:1, PAGES, :], newrow[0:1, s, KV:KV + ROPE]).then_inc(s_newc, 1)

            def new_latent(e, s):
                nc.gpsimd.tensor_copy(lat[e][0:1, PAGES, :], newrow[0:1, s, 0:KV]).then_inc(s_newc, 1)

            def all_max(e, v):
                pool.wait_ge(s_mx, v)
                nc.gpsimd.partition_all_reduce(mx[e], mx[e], P, RMAX).then_inc(s_am, 1)

            for n in range(2):
                new_key(n, n)
                new_latent(n, n)
            def low_latents(v, g):
                pool.wait_ge(s_tT, NG * (v - 1) + g + 1)
                if g < 2:
                    j = J_FIRST_T + g if v == 1 else J_UNIT1 + UNIT * (v - 3) + UJ["tn", g] if v > 2 else unit_job(J_DEC, "tn", g)
                else:
                    j = unit_job(J_DEC if v == 1 else J_UNIT1 + UNIT * (v - 2), "t", g)
                pool.wait_ge(psum_free[j % 4], free_value(j))
                c = 4 * P - GT[g] * P
                nc.gpsimd.tensor_tensor(latL[:, g % 3, c:4 * P], turned[:, g % 3, c:4 * P], latH[:, g % 3, c:4 * P].bitcast(F32), ALU.subtract).then_inc(s_lo, 1)

            for g in range(2):
                low_latents(1, g)
            for v in range(1, NS + 1):
                for g in range(NG):
                    if 1 < v < NS and g == 0:
                        j = unit_job(J_DEC if v == 2 else J_UNIT1 + UNIT * (v - 3), "t", NG - 1)
                        full(pool, j)
                        cached_keys(v % 2, v)
                        new_key(v % 2, v)
                    if v > 1 and g == 2:
                        all_max(v % 2, v - 1)
                    if g + 2 < NG:
                        low_latents(v, g + 2)
                    elif v < NS:
                        low_latents(v + 1, g + 2 - NG)
                    if 1 < v < NS and g == PV_AT:
                        full(pool, J_UNIT1 + UNIT * (v - 2) + UJ["pv", 0])
                        cached_latents(v % 2, v)
                        new_latent(v % 2, v)
            all_max(1, NS)
            with pool.Fori(0, FT // 2) as i:
                for e in range(2):
                    for g in range(2):
                        pool.wait_ge(psum_free[(J_UP + 2 * e + g) % 4], free_value(J_UP + 2 * e + g, i))
                        nc.gpsimd.tensor_copy(UT[:, bass.ds(FT * g + 2 * i + e, 1), :], UU[e][:, g, NP:UW]).then_inc(s_ut, 1)

        @block.tensor
        def _(pe):
            mm = nc.tensor.matmul

            def tr(out, in_, n):
                return nc.tensor.transpose(out, in_, ident[0:n, 0:n])

            def both(j, lhsT, src, start, stop, rows=(0, P), lap=0):
                for h in range(2):
                    last = mm(ps[j % 4][rows[0]:rows[1], h, 0:H], lhsT, src[:, h * H:(h + 1) * H], start=start, stop=stop)
                return last

            pe.wait_ge(s_cst, 16)
            pe.wait_ge(s_par, 16 * 21)
            tr(flat(0)[:, 0:NROWS], par_rows[0:NROWS, 0, :], NROWS).then_inc(psum_full[0], 1)
            tr(flat(1)[:, 0:88], par_rows[0:88, 1, :], 88)
            tr(flat(1)[:, 88:176], par_rows[0:88, 2, :], 88).then_inc(psum_full[1], 1)
            for k in range(LT):
                tr(flat(2)[:, 24 * k:24 * k + 24], st_tok[:, P * k:P * k + P], 24)
            for k in range(LT):
                last = tr(flat(2)[:, 96 + NS * k:96 + NS * k + NS], h0_tok[:, P * k:P * k + P], NS)
            last.then_inc(psum_full[2], 1)
            pe.wait_ge(s_silu, 2)
            for k in range(KT):
                last = tr(flat(3)[:, 9 * k:9 * k + 9], c_tok[:, P * k:P * k + P], 9)
            last.then_inc(psum_full[3], 1)
            pe.wait_ge(s_x, 64)
            for k in range(KT):
                j = J_XT + k
                claim(pe, j)
                for a in range(4):
                    tr(flat(j)[:, P * a:P * a + P], x_tok[:, a, P * k:P * k + P], P)
                tr(flat(j)[:, NP:T], xs_tok[:, P * k:P * k + P], NS).then_inc(psum_full[j % 4], 1)

            def mod_rows(n):
                j = J_ROW[n]
                claim(pe, j)
                for c in range(4):
                    if n < 2:
                        pe.wait_ge(s_ada[c], 16 * (n + 1))
                    else:
                        pe.wait_ge(s_ada2[c], 16 * (n - 1))
                    for k in range(KT):
                        last = mm(flat(j)[0:9, 256 * c:256 * c + 256], cT[:, k, :], ring[:, c, k, :], start=(k == 0), stop=(k == KT - 1))
                    last.then_inc(s_ada_used if c < 3 else psum_full[j % 4], 1)

            def mod_columns(n):
                j = J_COL[n]
                claim(pe, j)
                pe.wait_ge(psum_free[J_ROW[n] % 4], free_value(J_ROW[n]))
                for m in range(8):
                    last = tr(flat(j)[:, 9 * m:9 * m + 9], rows9(n)[:, P * m:P * m + P], 9)
                last.then_inc(psum_full[j % 4], 1)

            pe.wait_ge(psum_free[3], 1)
            mod_rows(0)
            mod_rows(1)
            mod_columns(0)
            mod_columns(1)

            def norm_sum(j, n, base, first=0):
                claim(pe, j)
                for k in range(n):
                    pe.wait_ge(s_sq, base + k + 1)
                    last = both(j, ones, sq[:, first + k, :], k == 0, k == n - 1)
                last.then_inc(psum_full[j % 4], 1)

            norm_sum(J_N1, KT, 0)
            def w_in(n):
                m = WIN_ORDER[n]
                j = J_WIN[m]
                rows = (0, P) if m < 11 else (NOPE, QK)
                w = P if m < 11 else ROPE
                claim(pe, j)
                pe.wait_ge(s_win[n % 4], 16 * (n // 4 + 1))
                for k in range(KT):
                    if n == 0:
                        pe.wait_ge(s_h, k + 1)
                        pe.wait_ge(s_hd, 1)
                    last = both(j, RA[:, n % 4, k, 0:w], hT[:, k, :], k == 0, k == KT - 1, rows)
                last.then_inc(psum_full[j % 4], 1)

            for n in range(8):
                w_in(n)
            pe.wait_ge(s_bd, 64)
            for g in range(2):
                for k in range(LT):
                    j = J_GATE + g * LT + k
                    claim(pe, j)
                    pe.wait_ge(s_xc, k + 1)
                    both(j, BD[:, g, k, :], XC[:, k, :], True, True).then_inc(psum_full[j % 4], 1)
            w_in(8)
            w_in(9)
            norm_sum(J_NQ, 2, KT)
            norm_sum(J_NKV, 1, KT + 2, 2)
            R = (NOPE, QK)
            j = J_KR[0]
            claim(pe, j)
            pe.wait_ge(s_sq, KT + 4)
            both(j, C("blk", QK, R)[:, NOPE:QK], sq[NOPE:QK, 3, :], True, True, R).then_inc(psum_full[j % 4], 1)
            w_in(10)
            w_in(11)
            j = J_KR[1]
            claim(pe, j)
            pe.wait_ge(s_kr, 1)
            both(j, C("perm", QK, R)[:, NOPE:QK], krT[NOPE:QK, :], True, True, R).then_inc(psum_full[j % 4], 1)
            mod_rows(2)
            mod_rows(3)
            mod_columns(2)
            norm_sum(J_NLRU, LT, KT + 4, 4)
            mod_rows(4)
            mod_columns(3)
            pe.wait_ge(s_kr, 2)
            pe.wait_ge(s_kvn, 1)
            for a in range(5):
                j = J_LOUT + a
                n = P if a < 4 else NS
                claim(pe, j)
                tr(flat(j)[0:n, 0:KV], kvT[:, P * a:P * a + n], P)
                mm(flat(j)[0:n, KV:KV + ROPE], krT[NOPE:QK, P * a:P * a + n], C("ident", QK, R)[:, NOPE:QK],
                   start=True, stop=True).then_inc(psum_full[j % 4], 1)
            pe.wait_ge(s_lrud, 1)
            for n, (src, c0, w) in enumerate(((TA, NP - 1, 9), (XX, NP, 11))):
                j = J_LOUT + 5 + n
                claim(pe, j)
                for k in range(LT):
                    last = tr(flat(j)[0:w, P * k:P * k + P], src[:, k, c0:c0 + w], P)
                last.then_inc(psum_full[j % 4], 1)

            mod_rows(5)
            mod_columns(4)
            mod_columns(5)

            def project(J, e, pair, lap):
                pe.wait_ge(s_hw[e], 32 * (pair + 1))
                claim(pe, J.q[e], lap)
                for k in range(2):
                    last = both(J.q[e], wuq[:, e, k, :], qlT[:, k, :], k == 0, k == 1, (0, QK))
                last.then_inc(psum_full[J.q[e] % 4], 1)
                claim(pe, J.kn[e], lap)
                mm(flat(J.kn[e])[0:NOPE, 0:NP], wukv[:, e, 0:NOPE], kvT[:, 0:NP], start=True, stop=True).then_inc(psum_full[J.kn[e] % 4], 1)

            def mean_squares(J, e, pair, lap):
                claim(pe, J.qms[e], lap)
                pe.wait_ge(s_qsq, 2 * pair + e + 1)
                both(J.qms[e], C("blk", QK, (0, QK)), sq[0:QK, 2 * e, :], True, True, (0, QK)).then_inc(psum_full[J.qms[e] % 4], 1)
                claim(pe, J.kms[e], lap)
                pe.wait_ge(s_ksq, 2 * pair + e + 1)
                mm(flat(J.kms[e])[:, 0:NP], C("blk", P, (0, NOPE)), sq[0:NOPE, 4 + 2 * e, 0:NP], start=True,
                   stop=True).then_inc(psum_full[J.kms[e] % 4], 1)

            def rotate(J, e, pair, lap):
                claim(pe, J.qrot[e], lap)
                pe.wait_ge(s_qn, 2 * pair + e + 1)
                both(J.qrot[e], C("perm", QK, (0, QK))[:, NOPE:QK], hb[e]["q"][0:QK, :], True, True, R).then_inc(psum_full[J.qrot[e] % 4], 1)

            def values(J, e, lap):
                claim(pe, J.vw[e], lap)
                for a in range(4):
                    mm(flat(J.vw[e])[:, VD * a:VD * a + VD], kvT[:, P * a:P * a + P], wukv[:, e, NOPE:P], start=True, stop=True)
                tr(flat(J.vw[e])[0:NOPE, 512:512 + P], wukv[:, e, 0:NOPE], P).then_inc(psum_full[J.vw[e] % 4], 1)

            def through_keys(J, e, pair, lap):
                claim(pe, J.qa[e], lap)
                pe.wait_ge(s_gq, 2 * pair + e + 1)
                pe.wait_ge(psum_free[J.vw[e] % 4], free_value(J.vw[e], lap))
                mm(flat(J.qa[e])[:, 0:NS], hb[e]["wt"][0:NOPE, :], hb[e]["gq"][0:NOPE, :], start=True, stop=True).then_inc(psum_full[J.qa[e] % 4], 1)

            def scores(J, e, pair, lap):
                pe.wait_ge(s_qr, 2 * pair + e + 1)
                pe.wait_ge(s_kn, 2 * pair + e + 1)
                for n in range(4):
                    j = J.s[e][n]
                    claim(pe, j, lap)
                    mm(flat(j)[:, 0:P * (n + 1)], hb[e]["q"][0:QK, P * n:P * n + P], hb[e]["k"][0:QK, 0:P * (n + 1)],
                       start=True, stop=True).then_inc(psum_full[j % 4], 1)

            def turn_probs(J, e, pair, lap):
                for n in range(4):
                    j = J.p[e][n]
                    claim(pe, j, lap)
                    pe.wait_ge(s_pn, 8 * pair + 4 * e + n + 1)
                    for a in range(n + 1):
                        last = tr(flat(j)[:, P * a:P * a + P], hb[e]["p"][:, POFF[n] + P * a:POFF[n] + P * a + P], P)
                    last.then_inc(psum_full[j % 4], 1)

            def mix(J, e, lap):
                claim(pe, J.pv[e], lap)
                for n in range(4):
                    pe.wait_ge(psum_free[J.p[e][n] % 4], free_value(J.p[e][n], lap))
                for a in range(4):
                    last = mm(flat(J.pv[e])[VD * e:VD * e + VD, P * a:NP], hb[e]["v"][:, VD * a:VD * a + VD],
                              hb[e]["pt"][:, a, P * a:NP], start=(a == 0), stop=(a == 3))
                last.then_inc(psum_full[J.pv[e] % 4], 1)

            pe.wait_ge(s_ql, 2)
            J = HEAD_FIRST
            for e in range(2):
                project(J, e, 0, 0)
            for e in range(2):
                mean_squares(J, e, 0, 0)
            for e in range(2):
                rotate(J, e, 0, 0)
            for e in range(2):
                values(J, e, 0)
            for e in range(2):
                through_keys(J, e, 0, 0)
            with pe.Fori(0, HEAD_LAPS) as i:
                J, lap = HEAD_LAP, HEAD_LAP.count // 4 * i
                for e in range(2):
                    scores(J, e, i, lap)
                for e in range(2):
                    project(J, e, i + 1, lap)
                turn_probs(J, 0, i, lap)
                for e in range(2):
                    mean_squares(J, e, i + 1, lap)
                turn_probs(J, 1, i, lap)
                for e in range(2):
                    rotate(J, e, i + 1, lap)
                for e in range(2):
                    mix(J, e, lap)
                for e in range(2):
                    values(J, e, lap)
                for e in range(2):
                    through_keys(J, e, i + 1, lap)
            J = HEAD_LAST
            for e in range(2):
                scores(J, e, HEAD_LAPS, 0)
            for e in range(2):
                turn_probs(J, e, HEAD_LAPS, 0)
            for e in range(2):
                mix(J, e, 0)

            j = J_SPREAD
            claim(pe, j)
            pe.wait_ge(s_qr, HEADS)
            mm(flat(j)[:, 0:NS * HEADS], C("spread", P, R), QRS[NOPE:QK, :, :], start=True, stop=True).then_inc(psum_full[j % 4], 1)
            pe.wait_ge(s_qbd, 1)
            pe.wait_ge(s_kw, 4)

            def pv(j, lap, e, v):
                claim(pe, j, lap)
                pe.wait_ge(s_pd, v)
                for n in range(KTILES):
                    last = mm(flat(j)[0:HEADS, 0:KV], snd[e][:, HEADS * n:HEADS * n + HEADS], lat[e][:, n, :], start=(n == 0), stop=(n == KTILES - 1))
                last.then_inc(psum_full[j % 4], 1)
                claim(pe, j + 1, lap)
                mm(flat(j + 1)[0:HEADS, 0:1], pd[e], ones[:, 0:1], start=True, stop=True).then_inc(psum_full[(j + 1) % 4], 1)

            def transposes(j, lap, e, v, g):
                claim(pe, j, lap)
                if g == 0:
                    pe.wait_ge(s_krc[e], 8 * (v + 1 - e))
                    pe.wait_ge(s_lat[0][e], 8 * (v + 1 - e))
                if g == 4:
                    pe.wait_ge(s_lat[1][e], 8 * (v + 1 - e))
                if g == NG - 1:
                    pe.wait_ge(s_newc, 2 * v)
                for n in range(GT[g]):
                    c = P * (4 - GT[g] + n)
                    tr(flat(j)[:, c:c + P], lat[e][:, 4 * g + n, :], P)
                tr(flat(j)[:, 512:512 + P], kr_[e][:, 4 * g:4 * g + 4, :].rearrange("p c d -> p (c d)"), P).then_inc(psum_full[j % 4], 1)

            def unit(base, lap, e, s, v):
                s_ = s if isinstance(s, int) else bass.ds(s, 1)

                pe.wait_ge(s_kwq, 2 * v)
                for g in range(NG):
                    if g + 2 < NG:
                        transposes(unit_job(base, "t", g + 2), lap, e, v, g + 2)
                    elif base != J_LAST:
                        transposes(unit_job(base, "tn", g + 2 - NG), lap, 1 - e, v + 1, g + 2 - NG)
                    t_ = unit_job(base, "t", g)
                    pe.wait_ge(psum_free[t_ % 4], free_value(t_, lap))
                    pe.wait_ge(s_lo, NG * (v - 1) + g + 1)
                    for n in range(GT[g]):
                        j = unit_job(base, "k", 4 * g + n)
                        claim(pe, j, lap)
                        if n == 0:
                            mm(ps[j % 4][:, 0, KWW:KWW + 4 * HEADS], turned[:, g % 3, 4 * P:5 * P], QBD[:, s_, :, :], start=True, stop=True)
                        at = P * (4 - GT[g] + n)
                        products = ((latH, kwH), (latH, kwL), (latL, kwH))
                        for i, (a, b) in enumerate(products):
                            for h in range(2):
                                last = mm(ps[j % 4][:, h, 0:KWW], a[:, g % 3, at:at + P], b[:, e, h, :],
                                          start=(i == 0), stop=(i == 2))
                        last.then_inc(psum_full[j % 4], 1)
                    if g == PV_AT and base != J_DEC:
                        pv(unit_job(base, "pv", 0), lap, 1 - e, v - 1)

            for g in range(2):
                transposes(J_FIRST_T + g, 0, 0, 1, g)
            unit(J_DEC, 0, 0, 0, 1)
            with pe.Fori(0, 3) as i:
                unit(J_UNIT1, 2 * UNIT // 4 * i, 1, 2 * i + 1, 2 * i + 2)
                unit(J_UNIT1 + UNIT, 2 * UNIT // 4 * i, 0, 2 * i + 2, 2 * i + 3)
            unit(J_LAST, 0, 1, 7, 8)
            pv(J_PVLAST, 0, 1, NS)
            claim(pe, J_OL)
            pe.wait_ge(psum_free[J_PVLAST % 4], free_value(J_PVLAST))
            for n in range(NS):
                last = tr(flat(J_OL)[:, HEADS * n:HEADS * n + HEADS], OLR[:, n, :], HEADS)
            last.then_inc(psum_full[J_OL % 4], 1)
            j = J_VP
            claim(pe, j)
            pe.wait_ge(s_wv, 16)
            pe.wait_ge(psum_free[J_OL % 4], free_value(J_OL))
            for h in range(HEADS):
                last = mm(flat(j)[VD * (h % 2):VD * (h % 2) + VD, NS * (h // 2):NS * (h // 2) + NS], wv[:, h, :], OL[:, :, h], start=True, stop=True)
            last.then_inc(psum_full[j % 4], 1)
            norm_sum(J_NMLA, LT, KT + 8)
            def three(j, wH, wL, m, srcH, srcL, k, first, final):
                for n, (w, src) in enumerate(((wH, srcH), (wH, srcL), (wL, srcH))):
                    last = both(j, w[:, m, :], src[:, k, :], first and n == 0, final and n == 2)
                return last

            for m in range(KT):
                j = J_WO + m
                claim(pe, j)
                pe.wait_ge(s_wolo, m + 1)
                for k in range(KT):
                    if m == 0:
                        pe.wait_ge(s_mlo, k + 1)
                    last = three(j, woH[:, m % 2, :, :], woL[:, m % 2, :, :], k, mxH, mxL, k, k == 0, k == KT - 1)
                last.then_inc(psum_full[j % 4], 1)
            norm_sum(J_N2, KT, KT + 12)
            j = J_FST
            claim(pe, j)
            pe.wait_ge(s_fst, 16)
            for m in range(2 * FT):
                last = tr(flat(j)[:, 2 * NS * m:2 * NS * m + 2 * NS], fs_tok[:, P * m:P * m + P], 2 * NS)
            last.then_inc(psum_full[j % 4], 1)
            with pe.Fori(0, FT // 2) as i:
                for e in range(2):
                    for g in range(2):
                        j = J_UP + 2 * e + g
                        claim(pe, j, i)
                        pe.wait_ge(s_wlo, 4 * i + 2 * e + g + 1)
                        for k in range(KT):
                            if e == 0 and g == 0:
                                pe.wait_ge(s_hlo, k + 1)
                            last = three(j, wuH, wuL, KT * g + k, hH, hL, k, k == 0, k == KT - 1)
                        last.then_inc(psum_full[j % 4], 1)
            for m in range(KT):
                j = J_DOWN + m
                claim(pe, j)
                for k in range(FT):
                    if k % (FT // 2) == 0:
                        pe.wait_ge(s_wlo, 2 * FT + 2 * m + 1 + k // (FT // 2))
                    if m == 0 and k in (0, FT - 2, FT - 1):
                        pe.wait_ge(s_hid, max(k + 1, FT - 2))
                    last = three(j, wdH[m % 2], wdL[m % 2], k, actH, actL, k, k == 0, k == FT - 1)
                last.then_inc(psum_full[j % 4], 1)
            pe.wait_ge(s_x2, KT)
            for n in range(5):
                j = J_Y + n
                w = P if n < 4 else NS
                claim(pe, j)
                for k in range(KT):
                    last = tr(flat(j)[0:w, P * k:P * k + P], xT[:, k, P * n:P * n + w], P)
                last.then_inc(psum_full[j % 4], 1)
            for n in range(6):
                j = J_FT + n
                claim(pe, j)
                for m in range(8 * n, min(8 * n + 8, 2 * FT)):
                    last = tr(flat(j)[0:10, P * (m - 8 * n):P * (m - 8 * n) + P], UT[:, m, :], P)
                last.then_inc(psum_full[j % 4], 1)

        @block.scalar
        def _(act):
            A = nc.scalar.activation
            st = Steps(act, s_act)

            def rstd(j, width, rows=(0, P), lap=0, dst=None):
                full(act, j, lap)
                dst = rs[rows[0]:rows[1], :] if dst is None else dst
                A(two(dst), halves(j, rows), ACT.Ln, bias=epsc[rows[0]:rows[1], :], scale=1.0 / width).then_inc(psum_free[j % 4], 1)
                act.wait_ge(psum_free[j % 4], free_value(j, lap))
                return A(dst, dst, ACT.Exp, scale=-0.5)

            epsc = small[:, 0:1]
            act.wait_ge(s_x, 64)
            A(c_th, c_tok, ACT.Tanh, scale=0.5).then_inc(s_silu, 1)
            act.wait_ge(s_sp, 1)
            A(small[:, 8:12], small[:, 4:8], ACT.Exp, scale=-1.0).then_inc(s_sp, 1)
            for k in range(KT):
                j = J_XT + k
                full(act, j)
                A(xT[:, k, :], flat(j)[:, 0:T], ACT.Copy).then_inc(psum_free[j % 4], 1)
                act.wait_ge(psum_free[j % 4], free_value(j))
                A(sq[:, k, :], xT[:, k, :], ACT.Square).then_inc(s_sq, 1)
            rstd(J_N1, D).then_inc(s_rs, 1)
            for k in range(KT):
                act.wait_ge(s_hp, k + 1)
                A(hT[:, k, 0:NP], hT[:, k, 0:NP], ACT.Identity, bias=modT[:, k, 0:1], scale=gmod[:, k, 0:1]).then_inc(s_h, 1)
            for m, dst in ((8, qlT[:, 0, :]), (9, qlT[:, 1, :]), (10, kvT[:, :]), (11, krT[NOPE:QK, :])):
                j = J_WIN[m]
                rows = (0, P) if m < 11 else (NOPE, QK)
                full(act, j)
                A(two(dst), halves(j, rows), ACT.Copy).then_inc(psum_free[j % 4], 1)
                act.wait_ge(psum_free[j % 4], free_value(j))
                A(sq[rows[0]:rows[1], m - 8, :], dst, ACT.Square).then_inc(s_sq, 1)
            act.wait_ge(s_sp, 3)
            for g, dst in ((0, TA), (1, TI)):
                for k in range(LT):
                    j = J_GATE + g * LT + k
                    full(act, j)
                    A(two(dst[:, k, :]), halves(j), ACT.Tanh, bias=small[:, 20 + 4 * g + k:21 + 4 * g + k],
                      scale=0.5).then_inc(psum_free[j % 4], 1)
            for k in range(LT):
                act.wait_ge(psum_free[(J_GATE + k) % 4], free_value(J_GATE + k))
            for k in range(LT):
                v = st.did(A(AA[:, k, :], TA[:, k, :], ACT.Exp, bias=small[:, 32 + k:33 + k], scale=small[:, 32 + k:33 + k]))
            st.need(v)
            for k in range(LT):
                A(TA[:, k, :], TA[:, k, :], ACT.Tanh, bias=small[:, 28 + k:29 + k], scale=small[:, 28 + k:29 + k]).then_inc(s_ta, 1)

            def gate_branch(k):
                j = J_WIN[LT + k]
                full(act, j)
                A(two(GG[:, k, :]), halves(j), ACT.Copy).then_inc(psum_free[j % 4], 1)

            nc.scalar.preload_act_table_set("natural_log_exp_and_others")
            gate_branch(0)
            act.wait_ge(s_tiny, 1)
            st.did(A(sq[:, 4:8, :], TA[:, :, :], ACT.Ln, bias=1.0))
            st.seq(A(TA[:, :, :], TA[:, :, :], ACT.Ln))
            act.sem_inc(s_lru, 1)
            gate_branch(1)
            act.wait_ge(s_tiny, 2)
            A(TA[:, :, :], TA[:, :, :], ACT.Exp, scale=0.5).then_inc(s_lru, 1)
            rstd(J_NQ, QL, dst=sq[:, 0, :]).then_inc(s_rs, 1)
            rstd(J_NKV, KV, dst=sq[:, 1, :]).then_inc(s_rs, 1)
            rstd(J_KR[0], 1, (NOPE, QK), dst=sq[NOPE:QK, 2, :]).then_inc(s_rs, 1)
            gate_branch(2)
            gate_branch(3)
            for k in range(LT):
                act.wait_ge(psum_free[J_WIN[LT + k] % 4], free_value(J_WIN[LT + k]))
            A(GG[:, :, :], GG[:, :, :], ACT.Gelu_apprx_tanh).then_inc(s_g, 1)
            nc.scalar.preload_act_table_set("natural_log_exp_and_others")
            act.wait_ge(s_lrud, 2)
            for k in range(LT):
                A(sq[:, 4 + k, :], XC[:, k, :], ACT.Square).then_inc(s_sq, 1)
            rstd(J_NLRU, LW).then_inc(s_rs, 1)

            def copy_out(j, dst, src, lap=0):
                full(act, j, lap)
                A(dst, src, ACT.Copy).then_inc(psum_free[j % 4], 1)
                act.wait_ge(psum_free[j % 4], free_value(j, lap))

            def projected(J, e, lap):
                q, k = hb[e]["q"][0:QK, :], hb[e]["k"][0:NOPE, :]
                copy_out(J.q[e], two(q), halves(J.q[e], (0, QK)), lap)
                A(sq[0:QK, 2 * e, :], q, ACT.Square).then_inc(s_qsq, 1)
                copy_out(J.kn[e], k, flat(J.kn[e])[0:NOPE, 0:NP], lap)
                A(sq[0:NOPE, 4 + 2 * e, 0:NP], k, ACT.Square).then_inc(s_ksq, 1)

            def head_rstd(J, e, lap):
                rstd(J.qms[e], 1, (0, QK), lap, sq[0:QK, 2 * e + 1, :]).then_inc(s_qrs, 1)
                r = sq[0:NOPE, 5 + 2 * e, 0:NP]
                full(act, J.kms[e], lap)
                A(r, flat(J.kms[e])[0:NOPE, 0:NP], ACT.Ln, bias=epsc[0:NOPE, :]).then_inc(psum_free[J.kms[e] % 4], 1)
                act.wait_ge(psum_free[J.kms[e] % 4], free_value(J.kms[e], lap))
                A(r, r, ACT.Exp, scale=-0.5).then_inc(s_krs, 1)

            def head_probs(J, e, pair):
                for n in range(4):
                    j = J.s[e][n]
                    act.wait_ge(s_nm, 8 * pair + 4 * e + n + 1)
                    A(hb[e]["p"][:, POFF[n]:POFF[n] + P * (n + 1)], flat(j)[:, 0:P * (n + 1)], ACT.Exp,
                      bias=hb[e]["nm"][:, n:n + 1], scale=SCALE, accum_out=hb[e]["l"][:, n:n + 1]).then_inc(psum_free[j % 4], 1)

            for e in range(2):
                projected(HEAD_FIRST, e, 0)
            for e in range(2):
                head_rstd(HEAD_FIRST, e, 0)
            with act.Fori(0, HEAD_LAPS) as i:
                nc.scalar.preload_act_table_set("natural_log_exp_and_others")
                lap = HEAD_LAP.count // 4 * i
                for e in range(2):
                    head_probs(HEAD_LAP, e, i)
                for e in range(2):
                    projected(HEAD_LAP, e, lap)
                for e in range(2):
                    head_rstd(HEAD_LAP, e, lap)
            nc.scalar.preload_act_table_set("natural_log_exp_and_others")
            for e in range(2):
                head_probs(HEAD_LAST, e, HEAD_LAPS)

            def rstd_keys(e, v):
                act.wait_ge(s_sqr, KTILES * v)
                A(ssd[e], ssd[e], ACT.Ln, bias=epsc, scale=1.0 / NOPE).then_inc(s_act2, 1)
                act.wait_ge(s_act2, v)
                A(ssd[e], ssd[e], ACT.Exp, scale=-0.5).then_inc(s_drs, 1)

            def probs(e, v):
                act.wait_ge(s_sh, v)
                A(snd[e], snd[e], ACT.Exp, scale=SCALE).then_inc(s_dp, 1)

            def latents(j, lap, g):
                full(act, j, lap)
                n = GT[g] * P
                A(turned[:, g % 3, 4 * P - n:5 * P], flat(j)[:, 4 * P - n:5 * P], ACT.Copy).then_inc(s_tT, 1)
                A(latH[:, g % 3, 4 * P - n:4 * P], flat(j)[:, 4 * P - n:4 * P], ACT.Copy).then_inc(psum_free[j % 4], 1)

            def unit(base, lap, e, v):
                for g in range(NG):
                    if g + 2 < NG:
                        latents(unit_job(base, "t", g + 2), lap, g + 2)
                    elif base != J_LAST:
                        latents(unit_job(base, "tn", g + 2 - NG), lap, g + 2 - NG)
                    for n in range(GT[g]):
                        c = 4 * g + n
                        j = unit_job(base, "k", c)
                        if base != J_DEC or c >= 3:
                            act.wait_ge(s_sqr, KTILES * (v - 1) + c - 2)
                        full(act, j, lap)
                        A(sqd[c % 3].rearrange("p (h n) -> p h n", h=2), ps[j % 4][:, :, 0:4 * NOPE], ACT.Square).then_inc(s_sqd, 1)
                    if base != J_DEC and g == 0:
                        rstd_keys(1 - e, v - 1)
                    if base != J_DEC and g == 2:
                        probs(1 - e, v - 1)

            for g in range(2):
                latents(J_FIRST_T + g, 0, g)
            unit(J_DEC, 0, 0, 1)
            with act.Fori(0, 3) as i:
                nc.scalar.preload_act_table_set("natural_log_exp_and_others")
                unit(J_UNIT1, 2 * UNIT // 4 * i, 1, 2 * i + 2)
                unit(J_UNIT1 + UNIT, 2 * UNIT // 4 * i, 0, 2 * i + 3)
            unit(J_LAST, 0, 1, 8)
            rstd_keys(1, NS)
            probs(1, NS)

            act.wait_ge(psum_free[J_VP % 4], free_value(J_VP))
            for k in range(LT):
                A(sq[:, k, :], hT[:, LT + k, :], ACT.Square).then_inc(s_sq, 1)

            def out_high(m):
                act.wait_ge(s_wo[m % 3], 16 * (m // 3 + 1))
                if m >= 2:
                    full(act, J_WO + m - 2)
                A(woH[:, m % 2, :, :], woR[:, m % 3, :, :], ACT.Copy).then_inc(s_wohi, 1)

            for k in range(LT):
                A(mxH[:, k, :], hT[:, k, :], ACT.Copy).then_inc(s_mhi, 1)
            out_high(0)
            act.wait_ge(s_mix, LT)
            rstd(J_NMLA, LW).then_inc(s_rs, 1)
            for k in range(LT, KT):
                act.wait_ge(s_mix, k + 1)
                A(mxH[:, k, :], hT[:, k, :], ACT.Copy).then_inc(s_mhi, 1)
            out_high(1)

            def up_high(c, g, loads, before=None, lap=0):
                act.wait_ge(s_wup[c], 32 * loads)
                if before is not None:
                    full(act, before, lap)
                A(wuH[:, KT * g:KT * g + KT, :], wup[:, c, KT * g:KT * g + KT, :], ACT.Copy).then_inc(s_whi, 1)

            for k in range(KT):
                if k + 2 < KT:
                    out_high(k + 2)
                act.wait_ge(s_x1, k + 1)
                A(sq[:, k, :], xT[:, k, :], ACT.Square).then_inc(s_sq, 1)
                if k == 3:
                    full(act, J_PVLAST + 1)
                    up_high(0, 0, 1)
                    up_high(0, 1, 1)
            act.wait_ge(s_mix, 2 * LT)
            rstd(J_N2, D).then_inc(s_rs, 1)
            for k in range(KT):
                act.wait_ge(s_hp, KT + k + 1)
                A(h2[:, k, 0:NP], h2[:, k, 0:NP], ACT.Identity, bias=modT[:, 3 * KT + k, 0:1], scale=gmod[:, k, 0:1]).then_inc(s_h, 1)
                act.wait_ge(s_h, KT + k + 1)
                A(hH[:, k, :], h2[:, k, :], ACT.Copy).then_inc(s_hhi, 1)
            act.wait_ge(s_pads, 2)
            def evacuate(m, i, e, g):
                act.wait_ge(s_cvfree, m + 1)
                j = J_UP + 2 * e + g
                full(act, j, i)
                A(two(UU[e % 2][:, g, 2:UW]), halves(j), ACT.Copy).then_inc(psum_free[j % 4], 1)

            def down_high(m):
                act.wait_ge(s_wdn[m % 2], 16 * (m // 2 + 1))
                full(act, J_UP + 2 * FT - 1 if m < 2 else J_DOWN + m - 2)
                if m == 1:
                    act.wait_ge(s_hid, FT)
                    act.wait_ge(s_ut, 2 * FT)
                for a in (0, FT // 2):
                    A(wdH[m % 2][:, a:a + FT // 2, :], wdn[:, m % 2, a:a + FT // 2, :], ACT.Copy).then_inc(s_whi, 1)

            def mlp(i, e, left):
                m = 2 * i + e
                if left >= 1:
                    up_high(1 - e, 1, i + 1 + e, J_UP + 2 * e + 1, i)
                evacuate(m, i, e, 1)
                if left >= 2:
                    up_high(e, 0, i + 2, J_UP + 2 * e + 2, i)
                if left >= 1:
                    evacuate(m + 1, i, e + 1, 0)
                else:
                    down_high(0)
                act.wait_ge(s_cv, m + 1)
                A(GE, CV[1], ACT.Gelu_apprx_tanh).then_inc(s_ge, 1)

            up_high(1, 0, 1, J_UP)
            evacuate(0, 0, 0, 0)
            with act.Fori(0, FT // 2 - 1) as i:
                mlp(i, 0, 2)
                mlp(i, 1, 2)
            mlp(FT // 2 - 1, 0, 1)
            mlp(FT // 2 - 1, 1, 0)
            for m in range(1, KT):
                down_high(m)
            for n in (0, 2, 4):
                j = J_Y + n
                w = P if n < 4 else NS
                full(act, j)
                A(y_tok[n][0:w, :], flat(j)[0:w, :], ACT.Copy).then_inc(psum_free[j % 4], 1)

        @block.vector
        def _(dve):
            V = nc.vector
            st = Steps(dve, s_dve)
            MUL, ADD, SUB = ALU.mult, ALU.add, ALU.subtract

            def copy_out(j, dst, src, ready=None):
                full(dve, j)
                V.tensor_copy(dst, src).then_inc(psum_free[j % 4], 1)
                dve.wait_ge(psum_free[j % 4], free_value(j))

            st.did(V.memset(small[:, 0:1], EPS))
            st.did(V.memset(small[:, 1:2], 0.0))
            dve.wait_ge(s_cst, 16)
            dve.wait_ge(s_pt, 64)
            V.tensor_scalar(row_of[:, :], page_of[:, :], 4.0, C("quarter", 1), MUL, ADD).then_inc(s_row, 1)
            dve.wait_ge(s_row, 1)
            for n in range(2):
                V.tensor_scalar(half_of[:, n, :], row_of[:, :], 2.0, float(n), MUL, ADD).then_inc(s_row, 1)
            dve.wait_ge(s_silu, 1)
            V.scalar_tensor_tensor(c_tok, c_th, 1.0, c_tok, ADD, MUL).then_inc(s_silu, 1)
            copy_out(0, par[:, :], flat(0)[:, 0:NROWS])
            copy_out(1, fpar[:, :], flat(1)[:, 0:8 * FT])
            full(dve, 2)
            st.did(V.tensor_copy(stT[:, :], flat(2)[:, 0:96]))
            V.tensor_copy(h0T[:, :], flat(2)[:, 96:128]).then_inc(psum_free[2], 1)
            full(dve, 3)
            V.tensor_scalar(cT[:, :, :], flat(3)[:, 0:72].rearrange("p (k n) -> p k n", n=9), 0.5, None, MUL).then_inc(psum_free[3], 1)
            lam = pr("lru_lambda", 0, 4)
            st.seq(V.tensor_scalar(small[:, 36:40], lam, -1.0, None, MUL))
            V.tensor_tensor(small[:, 4:8], small[:, 36:40], lam, ALU.max).then_inc(s_sp, 1)
            dve.wait_ge(s_sp, 2)
            u, z, acc, z2 = small[:, 8:12], small[:, 12:16], small[:, 16:20], small[:, 40:44]
            st.seq(V.tensor_scalar(acc, u, 2.0, None, ADD))
            st.seq(V.reciprocal(acc, acc))
            st.seq(V.tensor_tensor(z, u, acc, MUL))
            st.seq(V.tensor_tensor(z2, z, z, MUL))
            st.seq(V.tensor_scalar(acc, z2, 2.0 / 17, 2.0 / 15, MUL, ADD))
            for n in range(6, -1, -1):
                st.seq(V.tensor_tensor(acc, acc, z2, MUL))
                st.seq(V.tensor_scalar(acc, acc, 2.0 / (2 * n + 1), None, ADD))
            st.seq(V.tensor_tensor(acc, acc, z, MUL))
            st.seq(V.tensor_scalar(small[:, 36:40], small[:, 36:40], 0.0, None, ALU.max))
            st.seq(V.tensor_tensor(acc, acc, small[:, 36:40], ADD))
            st.did(V.tensor_scalar(small[:, 28:32], acc, 4.0, None, MUL))
            st.did(V.tensor_scalar(small[:, 32:36], acc, -4.0, None, MUL))
            v = st.did(V.tensor_scalar(small[:, 20:24], pr("lru_b_a", 0, 4), 0.5, None, MUL))
            st.need(v)
            V.tensor_scalar(small[:, 24:28], pr("lru_b_x", 0, 4), 0.5, None, MUL).then_inc(s_sp, 1)
            def mod_rows(n):
                full(dve, J_ROW[n])
                V.tensor_copy(rows9(n), flat(J_ROW[n])[0:9, :]).then_inc(psum_free[J_ROW[n] % 4], 1)

            def mod_columns(n):
                j, m = J_COL[n], 8 * n
                full(dve, j)
                V.tensor_tensor(modT[:, m:m + 8, :], flat(j)[:, 0:72].rearrange("p (m n) -> p m n", n=9),
                                pr("b_ada", m, 8).unsqueeze(2).to_broadcast([P, 8, 9]), ADD).then_inc(psum_free[j % 4], 1)

            mod_rows(0)
            mod_rows(1)
            mod_columns(0)
            mod_columns(1)
            for n in range(2):
                dve.wait_ge(psum_free[J_COL[n] % 4], free_value(J_COL[n]))
            st.seq(V.tensor_scalar(gmod[:, :, :], modT[:, KT:2 * KT, :], 1.0, None, ADD))
            st.seq(V.tensor_tensor(gmod[:, :, :], gmod[:, :, :], pr("norm1_g", 0, KT).unsqueeze(2).to_broadcast([P, KT, 9]), MUL))
            dve.wait_ge(s_rs, 1)
            for k in range(KT):
                V.tensor_tensor(hT[:, k, :], xT[:, k, :], rs[:, :], MUL).then_inc(s_hp, 1)
            dve.wait_ge(s_hp, KT)
            st.seq(V.tensor_tensor(hT[:, :, NP:T], hT[:, :, NP:T], gmod[:, :, 1:9], MUL))
            V.tensor_tensor(hT[:, :, NP:T], hT[:, :, NP:T], modT[:, 0:KT, 1:9], ADD).then_inc(s_hd, 1)

            full(dve, J_WIN[0])
            v = st.did(V.memset(XX[:, :, 0:3], 0.0))
            for k in range(LT):
                j = J_WIN[k]
                full(dve, j)
                V.tensor_copy(two(XX[:, k, 3:3 + T]), halves(j)).then_inc(psum_free[j % 4], 1)
            st.need(v)
            for tap in range(4):
                for k in range(LT):
                    w = pr("lru_conv_w", 4 * tap + k)
                    x = XX[:, k, tap:tap + NP]
                    if tap == 0:
                        dve.wait_ge(psum_free[J_WIN[k] % 4], free_value(J_WIN[k]))
                        v = st.did(V.tensor_scalar(XC[:, k, 0:NP], x, w, pr("lru_conv_b", k), MUL, ADD))
                    else:
                        v = st.did(V.scalar_tensor_tensor(XC[:, k, 0:NP], x, w, XC[:, k, 0:NP], MUL, ADD))
                st.need(v)
            dec, tmp = XC[:, :, NP:T], AA[:, :, 0:NS]
            for tap in range(4):
                w = pr("lru_conv_w", 4 * tap, 4).unsqueeze(2).to_broadcast([P, LT, NS])
                x = st4[:, :, :, tap] if tap < 3 else XX[:, :, 3 + NP:3 + T]
                st.seq(V.tensor_tensor(tmp, x, w, MUL))
                other = pr("lru_conv_b", 0, 4).unsqueeze(2).to_broadcast([P, LT, NS]) if tap == 0 else dec
                ins = V.tensor_tensor(dec, tmp, other, ADD)
                if tap < 3:
                    st.seq(ins)
                else:
                    ins.then_inc(s_xc, 4)
            for k in range(LT):
                j = J_GATE + LT + k
                dve.wait_ge(psum_free[j % 4], free_value(j))
            dve.wait_ge(s_xc, 4)
            v = st.did(V.scalar_tensor_tensor(TI[:, :, :], TI[:, :, :], 1.0, XC[:, :, :], ADD, MUL))
            dve.wait_ge(s_ta, 4)
            V.tensor_scalar(TA[:, :, :], TA[:, :, :], 1e-18, None, ALU.max).then_inc(s_tiny, 1)
            dve.wait_ge(s_lru, 1)
            V.scalar_tensor_tensor(TA[:, :, :], TA[:, :, :], LN2, sq[:, 4:8, :], ADD, SUB).then_inc(s_tiny, 1)
            dve.wait_ge(s_lru, 2)
            st.seq(V.memset(TA[:, :, 0:1], 1.0))
            st.seq(V.scalar_tensor_tensor(TI[:, :, :], TI[:, :, :], 0.5, TA[:, :, :], MUL, MUL))
            for k in range(LT):
                v = st.did(V.tensor_tensor_scan(TA[:, k, 0:NP], AA[:, k, 0:NP], TI[:, k, 0:NP], 0.0, MUL, ADD))
            v = st.did(V.tensor_tensor(TA[:, :, NP:T], AA[:, :, NP:T], h04, MUL))
            st.need(v)
            V.tensor_tensor(TA[:, :, NP:T], TA[:, :, NP:T], TI[:, :, NP:T], ADD).then_inc(s_lrud, 1)
            dve.wait_ge(s_lrud, 1)
            dve.wait_ge(s_rs, 2)
            for k in range(2):
                V.scalar_tensor_tensor(qlT[:, k, :], qlT[:, k, :], pr("q_lora_norm_g", k), sq[:, 0, :], MUL, MUL).then_inc(s_ql, 1)
            dve.wait_ge(s_rs, 3)
            V.scalar_tensor_tensor(kvT[:, :], kvT[:, :], pr("kv_lora_norm_g"), sq[:, 1, :], MUL, MUL).then_inc(s_kvn, 1)
            dve.wait_ge(s_rs, 4)
            R = (NOPE, QK)
            kr = krT[NOPE:QK, :]
            V.scalar_tensor_tensor(kr, kr, pr("gk", 0, 1, R), sq[NOPE:QK, 2, :], MUL, MUL).then_inc(s_kr, 1)
            dve.wait_ge(s_kr, 1)
            j = J_KR[1]
            full(dve, j)
            V.tensor_tensor(two(qrot[NOPE:QK, :]), halves(j, R), two(C("sin", T, R)), MUL).then_inc(psum_free[j % 4], 1)
            st.seq(V.tensor_tensor(kr, kr, C("cos", T, R), MUL))
            dve.wait_ge(psum_free[j % 4], free_value(j))
            V.tensor_tensor(kr, kr, qrot[NOPE:QK, :], ADD).then_inc(s_kr, 1)
            dve.wait_ge(s_g, 1)
            V.tensor_tensor(XC[:, :, :], TA[:, :, :], GG[:, :, :], MUL).then_inc(s_lrud, 1)
            mod_rows(2)
            mod_rows(3)
            mod_columns(2)
            dve.wait_ge(s_rs, 5)
            for k in range(LT):
                V.scalar_tensor_tensor(hT[:, k, :], XC[:, k, :], pr("lru_out_norm_g", k), rs[:, :], MUL, MUL).then_inc(s_mix, 1)
            mod_rows(4)
            mod_columns(3)
            for a in range(5):
                j = J_LOUT + a
                n = P if a < 4 else NS
                full(dve, j)
                V.tensor_copy(otok[0:n, a, :], flat(j)[0:n, 0:KV + ROPE]).then_inc(psum_free[j % 4], 1)
            for n, w in enumerate((9, 11)):
                j = J_LOUT + 5 + n
                full(dve, j)
                V.tensor_copy(lout[0:w, n, :], flat(j)[0:w, 0:LW]).then_inc(psum_free[j % 4], 1)

            mod_rows(5)
            mod_columns(4)
            mod_columns(5)
            for e in range(2):
                V.tensor_copy(hb[e]["k"][NOPE:QK, :], krT[NOPE:QK, 0:NP]).then_inc(s_krk, 1)
            N0 = (0, NOPE)

            def normed(e, pair):
                q, k = hb[e]["q"][0:QK, :], hb[e]["k"][0:NOPE, :]
                nth = 2 * pair + e + 1
                dve.wait_ge(s_qrs, nth)
                V.scalar_tensor_tensor(q, q, pr("gq", 0, 1, (0, QK)), sq[0:QK, 2 * e + 1, :], MUL, MUL).then_inc(s_qn, 1)
                dve.wait_ge(s_krs, nth)
                V.scalar_tensor_tensor(k, k, pr("gk", 0, 1, N0), sq[0:NOPE, 5 + 2 * e, 0:NP], MUL, MUL).then_inc(s_kn, 1)
                dve.wait_ge(s_qn, nth)
                V.tensor_scalar(hb[e]["gq"][0:NOPE, :], hb[e]["q"][0:NOPE, NP:T], pr("gk", 0, 1, N0), None, MUL).then_inc(s_gq, 1)

            def rotated(J, e, pair, lap):
                qr = hb[e]["q"][NOPE:QK, :]
                j = J.qrot[e]
                full(dve, j, lap)
                V.tensor_tensor(two(qrot[NOPE:QK, :]), halves(j, R), two(C("sin", T, R)), MUL).then_inc(psum_free[j % 4], 1)
                st.seq(V.tensor_tensor(qr, qr, C("cos", T, R), MUL))
                dve.wait_ge(psum_free[j % 4], free_value(j, lap))
                st.seq(V.tensor_tensor(qr, qr, qrot[NOPE:QK, :], ADD))
                V.tensor_copy(QRS[NOPE:QK, :, bass.ds(2 * pair + e, 1)], hb[e]["q"][NOPE:QK, NP:T].unsqueeze(2)).then_inc(s_qr, 1)

            def values(J, e, lap):
                j = J.vw[e]
                full(dve, j, lap)
                v = st.did(V.tensor_copy(hb[e]["v"], flat(j)[:, 0:4 * VD]))
                st.need(v)
                V.tensor_copy(hb[e]["wt"][0:NOPE, :], flat(j)[0:NOPE, 512:512 + P]).then_inc(psum_free[j % 4], 1)

            def through_keys(J, e, pair, lap):
                j = J.qa[e]
                full(dve, j, lap)
                V.tensor_copy(QA[:, :, bass.ds(2 * pair + e, 1)], flat(j)[:, 0:NS].unsqueeze(2)).then_inc(psum_free[j % 4], 1)

            def row_max(J, e, pair, lap):
                b = hb[e]
                for n in range(4):
                    j = J.s[e][n]
                    full(dve, j, lap)
                    d = flat(j)[:, P * n:P * n + P]
                    V.tensor_tensor(d, d, C("mask"), ADD).then_inc(s_msk, 1)
                    dve.wait_ge(s_msk, 8 * pair + 4 * e + n + 1)
                    st.seq(V.tensor_reduce(b["rl"][:, n:n + 1], flat(j)[:, 0:P * (n + 1)], AX.X, ALU.max))
                    V.tensor_scalar(b["nm"][:, n:n + 1], b["rl"][:, n:n + 1], -SCALE, None, MUL).then_inc(s_nm, 1)

            def norm_probs(J, e, lap):
                b = hb[e]
                for n in range(4):
                    dve.wait_ge(psum_free[J.s[e][n] % 4], free_value(J.s[e][n], lap))
                st.seq(V.reciprocal(b["rl"], b["l"]))
                for n in range(4):
                    p = b["p"][:, POFF[n]:POFF[n] + P * (n + 1)]
                    V.tensor_scalar(p, p, b["rl"][:, n:n + 1], None, MUL).then_inc(s_pn, 1)

            def turned_probs(J, e, lap):
                for n in range(4):
                    j = J.p[e][n]
                    full(dve, j, lap)
                    V.tensor_copy(hb[e]["pt"][:, 0:n + 1, P * n:P * n + P],
                                  flat(j)[:, 0:P * (n + 1)].rearrange("p (a n) -> p a n", n=P)).then_inc(psum_free[j % 4], 1)

            def mixed(J, e, pair, lap):
                j = J.pv[e]
                full(dve, j, lap)
                V.tensor_copy(hT[VD * e:VD * e + VD, bass.ds(LT + pair, 1), 0:NP], flat(j)[VD * e:VD * e + VD, 0:NP]).then_inc(psum_free[j % 4], 1)

            J = HEAD_FIRST
            for e in range(2):
                normed(e, 0)
            for e in range(2):
                rotated(J, e, 0, 0)
            for e in range(2):
                values(J, e, 0)
            for e in range(2):
                through_keys(J, e, 0, 0)
            with dve.Fori(0, HEAD_LAPS) as i:
                J, lap = HEAD_LAP, HEAD_LAP.count // 4 * i
                st.enter(i, 16)
                for e in range(2):
                    row_max(J, e, i, lap)
                for e in range(2):
                    norm_probs(J, e, lap)
                turned_probs(J, 0, lap)
                for e in range(2):
                    normed(e, i + 1)
                turned_probs(J, 1, lap)
                for e in range(2):
                    rotated(J, e, i + 1, lap)
                for e in range(2):
                    mixed(J, e, i, lap)
                for e in range(2):
                    values(J, e, lap)
                for e in range(2):
                    through_keys(J, e, i + 1, lap)
            st.leave(HEAD_LAPS)
            J = HEAD_LAST
            for e in range(2):
                row_max(J, e, HEAD_LAPS, 0)
            for e in range(2):
                norm_probs(J, e, 0)
            for e in range(2):
                turned_probs(J, e, 0)
            for e in range(2):
                mixed(J, e, HEAD_LAPS, 0)

            full(dve, J_SPREAD)
            dve.wait_ge(s_bdz, 2)
            src = flat(J_SPREAD)[:, 0:NS * HEADS].rearrange("p (b h) -> p b h", b=NS)
            for n in range(4):
                rows = slice(ROPE * n, ROPE * n + ROPE)
                ins = V.tensor_copy(QBD[rows, :, n, :], src[rows, :, :])
                st.did(ins) if n < 3 else ins.then_inc(psum_free[J_SPREAD % 4], 1)
            st.need(st.n)
            dve.wait_ge(psum_free[J_SPREAD % 4], free_value(J_SPREAD))
            dve.sem_inc(s_qbd, 1)

            def by_key(x):
                return x.rearrange("p (c h) -> p c h", h=HEADS)

            def scores_max(e, v):
                dve.wait_ge(s_drs, v)
                dve.wait_ge(s_snc, NG * v)
                V.tensor_tensor(snd[e], snd[e], ssd[e], MUL).then_inc(s_sm, 1)
                dve.wait_ge(s_sm, 3 * v - 2)
                V.tensor_tensor(snd[e], snd[e], srd[e], ADD).then_inc(s_sm, 1)
                dve.wait_ge(s_sm, 3 * v - 1)
                last = snd[e][:, HEADS * PAGES:HEADS * KTILES]
                V.tensor_scalar(last, last, C("tail", 1), None, ADD).then_inc(s_sm, 1)
                dve.wait_ge(s_sm, 3 * v)
                V.tensor_reduce(mx[e], snd[e].rearrange("p (c h) -> p h c", h=HEADS), AX.X, ALU.max).then_inc(s_mx, 1)

            def shift(e, v):
                dve.wait_ge(s_am, v)
                V.tensor_tensor(by_key(snd[e]), by_key(snd[e]), mx[e].unsqueeze(1).to_broadcast([P, KTILES, HEADS]), SUB).then_inc(s_sh, 1)

            def prob_sums(e, v):
                dve.wait_ge(s_dp, v)
                V.tensor_reduce(pd[e], snd[e].rearrange("p (c h) -> p h c", h=HEADS), AX.X, ADD).then_inc(s_pd, 1)

            def finish(j, lap, s, v):
                full(dve, j, lap)
                full(dve, j + 1, lap)
                V.reciprocal(rden[0:HEADS, 0:1], flat(j + 1)[0:HEADS, 0:1]).then_inc(psum_free[(j + 1) % 4], 1)
                dve.wait_ge(psum_free[(j + 1) % 4], free_value(j + 1, lap))
                row = OLR[:, s, :] if isinstance(s, int) else OLR[:, s, :].rearrange("p o d -> p (o d)")
                V.tensor_scalar(row, flat(j)[0:HEADS, 0:KV], rden[0:HEADS, 0:1], None, MUL).then_inc(psum_free[j % 4], 1)

            def queries(e, s):
                q = QA[:, s, :].rearrange("p (o a) h -> p (o a h)", o=1) if not isinstance(s, int) else QA[:, s, :]
                q = q.rearrange("p (g h) -> p g h", g=2)
                return q

            def split_queries(e, s, v):
                q = queries(e, s)
                V.tensor_copy(kwH[:, e, :, 4 * NOPE:KWW], q).then_inc(s_kwq, 1)
                dve.wait_ge(s_kwq, 2 * v - 1)
                V.tensor_tensor(kwL[:, e, :, 4 * NOPE:KWW], q, kwH[:, e, :, 4 * NOPE:KWW].bitcast(F32), SUB).then_inc(s_kwq, 1)

            def unit(base, lap, e, s_before, s_next, v):
                for g in range(NG):
                    for n in range(GT[g]):
                        c = 4 * g + n
                        j = unit_job(base, "k", c)
                        dve.wait_ge(s_sqd, KTILES * (v - 1) + c + 1)
                        if n == 0:
                            w = HEADS * GT[g]
                            V.tensor_copy(srd[e][:, HEADS * c:HEADS * c + w], flat(j)[:, KWW:KWW + w]).then_inc(s_snc, 1)
                        V.tensor_copy(snd[e][:, HEADS * c:HEADS * c + HEADS].rearrange("p (g h) -> p g h", g=2),
                                      ps[j % 4][:, :, 4 * NOPE:KWW]).then_inc(psum_free[j % 4], 1)
                        V.tensor_reduce(ssd[e][:, HEADS * c:HEADS * c + HEADS], sqd[c % 3].rearrange("p (m d) -> p m d", d=NOPE),
                                        AX.X, ADD).then_inc(s_sqr, 1)
                        if base != J_DEC and (g, n) == (1, 1):
                            scores_max(1 - e, v - 1)
                        if base != J_DEC and (g, n) == (2, 1):
                            shift(1 - e, v - 1)
                    if base != J_DEC:
                        if g == 3:
                            prob_sums(1 - e, v - 1)
                        if g == PV_AT:
                            finish(unit_job(base, "pv", 0), lap, s_before, v - 1)
                    if g == 6 and s_next is not None:
                        split_queries(1 - e, s_next, v + 1)
                dve.wait_ge(psum_free[j % 4], free_value(j, lap))

            dve.wait_ge(s_wkn, 16)
            wk2 = wkn[:, :].rearrange("p (g n) -> p g n", g=2)
            for e in range(2):
                V.tensor_copy(kwH[:, e, :, 0:4 * NOPE], wk2).then_inc(s_kw, 1)
            dve.wait_ge(s_kw, 2)
            for e in range(2):
                V.tensor_tensor(kwL[:, e, :, 0:4 * NOPE], wk2, kwH[:, e, :, 0:4 * NOPE].bitcast(F32), SUB).then_inc(s_kw, 1)
            split_queries(0, 0, 1)
            unit(J_DEC, 0, 0, None, 1, 1)
            with dve.Fori(0, 3) as i:
                unit(J_UNIT1, 2 * UNIT // 4 * i, 1, bass.ds(2 * i, 1), bass.ds(2 * i + 2, 1), 2 * i + 2)
                unit(J_UNIT1 + UNIT, 2 * UNIT // 4 * i, 0, bass.ds(2 * i + 1, 1), bass.ds(2 * i + 3, 1), 2 * i + 3)
            unit(J_LAST, 0, 1, 6, None, 8)
            scores_max(1, NS)
            shift(1, NS)
            prob_sums(1, NS)
            finish(J_PVLAST, 0, NS - 1, NS)
            full(dve, J_OL)
            V.tensor_copy(OL[:, :, :].rearrange("p b h -> p (b h)"), flat(J_OL)[:, 0:NS * HEADS]).then_inc(psum_free[J_OL % 4], 1)
            full(dve, J_VP)
            V.tensor_copy(hT[:, LT:KT, NP:T], flat(J_VP)[:, 0:LT * NS].rearrange("p (k n) -> p k n", n=NS)).then_inc(psum_free[J_VP % 4], 1)

            def mixed_low(k):
                dve.wait_ge(s_mhi, k + 1)
                V.tensor_tensor(mxL[:, k, :], hT[:, k, :], mxH[:, k, :].bitcast(F32), SUB).then_inc(s_mlo, 1)

            def out_low(m):
                dve.wait_ge(s_wohi, m + 1)
                V.tensor_tensor(woL[:, m % 2, :, :], woR[:, m % 3, :, :], woH[:, m % 2, :, :].bitcast(F32), SUB).then_inc(s_wolo, 1)

            for k in range(LT):
                mixed_low(k)
            out_low(0)
            dve.wait_ge(s_rs, 6)
            for k in range(LT):
                V.scalar_tensor_tensor(hT[:, LT + k, :], hT[:, LT + k, :], pr("mla_out_norm_g", k), rs[:, :], MUL, MUL).then_inc(s_mix, 1)
            for k in range(LT, KT):
                mixed_low(k)
            out_low(1)

            def residual(j, m, gate, done, nth):
                g = modT[:, gate + m, 0:1]
                full(dve, j)
                b0, b1 = ps[j % 4][:, 0, 0:H], ps[j % 4][:, 1, 0:NP - H]
                V.tensor_tensor(d8[:, m, :], ps[j % 4][:, 1, NP - H:H], modT[:, gate + m, 1:9], MUL).then_inc(s_d8, 1)
                v = st.did(V.scalar_tensor_tensor(xT[:, m, 0:H], b0, g, xT[:, m, 0:H], MUL, ADD))
                V.scalar_tensor_tensor(xT[:, m, H:NP], b1, g, xT[:, m, H:NP], MUL, ADD).then_inc(psum_free[j % 4], 1)
                dve.wait_ge(s_d8, nth)
                st.need(v)
                dve.wait_ge(psum_free[j % 4], free_value(j))
                V.tensor_tensor(xT[:, m, NP:T], xT[:, m, NP:T], d8[:, m, :], ADD).then_inc(done, 1)

            def up_low(c, g, nth):
                dve.wait_ge(s_whi, nth)
                V.tensor_tensor(wuL[:, KT * g:KT * g + KT, :], wup[:, c, KT * g:KT * g + KT, :],
                                wuH[:, KT * g:KT * g + KT, :].bitcast(F32), SUB).then_inc(s_wlo, 1)

            for m in range(KT):
                residual(J_WO + m, m, 2 * KT, s_x1, m + 1)
                if m + 2 < KT:
                    out_low(m + 2)
                if m == 4:
                    up_low(0, 0, 1)
                    up_low(0, 1, 2)
            st.seq(V.tensor_scalar(gmod[:, :, :], modT[:, 4 * KT:5 * KT, :], 1.0, None, ADD))
            st.seq(V.tensor_tensor(gmod[:, :, :], gmod[:, :, :], pr("norm2_g", 0, KT).unsqueeze(2).to_broadcast([P, KT, 9]), MUL))
            dve.wait_ge(s_rs, 7)
            dec = h2[:, :, NP:T]
            st.seq(V.tensor_tensor(dec, xT[:, :, NP:T], rs[:, NP:T].unsqueeze(1).to_broadcast([P, KT, NS]), MUL))
            st.seq(V.tensor_tensor(dec, dec, gmod[:, :, 1:9], MUL))
            st.seq(V.tensor_tensor(dec, dec, modT[:, 3 * KT:4 * KT, 1:9], ADD))
            for k in range(KT):
                V.tensor_tensor(h2[:, k, 0:NP], xT[:, k, 0:NP], rs[:, 0:NP], MUL).then_inc(s_hp, 1)
            for k in range(KT):
                dve.wait_ge(s_hhi, k + 1)
                V.tensor_tensor(hL[:, k, :], h2[:, k, :], hH[:, k, :].bitcast(F32), SUB).then_inc(s_hlo, 1)
            full(dve, J_FST)
            V.tensor_copy(FS[:, :, :].rearrange("p m n -> p (m n)"), flat(J_FST)[:, 0:4 * FT * NS]).then_inc(psum_free[J_FST % 4], 1)
            dve.wait_ge(psum_free[J_FST % 4], free_value(J_FST))
            for e in range(2):
                V.memset(UU[e][:, :, 0:2], 0.0).then_inc(s_pads, 1)
            dve.sem_inc(s_cvfree, 2)

            def down_low(m):
                for n, a in enumerate((0, FT // 2)):
                    dve.wait_ge(s_whi, 2 * FT + 2 * m + n + 1)
                    V.tensor_tensor(wdL[m % 2][:, a:a + FT // 2, :], wdn[:, m % 2, a:a + FT // 2, :],
                                    wdH[m % 2][:, a:a + FT // 2, :].bitcast(F32), SUB).then_inc(s_wlo, 1)

            def mlp(i, e, left):
                m = 2 * i + e
                if left >= 1:
                    up_low(1 - e, 1, 2 * m + 4)
                else:
                    down_low(0)
                for g in range(2):
                    j = J_UP + 2 * e + g
                    dve.wait_ge(psum_free[j % 4], free_value(j, i))
                    u, cv = UU[e][:, g, :], CV[g]
                    w = [fpar[:, bass.ds(2 * FT * n + FT * g + m, 1)] for n in range(4)]
                    fs = FS[:, bass.ds(FT * g + m, 1), :].rearrange("p o (b r) -> p (o b) r", r=2)
                    st.did(V.tensor_scalar(cv[:, 0:NP], u[:, 0:NP], w[0], w[3], MUL, ADD))
                    st.seq(V.tensor_scalar(cv[:, NP:T], fs[:, :, 0], w[0], w[3], MUL, ADD))
                    st.did(V.scalar_tensor_tensor(cv[:, 0:NP], u[:, 1:1 + NP], w[1], cv[:, 0:NP], MUL, ADD))
                    st.seq(V.scalar_tensor_tensor(cv[:, NP:T], fs[:, :, 1], w[1], cv[:, NP:T], MUL, ADD))
                    st.seq(V.scalar_tensor_tensor(cv[:, :], u[:, 2:2 + T], w[2], cv[:, :], MUL, ADD))
                V.memset(small[:, 50:51], 0.0).then_inc(s_cv, 1)
                if left >= 2:
                    up_low(e, 0, 2 * m + 5)
                dve.wait_ge(s_ge, m + 1)
                st.seq(V.tensor_tensor(CV[0], CV[0], GE, MUL))
                hi, lo = [x[:, bass.ds(m, 1), :].rearrange("p o n -> p (o n)") for x in (actH, actL)]
                st.seq(V.tensor_copy(hi, CV[0]))
                V.tensor_tensor(lo, CV[0], hi.bitcast(F32), SUB).then_inc(s_hid, 1)
                dve.wait_ge(s_hid, m + 1)
                dve.wait_ge(s_ut, 2 * m + 2)
                dve.sem_inc(s_cvfree, 1)

            up_low(1, 0, 3)
            with dve.Fori(0, FT // 2 - 1) as i:
                st.enter(i, 24)
                mlp(i, 0, 2)
                mlp(i, 1, 2)
            st.leave(FT // 2 - 1)
            mlp(FT // 2 - 1, 0, 1)
            mlp(FT // 2 - 1, 1, 0)

            down_low(1)
            for m in range(KT):
                residual(J_DOWN + m, m, 5 * KT, s_x2, KT + m + 1)
                if m + 2 < KT:
                    down_low(m + 2)
            for n in (1, 3):
                j = J_Y + n
                full(dve, j)
                V.tensor_copy(y_tok[n], flat(j)[:, :]).then_inc(psum_free[j % 4], 1)
            for n in range(6):
                j = J_FT + n
                w = P * (min(8 * n + 8, 2 * FT) - 8 * n)
                full(dve, j)
                V.tensor_copy(ft_tok[:, D * n:D * n + w], flat(j)[0:10, 0:w]).then_inc(psum_free[j % 4], 1)


_INS = ["x_prompt", "x_sample", "cache_kv_latent", "cache_k_rope", "state_lru_h", "state_lru_conv", "state_ffn_conv",
        "page_table", "c_prompt", "c_sample", "w_ada", "b_ada", "norm1_g", "w_in", "lru_conv_w", "lru_conv_b", "lru_w_a",
        "lru_b_a", "lru_w_x", "lru_b_x", "lru_lambda", "q_lora_norm_g", "w_uq", "q_nope_norm_g", "q_rope_norm_g",
        "kv_lora_norm_g", "k_rope_norm_g", "w_ukv", "k_nope_norm_g", "lru_out_norm_g", "mla_out_norm_g", "w_o", "norm2_g",
        "w_up", "ffn_conv_w", "ffn_conv_b", "w_down"]
_OUTS = [("o_y_p", (1, NP, D)), ("o_y_s", (NS, 1, D)), ("o_kv_p", (1, 1, NP, KV)), ("o_kr_p", (1, 1, NP, ROPE)),
         ("o_lru_h_p", (1, 1, LW)), ("o_lru_conv_p", (1, 1, 3, LW)), ("o_ffn_conv_p", (1, 1, 2, 2 * FF)),
         ("o_kv_s", (1, NS, 1, KV)), ("o_kr_s", (1, NS, 1, ROPE)), ("o_lru_h_s", (1, NS, LW)),
         ("o_lru_conv_s", (1, NS, 3, LW)), ("o_ffn_conv_s", (1, NS, 2, 2 * FF))]


def kernel(**inputs):
    import numpy as np
    import concourse.bacc as bacc
    from concourse.bass_utils import run_bass_kernel_spmd as run

    nc = bacc.Bacc("TRN2", target_bir_lowering=False, num_devices=1)
    arrays, t = {}, {}
    for name in _INS:
        arrays[name] = np.ascontiguousarray(inputs[name])
    arrays["consts"] = constants()
    for name, a in arrays.items():
        t[name] = nc.dram_tensor(name, a.shape, mybir.dt.from_np(a.dtype), kind="ExternalInput").ap()
    for name, shape in _OUTS:
        t[name] = nc.dram_tensor(name, shape, F32, kind="ExternalOutput").ap()
    build(nc, t)
    r = run(nc, [arrays], core_ids=[0])
    return tuple(r.results[0][name] for name, _ in _OUTS)
```

```python
import math
from contextlib import ExitStack

import concourse.bass as bass
from concourse import mybir

F32 = mybir.dt.float32
FR = mybir.dt.float32r
I32 = mybir.dt.int32
ALU = mybir.AluOpType
ACT = mybir.ActivationFunctionType
AX = mybir.AxisListType
RMAX = bass.bass_isa.ReduceOp.max

P = 128
D = 1024
KT = D // P
NP, NS = 512, 8
T = NP + NS
H = T // 2
LT = 4
LW = LT * P
HEADS = 8
NOPE, ROPE, VD = 64, 32, 64
QK = NOPE + ROPE
KV = 128
QL = 256
IN = 2 * LW + QL + KV + ROPE
FF = 2816
FT = FF // P
PAGE = 128
PAGES = 32
POOL = 320
KTILES = PAGES + 1
EPS = 1e-6
SCALE = float(QK) ** -0.5
NEG = -1e30
LN2 = 0.6931471805599453

ROWS = {}
_r = 0
for _name, _n in (("b_ada", 48), ("norm1_g", 8), ("lru_conv_w", 16), ("lru_conv_b", 4), ("lru_b_a", 4), ("lru_b_x", 4),
                  ("lru_lambda", 4), ("q_lora_norm_g", 2), ("kv_lora_norm_g", 1), ("lru_out_norm_g", 4),
                  ("mla_out_norm_g", 4), ("norm2_g", 8), ("gq", 1), ("gk", 1)):
    ROWS[_name] = _r
    _r += _n
NROWS = _r

CC = {}
_c = 0
for _name, _n in (("ident", P), ("ones", P), ("blk", P), ("perm", QK), ("mask", P), ("spread", P), ("cos", T),
                  ("sin", T), ("tail", 1), ("quarter", 1)):
    CC[_name] = _c
    _c += _n
NCONST = _c


def constants():
    import numpy as np
    c = np.zeros((P, NCONST), np.float32)
    c[:, CC["ident"]:CC["ident"] + P] = np.eye(P)
    c[:, CC["ones"]:CC["ones"] + P] = 1.0
    blk = np.zeros((QK, QK), np.float32)
    blk[:NOPE, :NOPE] = 1.0 / NOPE
    blk[NOPE:, NOPE:] = 1.0 / ROPE
    c[:QK, CC["blk"]:CC["blk"] + QK] = blk
    half = ROPE // 2
    for m in range(half):
        c[NOPE + half + m, CC["perm"] + NOPE + m] = -1.0
        c[NOPE + m, CC["perm"] + NOPE + half + m] = 1.0
    q = np.arange(P)
    c[:, CC["mask"]:CC["mask"] + P] = np.where(q[None, :] <= q[:, None], 0.0, NEG)
    for j in range(4):
        for d in range(ROPE):
            c[NOPE + d, CC["spread"] + ROPE * j + d] = 1.0
    inv = (np.float32(10000.0) ** (-np.arange(0, ROPE, 2, dtype=np.float32) / np.float32(ROPE))).astype(np.float32)
    pos = np.concatenate([np.arange(NP), np.full(NS, PAGES * PAGE)]).astype(np.float32)
    ang = (pos[None, :] * inv[:, None]).astype(np.float32)
    c[NOPE:NOPE + half, CC["cos"]:CC["cos"] + T] = np.cos(ang)
    c[NOPE + half:QK, CC["cos"]:CC["cos"] + T] = np.cos(ang)
    c[NOPE:NOPE + half, CC["sin"]:CC["sin"] + T] = np.sin(ang)
    c[NOPE + half:QK, CC["sin"]:CC["sin"] + T] = np.sin(ang)
    c[1:, CC["tail"]] = NEG
    c[:, CC["quarter"]] = q % 4
    return c


class Steps:

    def __init__(self, eng, sem):
        self.eng, self.sem, self.n, self.base = eng, sem, 0, 0

    def did(self, ins):
        ins.then_inc(self.sem, 1)
        self.n += 1
        return self.base + self.n

    def need(self, v):
        self.eng.wait_ge(self.sem, v)

    def seq(self, ins):
        self.need(self.did(ins))

    def enter(self, i, per):
        self.start, self.base, self.n, self.per = self.n, self.n + i * per, 0, per

    def leave(self, laps):
        assert self.n == self.per, (self.n, self.per)
        self.n, self.base = self.start + laps * self.per, 0


J_XT = 0
J_C = J_XT + KT
J_ROW = [J_C + 1]
J_PAR = J_ROW[0] + 1
J_FPAR = J_PAR + 1
J_STATE = J_FPAR + 1
J_N1 = J_STATE + 1
J_ROW.append(J_N1 + 1)
J_COL = [J_ROW[1] + 1, J_ROW[1] + 2]
J_IN = J_COL[1] + 1
WIN_ORDER = [0, 1, 2, 3, 8, 9, 10, 11, 4, 5, 6, 7]
N_KR = WIN_ORDER.index(11)
J_GATE = J_IN + 8
J_WIN = {m: J_IN + n + (8 if n >= 8 else 0) + (3 if n >= 10 else 0) for n, m in enumerate(WIN_ORDER)}
J_NQ = J_WIN[5] + 1
J_NKV = J_NQ + 1
J_KR = [J_NKV + 1, J_WIN[7] + 1]
J_ROW.append(J_KR[1] + 1)
J_ROW.append(J_ROW[2] + 1)
J_COL.append(J_ROW[3] + 1)
J_NLRU = J_COL[2] + 1
J_ROW.append(J_NLRU + 1)
J_COL.append(J_ROW[4] + 1)
J_LOUT = J_COL[3] + 1
J_ROW.append(J_LOUT + 7)
J_COL.append(J_ROW[5] + 1)
J_COL.append(J_COL[4] + 1)
J_HEAD = J_COL[5] + 1


RB_SIZE = 13200

POFF = [0, P, 3 * P, 6 * P]


class HeadJobs:

    def __init__(self, first, order):
        self.count = len(order)
        self.q, self.qms, self.qrot, self.kn, self.kms, self.vw, self.qa, self.pv = ({} for _ in range(8))
        self.s, self.p = [{}, {}], [{}, {}]
        whole = dict(q=self.q, qms=self.qms, qrot=self.qrot, kn=self.kn, kms=self.kms, vw=self.vw, qa=self.qa, pv=self.pv)
        blocks = dict(s=self.s, p=self.p)
        for n, (kind, e, *block) in enumerate(order):
            if block:
                blocks[kind][e][block[0]] = first + n
            else:
                whole[kind][e] = first + n


def _each(*kinds):
    return [(kind, e) for e in range(2) for kind in kinds]


_S = [("s", e, n) for e in range(2) for n in range(4)]
_P0, _P1 = [[("p", e, n) for n in range(4)] for e in range(2)]
HEAD_FIRST = HeadJobs(J_HEAD, _each("q", "kn") + _each("qms", "kms") + _each("qrot") + _each("qa") + _each("vw"))
HEAD_LAP = HeadJobs(J_HEAD + HEAD_FIRST.count, _S + _each("q", "kn") + _P0 + _each("qms", "kms") + _P1 + _each("qrot")
                    + _each("qa") + _each("pv") + _each("vw"))
HEAD_LAPS = HEADS // 2 - 1
assert HEAD_LAP.count % 4 == 0
HEAD_LAST = HeadJobs(J_HEAD + HEAD_FIRST.count + HEAD_LAPS * HEAD_LAP.count, _S + _P0 + _P1 + _each("pv"))
J_SPREAD = J_HEAD + HEAD_FIRST.count + HEAD_LAPS * HEAD_LAP.count + HEAD_LAST.count
J_FIRST_T = J_SPREAD + 1
J_DEC = J_FIRST_T + 2
NG = 9
GT = [4] * (NG - 1) + [1]
UNIT = NG + KTILES + 2
PV_AT = 4


def unit_jobs():
    order = []
    for g in range(NG):
        order.append(("t", g + 2) if g + 2 < NG else ("tn", g + 2 - NG))
        order += [("k", 4 * g + n) for n in range(GT[g])]
        if g == PV_AT:
            order += [("pv", 0), ("den", 0)]
    assert len(order) == UNIT
    return {x: n for n, x in enumerate(order)}


UJ = unit_jobs()
J_UNIT1 = J_DEC + UNIT - 2
J_LAST = J_UNIT1 + UNIT * (NS - 2)


def unit_job(base, kind, n):
    if kind == "t" and n < 2:
        return J_FIRST_T + n if base == J_DEC else base - UNIT + UJ["tn", n]
    u = UJ[kind, n]
    if base == J_DEC and u > UJ["pv", 0]:
        return base + u - 2
    if base == J_LAST:
        return base + u - (u > UJ["tn", 0]) - (u > UJ["tn", 1])
    return base + u


J_PVLAST = J_LAST + UNIT - 2
J_OL = J_PVLAST + 2
J_WO = [J_OL + 1]
J_VP = J_WO[0] + 1
J_NMLA = J_VP + 1
J_WO += [J_NMLA + m for m in range(1, KT)]
J_N2 = J_WO[KT - 1] + 1
J_FST = J_N2 + 1
J_UP = J_FST + 1
J_DOWN = [J_UP + 2 * FT + 4 * (m // 2) + m % 2 for m in range(KT)]
J_FT = [J_UP + 2 * FT + 4 * (n // 2) + 2 + n % 2 for n in range(6)]
J_Y = J_DOWN[KT - 1] + 1


def build(nc, t):
    with ExitStack() as ctx:
        def sb(name, shape, dt=F32):
            return ctx.enter_context(nc.sbuf_tensor(name, shape, dt))

        def parts_at(name, shape, at):
            size = 4 * math.prod(shape[1:])
            return [nc.alloc_sbuf_tensor_at(f"{name}_{part}", shape, FR, offset=at + n * size) for n, part in enumerate(("high", "low"))]

        def sem(name):
            return ctx.enter_context(nc.semaphore(name))

        cst = sb("cst", [P, NCONST])
        par_rows = sb("par_rows", [P, 3, P])
        par = sb("par", [P, NROWS])
        fpar = sb("fpar", [P, 4 * 2 * FT])
        xT = sb("xT", [P, KT, T])
        h_at = -(-nc.sbuf_base // 32) * 32
        hT = sb("hT", [P, KT, T])
        sq = sb("sq", [P, KT, T])
        rs = sb("rs", [P, T])
        modT = sb("modT", [P, 48, 9])
        gmod = sb("gmod", [P, KT, 9])
        cT = sb("cT", [P, KT, 9])
        small = sb("small", [P, 64])
        d8 = sb("d8", [P, KT, NS])
        page_of = sb("page_of", [P, NS], I32)
        row_of = sb("row_of", [P, NS], I32)
        half_of = sb("half_of", [P, 2, NS], I32)
        UT = sb("UT", [P, 2 * FT, 10])
        FS = sb("FS", [P, 2 * FT, 2 * NS])
        rw_at = -(-nc.sbuf_base // 32) * 32
        RW = sb("RW", [P, 12288])
        rb_at = -(-nc.sbuf_base // 32) * 32
        RB = sb("RB", [P, RB_SIZE])
        ring = RW[:, 0:8192].rearrange("p (c k n) -> p c k n", c=4, k=KT)
        RA = RW[:, 8256:11328].rearrange("p (c k n) -> p c k n", c=3, k=KT)

        def C(name, w=P, rows=(0, P)):
            return cst[rows[0]:rows[1], CC[name]:CC[name] + w]

        ident, ones = C("ident"), C("ones")

        def pr(name, k=0, n=1, rows=(0, P)):
            return par[rows[0]:rows[1], ROWS[name] + k:ROWS[name] + k + n]

        x_tok = RB[:, 0:4 * D].rearrange("p (a d) -> p a d", a=4)
        xs_tok = RB[0:NS, 4 * D:5 * D]
        c_tok = RB[0:9, 5 * D:6 * D]
        c_th = RB[0:9, 6 * D:7 * D]
        st_tok = RB[0:24, 7 * D:7 * D + LW]
        h0_tok = RB[0:NS, 7 * D + LW:8 * D]
        o = 0

        def take(n):
            nonlocal o
            o += n
            assert o <= RB_SIZE, o
            return RB[:, o - n:o]

        XX = take(LT * (3 + T)).rearrange("p (t n) -> p t n", t=LT)
        GG = take(LT * T).rearrange("p (t n) -> p t n", t=LT)
        XC = take(LT * T).rearrange("p (t n) -> p t n", t=LT)
        TA = take(LT * T).rearrange("p (t n) -> p t n", t=LT)
        TI = take(LT * T).rearrange("p (t n) -> p t n", t=LT)
        AA = take(LT * T).rearrange("p (t n) -> p t n", t=LT)
        stT = sb("stT", [P, LT * 24])
        h0T = sb("h0T", [P, LT * NS])
        st4 = stT[:, :].rearrange("p (t b r) -> p t b r", t=LT, b=NS)
        h04 = h0T[:, :].rearrange("p (t b) -> p t b", t=LT)
        bd_at = -(-nc.sbuf_base // 32) * 32
        BD = sb("BD", [P, 2, LT, P])
        qlT = sb("qlT", [P, 2, T])
        kvT = sb("kvT", [P, T])
        krT = sb("krT", [P, T])
        qrot = sb("qrot", [P, T])
        behind_at = -(-nc.sbuf_base // 32) * 32
        otok = sb("otok", [P, 5, 160])
        lout = sb("lout", [16, 2, LW])

        o = 0
        hb = []
        for e in range(2):
            hb.append(dict(q=take(T), k=take(NP), p=take(10 * P),
                           pt=take(4 * NP).rearrange("p (a n) -> p a n", a=4),
                           v=take(4 * VD), wt=take(P),
                           nm=take(4), l=take(4), rl=take(4), gq=take(NS)))
        wuq = sb("wuq", [P, 2, 2, QK])
        wukv = sb("wukv", [P, 2, P])
        QA = sb("QA", [P, NS, HEADS])
        QRS = sb("QRS", [P, NS, HEADS])
        OLR = sb("OLR", [HEADS, NS, KV])
        QBD = sb("QBD", [P, NS, 4, HEADS])
        OL = sb("OL", [P, NS, HEADS])
        rden = sb("rden", [HEADS, 1])[:, :]
        wkn = sb("wkn", [P, HEADS * NOPE])
        newrow = sb("newrow", [1, NS, KV + ROPE])
        o = 0
        sqd = [take(512), qrot[:, 0:512], krT[:, 0:512]]
        ssd = [take(KTILES * HEADS) for _ in range(2)]
        snd = [take(KTILES * HEADS) for _ in range(2)]
        srd = [take(KTILES * HEADS) for _ in range(2)]
        mx = [take(HEADS) for _ in range(2)]
        pd = [take(HEADS) for _ in range(2)]
        wv = take(HEADS * VD).rearrange("p (h d) -> p h d", h=HEADS)
        KWW = 4 * NOPE + 4
        turned = take(3 * 5 * P).rearrange("p (g n) -> p g n", g=3)
        latH, latL = parts_at("latents", [P, 3, 4 * P], rb_at + 4 * o)
        o += 2 * 3 * 4 * P
        kwH, kwL = parts_at("key_weights", [P, 2, 2, KWW], rb_at + 4 * o)
        o += 2 * 2 * 2 * KWW
        recH = nc.alloc_sbuf_tensor_at("recurrent_high", [P, LT, T], FR, offset=bd_at)
        recL = nc.alloc_sbuf_tensor_at("recurrent_low", [P, LT, T], FR, offset=behind_at)
        assert 2 * LT * P + 3 * T >= LT * T and 5 * 160 + 2 * LW + 4 * QK + 2 * P >= LT * T
        mxH, mxL = parts_at("mixed", [P, LT, T], rb_at)
        mixed_high = [recH[:, k, :] for k in range(LT)] + [mxH[:, k, :] for k in range(LT)]
        mixed_low = [recL[:, k, :] for k in range(LT)] + [mxL[:, k, :] for k in range(LT)]
        woH, woL = parts_at("output_weights", [P, 2, KT, P], rw_at + 4 * 8192)
        woR = RB[:, RB_SIZE - 3072:RB_SIZE].rearrange("p (c k n) -> p c k n", c=3, k=KT)
        assert o <= RB_SIZE - 3072
        n_lat = KTILES * P
        n_kr = 36 * ROPE
        lat = [RW[:, e * n_lat:(e + 1) * n_lat].rearrange("p (c d) -> p c d", c=KTILES) for e in (1, 0)]
        kr_ = [RW[:, 2 * n_lat + e * n_kr:2 * n_lat + (e + 1) * n_kr].rearrange("p (c d) -> p c d", c=36) for e in range(2)]
        sb("hidden_tail", [P, (rb_at + 4 * 2 * FT * T - nc.sbuf_base) // 4])
        hH, hL = parts_at("normed", [P, KT, T], h_at)
        actH, actL = parts_at("hidden", [P, FT, T], rb_at)
        h2 = RB[:, 2 * FF:2 * FF + KT * T].rearrange("p (k n) -> p k n", k=KT)
        h1 = RB[:, 2092 + 2 * LT * T:2092 + 4 * LT * T].rearrange("p (k n) -> p k n", k=KT)
        h1L = nc.alloc_sbuf_tensor_at("input_low", [P, KT, T], FR, offset=rw_at + 4 * 4096)
        wiH, wiL = parts_at("input_weights", [P, 2, KT, P], behind_at)
        assert nc.sbuf_base >= behind_at + 4 * 4 * KT * P
        wup = RW[:, 0:4096].rearrange("p (c k n) -> p c k n", c=2, k=2 * KT)
        wuH, wuL = parts_at("up_weights", [P, 2 * KT, P], rw_at + 4 * 4096)
        wdn = RW[:, 0:2 * FT * P].rearrange("p (c k n) -> p c k n", c=2, k=FT)
        wdH, wdL = zip(parts_at("down_weights0", [P, FT, P], h_at), parts_at("down_weights1", [P, FT, P], rw_at + 4 * 2 * FT * P))
        PIECES = ((0, 3), (3, FT // 2), (FT // 2, FT))
        UW = 2 + T
        UU = [RW[:, 8192 + 2 * UW * e:8192 + 2 * UW * (e + 1)].rearrange("p (g n) -> p g n", g=2) for e in range(2)]
        CV = [RW[:, 8192 + 4 * UW + T * g:8192 + 4 * UW + T * (g + 1)] for g in range(2)]
        GE = RW[:, 8192 + 4 * UW + 2 * T:8192 + 4 * UW + 3 * T]
        fs_tok = RB[0:2 * NS, 0:2 * FF]
        y_tok = [RB[:, D * n:D * n + D] for n in range(5)]
        ft_tok = sq[0:10, :, :].rearrange("p k n -> p (k n)")[:, 1536:1536 + 2 * D]
        assert 2 * FT * P <= KT * T + 1536

        def ft_width(n):
            return min(D, 2 * FF - D * n)

        ps = [ctx.enter_context(nc.psum_tensor(f"ps{i}", [P, 2, 512], F32)) for i in range(4)]
        psum_full = [sem(f"psum_full{i}") for i in range(4)]
        psum_free = [sem(f"psum_free{i}") for i in range(4)]

        def halves(j, rows=(0, P)):
            return ps[j % 4][rows[0]:rows[1], :, 0:H]

        def flat(j):
            return ps[j % 4][:, :, :].rearrange("p a b -> p (a b)")

        def two(ap):
            return ap.rearrange("p (a n) -> p a n", a=2)

        s_ident = sem("identity_in")
        s_cst = sem("other_consts_in")
        s_par = sem("params_in")
        s_x = sem("x_in")
        s_c = sem("conditions_in")
        s_nsum = sem("squares_added")
        s_ada = [sem(f"w_ada_in{i}") for i in range(4)]
        s_ada2 = [sem(f"w_ada_second_in{i}") for i in range(4)]
        s_hp = sem("h_scaled")
        s_gain = sem("norm1_gains_known")
        s_hq = sem("h_scaled_by_gpsimd")
        s_tiny = sem("mult_argument_done")
        s_win = [sem(f"w_in_in{i}") for i in range(3)]
        s_bd = sem("gate_weights_in")
        s_bdz = sem("gate_weights_cleared")
        s_parz = sem("param_rows_cleared")
        s_out = sem("outputs_stored")
        s_kept = sem("last_rows_stored")
        s_silu = sem("silu_c_done")
        s_sq = sem("squares_done")
        s_rs = sem("rstd_done")
        s_h = sem("normed_done")
        s_dve = sem("dve_steps")
        s_act2 = sem("key_ln_done")
        s_cvfree = sem("up_buffers_free")
        s_act = sem("act_steps")
        s_xc = sem("x_conv_done")
        s_ta = sem("tanh_a_done")
        s_lru = sem("lru_act_done")
        s_lrud = sem("lru_dve_done")
        s_sp = sem("softplus_done")
        s_g = sem("gelu_done")
        s_kr = sem("k_rope_done")
        s_ql = sem("q_latent_normed")
        s_kvn = sem("kv_latent_normed")
        s_mix = sem("mixed_done")
        s_hw = [sem(f"head_weights_in{e}") for e in range(2)]
        s_wo = [sem(f"w_o_in{e}") for e in range(3)]
        s_qsq = sem("q_squares_done")
        s_qrs = sem("q_rstd_done")
        s_qn = sem("q_normed")
        s_qr = sem("q_rotated")
        s_ksq = sem("k_squares_done")
        s_krs = sem("k_rstd_done")
        s_kn = sem("k_head_done")
        s_gq = sem("q_times_k_gain_done")
        s_wt = sem("key_projection_turned")
        s_nm = sem("row_max_done")
        s_pn = sem("probs_normed")
        s_pt = sem("page_table_in")
        s_row = sem("cache_rows_known")
        s_ada_used = sem("w_ada_chunks_used")
        s_lat = [[sem(f"cached_latents{n}_in{e}") for e in range(2)] for n in range(2)]
        s_krc = [sem(f"cached_keys_in{e}") for e in range(2)]
        s_new = sem("new_token_rows_in")
        s_newc = sem("new_token_tile_done")
        s_clr = sem("new_token_tiles_cleared")
        s_tT = sem("latents_transposed_copied")
        s_lo = sem("latents_low_done")
        s_kw = sem("key_weights_split")
        s_kwq = sem("queries_split")
        s_sqd = sem("key_squares_done")
        s_sqr = sem("key_squares_summed")
        s_drs = sem("key_rstd_done")
        s_mx = sem("partition_max_done")
        s_am = sem("all_max_done")
        s_sh = sem("scores_shifted")
        s_dp = sem("decode_probs_done")
        s_pd = sem("decode_prob_sums_done")
        s_wkn = sem("key_weights_in")
        s_krk = sem("rope_key_rows_set")
        s_msk = sem("scores_masked")
        s_snc = sem("decode_scores_copied")
        s_sm = sem("decode_score_steps")
        s_d8 = sem("decode_residual_scaled")
        s_pads = sem("conv_pads_cleared")
        s_ut = sem("last_rows_kept")
        s_wv = sem("value_weights_in")
        s_qbd = sem("decode_rope_queries_done")
        s_x1 = sem("x1_done")
        s_wup = [sem(f"w_up_in{e}") for e in range(2)]
        s_whi = sem("mlp_weights_high")
        s_wlo = sem("mlp_weights_low")
        s_mhi = sem("mixed_high")
        s_mlo = sem("mixed_low")
        s_wohi = sem("output_weights_high")
        s_wolo = sem("output_weights_low")
        s_wihi = sem("input_weights_high")
        s_wilo = sem("input_weights_low")
        s_hhi = sem("normed_high")
        s_hlo = sem("normed_low")
        s_wdn = [sem(f"w_down_in{e}") for e in range(2)]
        s_fst = sem("ffn_state_in")
        s_cv = sem("conv_done")
        s_ge = sem("gelu_gate_done")
        s_hid = sem("hidden_done")
        s_x2 = sem("x2_done")

        def full(eng, j, lap=0):
            eng.wait_ge(psum_full[j % 4], j // 4 + 1 + lap)

        def claim(eng, j, lap=0):
            if j // 4 >= 1 or not isinstance(lap, int):
                eng.wait_ge(psum_free[j % 4], j // 4 + lap)

        def free_value(j, lap=0):
            return j // 4 + 1 + lap

        def split_tiles(n):
            return n + 1 - (n >= N_KR)

        def chunk_used(eng, c):
            if c % 4 == 3:
                full(eng, J_ROW[c // 4])
            else:
                eng.wait_ge(s_ada_used, 3 * (c // 4) + c % 4 + 1)

        hflat = hT[:, :, :].rearrange("p k n -> p (k n)")

        def rows9(n):
            return hflat[0:9, 2080 + D * (n % 2):2080 + D * (n % 2) + D]

        block = ctx.enter_context(nc.Block())

        @block.sync
        def _(sp):
            x3 = t["x_prompt"].rearrange("b (a p) d -> p (b a) d", p=P)
            sp.dma_start(x_tok, x3).then_inc(s_x, 16)
            sp.dma_start(cst[:, 0:P], t["consts"][:, 0:P]).then_inc(s_ident, 16)
            sp.dma_start(xs_tok, t["x_sample"].rearrange("b s d -> (b s) d")).then_inc(s_x, 16)
            sp.dma_start(c_tok[0:1, :], t["c_prompt"]).then_inc(s_c, 16)
            sp.dma_start(c_tok[1:9, :], t["c_sample"]).then_inc(s_c, 16)

            wa = t["w_ada"].rearrange("l (k p) (c n) -> p (l k) c n", p=P, n=256)
            for c in range(4):
                sp.dma_start(ring[:, c, :, :], wa[:, :, c, :]).then_inc(s_ada[c], 16)
                if c == 1:
                    sp.dma_start(cst[:, P:NCONST], t["consts"][:, P:NCONST]).then_inc(s_cst, 16)
            for c in range(4):
                chunk_used(sp, c)
                sp.dma_start(ring[:, c, :, :], wa[:, :, 4 + c, :]).then_inc(s_ada[c], 16)
            wi = t["w_in"].rearrange("l (k p) n -> p (l k) n", p=P)

            def w_in(n):
                m = WIN_ORDER[n]
                w = P if m < 11 else ROPE
                if n == N_KR + 3:
                    full(sp, J_WIN[WIN_ORDER[N_KR]])
                elif n >= 3:
                    sp.wait_ge(s_wilo, split_tiles(n - 3))
                sp.dma_start(RA[:, n % 3, :, 0:w], wi[:, :, P * m:P * m + w]).then_inc(s_win[n % 3], 16)

            for n in range(3):
                w_in(n)
            sp.wait_ge(s_bdz, 1)
            for g, name in enumerate(("lru_w_a", "lru_w_x")):
                w = t[name].rearrange("l (t e) i j -> (l e) i t j", e=2)
                for e in range(2):
                    sp.dma_start(BD[64 * e:64 * e + 64, g, :, 64 * e:64 * e + 64], w[e]).then_inc(s_bd, 16)
            for n in range(3, 12):
                w_in(n)
            full(sp, J_WIN[7])
            wq = t["w_uq"].rearrange("l (k p) (h n) -> p (l k) h n", p=P, h=HEADS)
            wk = t["w_ukv"].rearrange("l p (h n) -> p (l h) n", h=HEADS)

            def head_weights(e, h):
                sp.dma_start(wuq[:, e, :, :], wq[:, :, h, :]).then_inc(s_hw[e], 16)
                sp.dma_start(wukv[:, e, :], wk[:, h, :]).then_inc(s_hw[e], 16)

            sp.dma_start(wkn[:, :].rearrange("p (h n) -> p h n", h=HEADS),
                         t["w_ukv"][0].rearrange("p (h n) -> p h n", h=HEADS)[:, :, 0:NOPE]).then_inc(s_wkn, 16)
            for e in range(2):
                head_weights(e, bass.ds(e, 1))
            sp.dma_start(t["o_lru_conv_s"][0, :, 0:2, :], t["state_lru_conv"][0, :, 1:3, :]).then_inc(s_out, 16)
            sp.dma_start(t["o_ffn_conv_s"][0, :, 0:1, :], t["state_ffn_conv"][0, :, 1:2, :]).then_inc(s_out, 16)

            for a in range(5):
                sp.wait_ge(psum_free[(J_LOUT + a) % 4], free_value(J_LOUT + a))
            sp.dma_start(t["o_kv_p"].rearrange("l b (a p) d -> p (l b a) d", p=P), otok[:, 0:4, 0:KV]).then_inc(s_out, 16)
            sp.dma_start(t["o_kr_p"].rearrange("l b (a p) d -> p (l b a) d", p=P), otok[:, 0:4, KV:KV + ROPE]).then_inc(s_out, 16)
            sp.dma_start(t["o_kv_s"].rearrange("l b s d -> (l b s) d"), otok[0:NS, 4, 0:KV]).then_inc(s_out, 16)
            sp.dma_start(t["o_kr_s"].rearrange("l b s d -> (l b s) d"), otok[0:NS, 4, KV:KV + ROPE]).then_inc(s_out, 16)
            for a in range(5, 7):
                sp.wait_ge(psum_free[(J_LOUT + a) % 4], free_value(J_LOUT + a))
            sp.dma_start(t["o_lru_h_p"].rearrange("l b w -> (l b) w"), lout[0:1, 0, :]).then_inc(s_out, 16)
            sp.dma_start(t["o_lru_h_s"].rearrange("l b w -> (l b) w"), lout[1:9, 0, :]).then_inc(s_out, 16)
            sp.dma_start(t["o_lru_conv_p"].rearrange("l b r w -> (l b r) w"), lout[0:3, 1, :]).then_inc(s_out, 16)
            sp.dma_start(t["o_lru_conv_s"][0, :, 2, :], lout[3:11, 1, :]).then_inc(s_out, 16)
            sp.dma_start(newrow[0:1, :, :], otok[0:NS, 4, :]).then_inc(s_new, 16)
            for e in range(2):
                full(sp, HEAD_FIRST.vw[e])
                head_weights(e, bass.ds(2 + e, 1))
            with sp.Fori(0, HEAD_LAPS - 1) as i:
                for e in range(2):
                    full(sp, HEAD_LAP.vw[e], HEAD_LAP.count // 4 * i)
                    head_weights(e, bass.ds(2 * i + 4 + e, 1))
            full(sp, J_SPREAD)
            sp.dma_start(wv, t["w_ukv"][0].rearrange("p (h n) -> p h n", h=HEADS)[:, :, NOPE:]).then_inc(s_wv, 16)
            wo = t["w_o"].rearrange("l (k p) n -> p (l k) n", p=P)
            for m in range(KT):
                if m >= 3:
                    sp.wait_ge(s_wolo, m - 2)
                sp.dma_start(woR[:, m % 3, :, :], wo[:, :, P * m:P * m + P]).then_inc(s_wo[m % 3], 16)
            full(sp, J_PVLAST)
            wu = t["w_up"].rearrange("l (k p) (g n) -> p (l k) g n", p=P, g=2)

            def up_weights(c, m):
                for g in range(2):
                    sp.dma_start(wup[:, c, KT * g:KT * g + KT, :], wu[:, :, g, m]).then_inc(s_wup[c], 16)

            for m in range(2):
                up_weights(m, bass.ds(P * m, P))
            full(sp, J_WO[KT - 1])
            sp.dma_start(fs_tok, t["state_ffn_conv"].rearrange("l b r w -> (l b r) w")).then_inc(s_fst, 16)
            wd = t["w_down"].rearrange("l (k p) n -> p (l k) n", p=P)
            with sp.Fori(1, FT // 2) as i:
                for e in range(2):
                    sp.wait_ge(s_wlo, 4 * i + 2 * e - 2)
                    up_weights(e, bass.ds(2 * P * i + P * e, P))

            def last_rows(r):
                for j in J_FT[2 * r:2 * r + 2]:
                    sp.wait_ge(psum_free[j % 4], free_value(j))
                c, w = 2 * D * r, min(2 * D, 2 * FF - 2 * D * r)
                sp.dma_start(t["o_ffn_conv_p"][0, 0, :, c:c + w], ft_tok[0:2, 0:w]).then_inc(s_kept, 16)
                sp.dma_start(t["o_ffn_conv_s"][0, :, 1, c:c + w], ft_tok[2:10, 0:w]).then_inc(s_kept, 16)

            for m in range(KT):
                if m == 1:
                    full(sp, J_UP + 2 * FT - 1)
                else:
                    sp.wait_ge(s_wlo, 2 * FT + 3 * max(m - 1, 0))
                sp.dma_start(wdn[:, m % 2, :, :], wd[:, :, P * m:P * m + P]).then_inc(s_wdn[m % 2], 16)
                if m == 5:
                    last_rows(0)
            last_rows(1)
            last_rows(2)
            for n in range(5):
                sp.wait_ge(psum_free[(J_Y + n) % 4], free_value(J_Y + n))
                if n < 4:
                    sp.dma_start(t["o_y_p"][0, P * n:P * n + P, :], y_tok[n]).then_inc(s_out, 16)
                else:
                    sp.dma_start(t["o_y_s"].rearrange("b s d -> (b s) d"), y_tok[n][0:NS, :]).then_inc(s_out, 16)
            sp.wait_ge(s_kept, 16 * 6)
            sp.wait_ge(s_out, 16 * 15)

        @block.gpsimd
        def _(pool):
            nc.gpsimd.memset(par_rows[:, :, :], 0.0).then_inc(s_parz, 1)
            nc.gpsimd.memset(BD[:, :, :, :], 0.0).then_inc(s_bdz, 1)

            def add_squares(first, n, squares, added):
                for k in range(1, n):
                    pool.wait_ge(s_sq, squares + k + 1)
                    if k > 1:
                        pool.wait_ge(s_nsum, added + k - 1)
                    nc.gpsimd.tensor_tensor(sq[:, first, :], sq[:, first, :], sq[:, first + k, :], ALU.add).then_inc(s_nsum, 1)

            add_squares(0, KT, 0, 0)
            wa = t["w_ada"].rearrange("l (k p) (c n) -> p (l k) c n", p=P, n=256)

            def second_chunk(c):
                chunk_used(pool, 4 + c)
                nc.gpsimd.dma_start(ring[:, c % 4, :, :], wa[:, :, 8 + c, :]).then_inc(s_ada2[c % 4], 16)

            def in_low(n):
                pool.wait_ge(s_wihi, split_tiles(n))
                nc.gpsimd.tensor_tensor(wiL[:, n % 2, :, :], RA[:, n % 3, :, :], wiH[:, n % 2, :, :].bitcast(F32), ALU.subtract).then_inc(s_wilo, 1)

            for c in range(2):
                second_chunk(c)
            for n in range(12):
                if n != N_KR:
                    in_low(n)
            full(pool, J_WIN[7])
            nc.gpsimd.memset(QBD[:, :, :, :], 0.0).then_inc(s_bdz, 1)
            for c in range(2, 8):
                second_chunk(c)
            add_squares(4, LT, KT + 4, KT - 1)
            for c in range(8, 16):
                second_chunk(c)
            cl = t["cache_kv_latent"].rearrange("l n (r k) d -> (l n r) (k d)", r=8)
            ck = t["cache_k_rope"].rearrange("l n (r k) d -> (l n r) (k d)", r=4)

            def fetch(dst, src, rows, done):
                nc.gpsimd.indirect_dma_start(dst.rearrange("p c d -> p (c d)"), None, src, bass.IndirectOffsetOnAxis(ap=rows, axis=0)).then_inc(done, 16)

            def cached_keys(e, s):
                fetch(kr_[e][:, 0:PAGES, :], ck, row_of[:, s:s + 1], s_krc[e])

            def cached_latents(e, s):
                for n in range(2):
                    fetch(lat[e][:, n * PAGES // 2:(n + 1) * PAGES // 2, :], cl, half_of[:, n, s:s + 1], s_lat[n][e])

            full(pool, J_ROW[5])
            pool.wait_ge(s_row, 3)
            for n in range(2):
                cached_keys(n, n)
                cached_latents(n, n)
            for e in range(2):
                nc.gpsimd.memset(lat[e][:, PAGES, :], 0.0).then_inc(s_clr, 1)
                nc.gpsimd.memset(kr_[e][:, PAGES:36, :], 0.0).then_inc(s_clr, 1)
            pool.wait_ge(s_clr, 4)
            pool.wait_ge(s_new, 16)

            def new_key(e, s):
                nc.gpsimd.tensor_copy(kr_[e][0:1, PAGES, :], newrow[0:1, s, KV:KV + ROPE]).then_inc(s_newc, 1)

            def new_latent(e, s):
                nc.gpsimd.tensor_copy(lat[e][0:1, PAGES, :], newrow[0:1, s, 0:KV]).then_inc(s_newc, 1)

            def all_max(e, v):
                pool.wait_ge(s_mx, v)
                nc.gpsimd.partition_all_reduce(mx[e], mx[e], P, RMAX).then_inc(s_am, 1)

            for n in range(2):
                new_key(n, n)
                new_latent(n, n)
            def low_latents(v, g):
                pool.wait_ge(s_tT, NG * (v - 1) + g + 1)
                if g < 2:
                    j = J_FIRST_T + g if v == 1 else J_UNIT1 + UNIT * (v - 3) + UJ["tn", g] if v > 2 else unit_job(J_DEC, "tn", g)
                else:
                    j = unit_job(J_DEC if v == 1 else J_UNIT1 + UNIT * (v - 2), "t", g)
                pool.wait_ge(psum_free[j % 4], free_value(j))
                c = 4 * P - GT[g] * P
                nc.gpsimd.tensor_tensor(latL[:, g % 3, c:4 * P], turned[:, g % 3, c:4 * P], latH[:, g % 3, c:4 * P].bitcast(F32), ALU.subtract).then_inc(s_lo, 1)

            for g in range(2):
                low_latents(1, g)
            for v in range(1, NS + 1):
                for g in range(NG):
                    if 1 < v < NS and g == 0:
                        j = unit_job(J_DEC if v == 2 else J_UNIT1 + UNIT * (v - 3), "t", NG - 1)
                        full(pool, j)
                        cached_keys(v % 2, v)
                        new_key(v % 2, v)
                    if v > 1 and g == 2:
                        all_max(v % 2, v - 1)
                    if g + 2 < NG:
                        low_latents(v, g + 2)
                    elif v < NS:
                        low_latents(v + 1, g + 2 - NG)
                    if 1 < v < NS and g == PV_AT:
                        full(pool, J_UNIT1 + UNIT * (v - 2) + UJ["pv", 0])
                        cached_latents(v % 2, v)
                        new_latent(v % 2, v)
            all_max(1, NS)
            add_squares(0, KT - 1, KT + 12, KT - 1 + LT - 1)
            pool.wait_ge(s_rs, 7)
            for k in range(KT // 2, KT):
                nc.gpsimd.tensor_tensor(h2[:, k, 0:NP], xT[:, k, 0:NP], rs[:, 0:NP], ALU.mult).then_inc(s_hq, 1)
            with pool.Fori(0, FT // 2) as i:
                for e in range(2):
                    for g in range(2):
                        pool.wait_ge(psum_free[(J_UP + 2 * e + g) % 4], free_value(J_UP + 2 * e + g, i))
                        nc.gpsimd.tensor_copy(UT[:, bass.ds(FT * g + 2 * i + e, 1), :], UU[e][:, g, NP:UW]).then_inc(s_ut, 1)

        @block.tensor
        def _(pe):
            mm = nc.tensor.matmul

            def tr(out, in_, n):
                return nc.tensor.transpose(out, in_, ident[0:n, 0:n])

            def both(j, lhsT, src, start, stop, rows=(0, P), lap=0):
                for h in range(2):
                    last = mm(ps[j % 4][rows[0]:rows[1], h, 0:H], lhsT, src[:, h * H:(h + 1) * H], start=start, stop=stop)
                return last

            pe.wait_ge(s_ident, 16)
            pe.wait_ge(s_x, 32)
            for k in range(KT):
                j = J_XT + k
                claim(pe, j)
                for a in range(4):
                    tr(flat(j)[:, P * a:P * a + P], x_tok[:, a, P * k:P * k + P], P)
                tr(flat(j)[:, NP:T], xs_tok[:, P * k:P * k + P], NS).then_inc(psum_full[j % 4], 1)
            claim(pe, J_C)
            pe.wait_ge(s_silu, 2)
            for k in range(KT):
                last = tr(flat(J_C)[:, 9 * k:9 * k + 9], c_tok[:, P * k:P * k + P], 9)
            last.then_inc(psum_full[J_C % 4], 1)
            def mod_rows(n):
                j = J_ROW[n]
                claim(pe, j)
                for c in range(4):
                    if n < 2:
                        pe.wait_ge(s_ada[c], 16 * (n + 1))
                    else:
                        pe.wait_ge(s_ada2[c], 16 * (n - 1))
                    for k in range(KT):
                        last = mm(flat(j)[0:9, 256 * c:256 * c + 256], cT[:, k, :], ring[:, c, k, :], start=(k == 0), stop=(k == KT - 1))
                    last.then_inc(s_ada_used if c < 3 else psum_full[j % 4], 1)

            def mod_columns(n):
                j = J_COL[n]
                claim(pe, j)
                pe.wait_ge(psum_free[J_ROW[n] % 4], free_value(J_ROW[n]))
                for m in range(8):
                    last = tr(flat(j)[:, 9 * m:9 * m + 9], rows9(n)[:, P * m:P * m + P], 9)
                last.then_inc(psum_full[j % 4], 1)

            def norm_sum(j, n, base, first=0):
                claim(pe, j)
                for k in range(n):
                    pe.wait_ge(s_sq, base + k + 1)
                    last = both(j, ones, sq[:, first + k, :], k == 0, k == n - 1)
                last.then_inc(psum_full[j % 4], 1)

            def added_sum(j, tile, nth):
                claim(pe, j)
                pe.wait_ge(s_nsum, nth)
                both(j, ones, sq[:, tile, :], True, True).then_inc(psum_full[j % 4], 1)

            pe.wait_ge(psum_free[J_C % 4], free_value(J_C))
            mod_rows(0)
            claim(pe, J_PAR)
            pe.wait_ge(s_par, 16 * 21)
            tr(flat(J_PAR)[:, 0:NROWS], par_rows[0:NROWS, 0, :], NROWS).then_inc(psum_full[J_PAR % 4], 1)
            claim(pe, J_FPAR)
            tr(flat(J_FPAR)[:, 0:88], par_rows[0:88, 1, :], 88)
            tr(flat(J_FPAR)[:, 88:176], par_rows[0:88, 2, :], 88).then_inc(psum_full[J_FPAR % 4], 1)
            claim(pe, J_STATE)
            for k in range(LT):
                tr(flat(J_STATE)[:, 24 * k:24 * k + 24], st_tok[:, P * k:P * k + P], 24)
            for k in range(LT):
                last = tr(flat(J_STATE)[:, 96 + NS * k:96 + NS * k + NS], h0_tok[:, P * k:P * k + P], NS)
            last.then_inc(psum_full[J_STATE % 4], 1)
            pe.wait_ge(s_cst, 16)
            added_sum(J_N1, 0, KT - 1)
            mod_rows(1)
            mod_columns(0)
            mod_columns(1)

            def three(j, wH, wL, m, srcH, srcL, k, first, final):
                for n, (w, src) in enumerate(((wH, srcH), (wH, srcL), (wL, srcH))):
                    last = both(j, w[:, m, :], src[:, k, :], first and n == 0, final and n == 2)
                return last

            def w_in(n):
                m = WIN_ORDER[n]
                j = J_WIN[m]
                rows = (0, P) if m < 11 else (NOPE, QK)
                w = P if m < 11 else ROPE
                claim(pe, j)
                if n == N_KR:
                    pe.wait_ge(s_win[n % 3], 16 * (n // 3 + 1))
                else:
                    pe.wait_ge(s_wilo, split_tiles(n))
                for k in range(KT):
                    if n == 0:
                        pe.wait_ge(s_hlo, k + 1)
                    if n == N_KR:
                        last = both(j, RA[:, n % 3, k, 0:w], h1[:, k, :], k == 0, k == KT - 1, rows)
                    else:
                        last = three(j, wiH[:, n % 2, :, :], wiL[:, n % 2, :, :], k, hH, h1L, k, k == 0, k == KT - 1)
                last.then_inc(psum_full[j % 4], 1)

            for n in range(8):
                w_in(n)
            pe.wait_ge(s_bd, 64)
            for g in range(2):
                for k in range(LT):
                    j = J_GATE + g * LT + k
                    claim(pe, j)
                    pe.wait_ge(s_xc, k + 1)
                    both(j, BD[:, g, k, :], XC[:, k, :], True, True).then_inc(psum_full[j % 4], 1)
            w_in(8)
            w_in(9)
            norm_sum(J_NQ, 2, KT)
            norm_sum(J_NKV, 1, KT + 2, 2)
            R = (NOPE, QK)
            j = J_KR[0]
            claim(pe, j)
            pe.wait_ge(s_sq, KT + 4)
            both(j, C("blk", QK, R)[:, NOPE:QK], sq[NOPE:QK, 3, :], True, True, R).then_inc(psum_full[j % 4], 1)
            w_in(10)
            w_in(11)
            j = J_KR[1]
            claim(pe, j)
            pe.wait_ge(s_kr, 1)
            both(j, C("perm", QK, R)[:, NOPE:QK], krT[NOPE:QK, :], True, True, R).then_inc(psum_full[j % 4], 1)
            mod_rows(2)
            mod_rows(3)
            mod_columns(2)
            added_sum(J_NLRU, 4, KT - 1 + LT - 1)
            mod_rows(4)
            mod_columns(3)
            pe.wait_ge(s_kr, 2)
            pe.wait_ge(s_kvn, 1)
            for a in range(5):
                j = J_LOUT + a
                n = P if a < 4 else NS
                claim(pe, j)
                tr(flat(j)[0:n, 0:KV], kvT[:, P * a:P * a + n], P)
                mm(flat(j)[0:n, KV:KV + ROPE], krT[NOPE:QK, P * a:P * a + n], C("ident", QK, R)[:, NOPE:QK],
                   start=True, stop=True).then_inc(psum_full[j % 4], 1)
            pe.wait_ge(s_lrud, 1)
            for n, (src, c0, w) in enumerate(((TA, NP - 1, 9), (XX, NP, 11))):
                j = J_LOUT + 5 + n
                claim(pe, j)
                for k in range(LT):
                    last = tr(flat(j)[0:w, P * k:P * k + P], src[:, k, c0:c0 + w], P)
                last.then_inc(psum_full[j % 4], 1)

            mod_rows(5)
            mod_columns(4)
            mod_columns(5)

            def project(J, e, pair, lap):
                pe.wait_ge(s_hw[e], 32 * (pair + 1))
                claim(pe, J.q[e], lap)
                for k in range(2):
                    last = both(J.q[e], wuq[:, e, k, :], qlT[:, k, :], k == 0, k == 1, (0, QK))
                last.then_inc(psum_full[J.q[e] % 4], 1)
                claim(pe, J.kn[e], lap)
                mm(flat(J.kn[e])[0:NOPE, 0:NP], wukv[:, e, 0:NOPE], kvT[:, 0:NP], start=True, stop=True)
                tr(flat(J.kn[e])[0:NOPE, 512:512 + P], wukv[:, e, 0:NOPE], P).then_inc(psum_full[J.kn[e] % 4], 1)

            def mean_squares(J, e, pair, lap):
                claim(pe, J.qms[e], lap)
                pe.wait_ge(s_qsq, 2 * pair + e + 1)
                both(J.qms[e], C("blk", QK, (0, QK)), sq[0:QK, 2 * e, :], True, True, (0, QK)).then_inc(psum_full[J.qms[e] % 4], 1)
                claim(pe, J.kms[e], lap)
                pe.wait_ge(s_ksq, 2 * pair + e + 1)
                mm(flat(J.kms[e])[:, 0:NP], C("blk", P, (0, NOPE)), sq[0:NOPE, 4 + 2 * e, 0:NP], start=True,
                   stop=True).then_inc(psum_full[J.kms[e] % 4], 1)

            def rotate(J, e, pair, lap):
                claim(pe, J.qrot[e], lap)
                pe.wait_ge(s_qn, 2 * pair + e + 1)
                both(J.qrot[e], C("perm", QK, (0, QK))[:, NOPE:QK], hb[e]["q"][0:QK, :], True, True, R).then_inc(psum_full[J.qrot[e] % 4], 1)

            def values(J, e, lap):
                claim(pe, J.vw[e], lap)
                for a in range(4):
                    last = mm(flat(J.vw[e])[:, VD * a:VD * a + VD], kvT[:, P * a:P * a + P], wukv[:, e, NOPE:P], start=True, stop=True)
                last.then_inc(psum_full[J.vw[e] % 4], 1)

            def through_keys(J, e, pair, lap):
                claim(pe, J.qa[e], lap)
                pe.wait_ge(s_gq, 2 * pair + e + 1)
                pe.wait_ge(s_wt, 2 * pair + e + 1)
                mm(flat(J.qa[e])[:, 0:NS], hb[e]["wt"][0:NOPE, :], hb[e]["gq"][0:NOPE, :], start=True, stop=True).then_inc(psum_full[J.qa[e] % 4], 1)

            def scores(J, e, pair, lap):
                pe.wait_ge(s_qr, 2 * pair + e + 1)
                pe.wait_ge(s_kn, 2 * pair + e + 1)
                for n in range(4):
                    j = J.s[e][n]
                    claim(pe, j, lap)
                    mm(flat(j)[:, 0:P * (n + 1)], hb[e]["q"][0:QK, P * n:P * n + P], hb[e]["k"][0:QK, 0:P * (n + 1)],
                       start=True, stop=True).then_inc(psum_full[j % 4], 1)

            def turn_probs(J, e, pair, lap):
                for n in range(4):
                    j = J.p[e][n]
                    claim(pe, j, lap)
                    pe.wait_ge(s_pn, 8 * pair + 4 * e + n + 1)
                    for a in range(n + 1):
                        last = tr(flat(j)[:, P * a:P * a + P], hb[e]["p"][:, POFF[n] + P * a:POFF[n] + P * a + P], P)
                    last.then_inc(psum_full[j % 4], 1)

            def mix(J, e, lap):
                claim(pe, J.pv[e], lap)
                for n in range(4):
                    pe.wait_ge(psum_free[J.p[e][n] % 4], free_value(J.p[e][n], lap))
                for a in range(4):
                    last = mm(flat(J.pv[e])[VD * e:VD * e + VD, P * a:NP], hb[e]["v"][:, VD * a:VD * a + VD],
                              hb[e]["pt"][:, a, P * a:NP], start=(a == 0), stop=(a == 3))
                last.then_inc(psum_full[J.pv[e] % 4], 1)

            pe.wait_ge(s_ql, 2)
            J = HEAD_FIRST
            for e in range(2):
                project(J, e, 0, 0)
            for e in range(2):
                mean_squares(J, e, 0, 0)
            for e in range(2):
                rotate(J, e, 0, 0)
            for e in range(2):
                through_keys(J, e, 0, 0)
            for e in range(2):
                values(J, e, 0)
            with pe.Fori(0, HEAD_LAPS) as i:
                J, lap = HEAD_LAP, HEAD_LAP.count // 4 * i
                for e in range(2):
                    scores(J, e, i, lap)
                for e in range(2):
                    project(J, e, i + 1, lap)
                turn_probs(J, 0, i, lap)
                for e in range(2):
                    mean_squares(J, e, i + 1, lap)
                turn_probs(J, 1, i, lap)
                for e in range(2):
                    rotate(J, e, i + 1, lap)
                for e in range(2):
                    through_keys(J, e, i + 1, lap)
                for e in range(2):
                    mix(J, e, lap)
                for e in range(2):
                    values(J, e, lap)
            J = HEAD_LAST
            for e in range(2):
                scores(J, e, HEAD_LAPS, 0)
            for e in range(2):
                turn_probs(J, e, HEAD_LAPS, 0)
            for e in range(2):
                mix(J, e, 0)

            j = J_SPREAD
            claim(pe, j)
            pe.wait_ge(s_qr, HEADS)
            mm(flat(j)[:, 0:NS * HEADS], C("spread", P, R), QRS[NOPE:QK, :, :], start=True, stop=True).then_inc(psum_full[j % 4], 1)

            def pv(j, lap, e, v):
                claim(pe, j, lap)
                pe.wait_ge(s_pd, v)
                for n in range(KTILES):
                    last = mm(flat(j)[0:HEADS, 0:KV], snd[e][:, HEADS * n:HEADS * n + HEADS], lat[e][:, n, :], start=(n == 0), stop=(n == KTILES - 1))
                last.then_inc(psum_full[j % 4], 1)
                claim(pe, j + 1, lap)
                mm(flat(j + 1)[0:HEADS, 0:1], pd[e], ones[:, 0:1], start=True, stop=True).then_inc(psum_full[(j + 1) % 4], 1)

            def transposes(j, lap, e, v, g):
                claim(pe, j, lap)
                if g == 0:
                    pe.wait_ge(s_krc[e], 8 * (v + 1 - e))
                    pe.wait_ge(s_lat[0][e], 8 * (v + 1 - e))
                if g == 4:
                    pe.wait_ge(s_lat[1][e], 8 * (v + 1 - e))
                if g == NG - 1:
                    pe.wait_ge(s_newc, 2 * v)
                for n in range(GT[g]):
                    c = P * (4 - GT[g] + n)
                    tr(flat(j)[:, c:c + P], lat[e][:, 4 * g + n, :], P)
                tr(flat(j)[:, 512:512 + P], kr_[e][:, 4 * g:4 * g + 4, :].rearrange("p c d -> p (c d)"), P).then_inc(psum_full[j % 4], 1)

            def unit(base, lap, e, s, v):
                pe.wait_ge(s_kwq, 2 * v)
                for g in range(NG):
                    if g + 2 < NG:
                        transposes(unit_job(base, "t", g + 2), lap, e, v, g + 2)
                    elif base != J_LAST:
                        transposes(unit_job(base, "tn", g + 2 - NG), lap, 1 - e, v + 1, g + 2 - NG)
                    t_ = unit_job(base, "t", g)
                    pe.wait_ge(psum_free[t_ % 4], free_value(t_, lap))
                    pe.wait_ge(s_lo, NG * (v - 1) + g + 1)
                    for n in range(GT[g]):
                        j = unit_job(base, "k", 4 * g + n)
                        claim(pe, j, lap)
                        if n == 0:
                            mm(ps[j % 4][:, 0, KWW:KWW + 4 * HEADS], turned[:, g % 3, 4 * P:5 * P], QBD[:, bass.ds(s, 1), :, :], start=True, stop=True)
                        at = P * (4 - GT[g] + n)
                        products = ((latH, kwH), (latH, kwL), (latL, kwH))
                        for i, (a, b) in enumerate(products):
                            for h in range(2):
                                last = mm(ps[j % 4][:, h, 0:KWW], a[:, g % 3, at:at + P], b[:, e, h, :],
                                          start=(i == 0), stop=(i == 2))
                        last.then_inc(psum_full[j % 4], 1)
                    if g == PV_AT and base != J_DEC:
                        pv(unit_job(base, "pv", 0), lap, 1 - e, v - 1)

            for g in range(2):
                transposes(J_FIRST_T + g, 0, 0, 1, g)
            pe.wait_ge(s_qbd, 1)
            pe.wait_ge(s_kw, 4)
            unit(J_DEC, 0, 0, 0, 1)
            with pe.Fori(0, 3) as i:
                unit(J_UNIT1, 2 * UNIT // 4 * i, 1, 2 * i + 1, 2 * i + 2)
                unit(J_UNIT1 + UNIT, 2 * UNIT // 4 * i, 0, 2 * i + 2, 2 * i + 3)
            unit(J_LAST, 0, 1, 7, 8)
            pv(J_PVLAST, 0, 1, NS)
            claim(pe, J_OL)
            pe.wait_ge(psum_free[J_PVLAST % 4], free_value(J_PVLAST))
            for n in range(NS):
                last = tr(flat(J_OL)[:, HEADS * n:HEADS * n + HEADS], OLR[:, n, :], HEADS)
            last.then_inc(psum_full[J_OL % 4], 1)

            def out_projection(m, ks):
                j = J_WO[m]
                if ks[0] == 0:
                    claim(pe, j)
                    pe.wait_ge(s_wolo, m + 1)
                for k in ks:
                    if m == 0:
                        pe.wait_ge(s_mlo, k + 1)
                    for n, (w, src) in enumerate(((woH, mixed_high), (woH, mixed_low), (woL, mixed_high))):
                        last = both(j, w[:, m % 2, k, :], src[k], k == 0 and n == 0, k == KT - 1 and n == 2)
                if ks[-1] == KT - 1:
                    last.then_inc(psum_full[j % 4], 1)

            out_projection(0, (0, 1))
            j = J_VP
            claim(pe, j)
            pe.wait_ge(s_wv, 16)
            pe.wait_ge(psum_free[J_OL % 4], free_value(J_OL))
            for h in range(HEADS):
                last = mm(flat(j)[VD * (h % 2):VD * (h % 2) + VD, NS * (h // 2):NS * (h // 2) + NS], wv[:, h, :], OL[:, :, h], start=True, stop=True)
            last.then_inc(psum_full[j % 4], 1)
            out_projection(0, (2, 3))
            norm_sum(J_NMLA, LT, KT + 8)
            out_projection(1, range(LT))
            out_projection(0, range(LT, KT))
            out_projection(1, range(LT, KT))
            for m in range(2, KT):
                out_projection(m, range(KT))
            claim(pe, J_N2)
            pe.wait_ge(s_nsum, KT - 1 + LT - 1 + KT - 2)
            both(J_N2, ones, sq[:, 0, :], True, False)
            pe.wait_ge(s_sq, 2 * KT + 12)
            both(J_N2, ones, sq[:, KT - 1, :], False, True).then_inc(psum_full[J_N2 % 4], 1)
            j = J_FST
            claim(pe, j)
            pe.wait_ge(s_fst, 16)
            for m in range(2 * FT):
                last = tr(flat(j)[:, 2 * NS * m:2 * NS * m + 2 * NS], fs_tok[:, P * m:P * m + P], 2 * NS)
            last.then_inc(psum_full[j % 4], 1)
            with pe.Fori(0, FT // 2) as i:
                for e in range(2):
                    for g in range(2):
                        j = J_UP + 2 * e + g
                        claim(pe, j, i)
                        pe.wait_ge(s_wlo, 4 * i + 2 * e + g + 1)
                        for k in range(KT):
                            if e == 0 and g == 0:
                                pe.wait_ge(s_hlo, KT + k + 1)
                            last = three(j, wuH, wuL, KT * g + k, hH, hL, k, k == 0, k == KT - 1)
                        last.then_inc(psum_full[j % 4], 1)
            for m in range(KT):
                j = J_DOWN[m]
                claim(pe, j)
                for k in range(FT):
                    for n, (a, b) in enumerate(PIECES):
                        if k == a:
                            pe.wait_ge(s_wlo, 2 * FT + 3 * m + n + 1)
                    if m == 0 and k in (0, FT - 2, FT - 1):
                        pe.wait_ge(s_hid, max(k + 1, FT - 2))
                    last = three(j, wdH[m % 2], wdL[m % 2], k, actH, actL, k, k == 0, k == FT - 1)
                last.then_inc(psum_full[j % 4], 1)
                if m % 2 == 1 and m < KT - 1:
                    pe.wait_ge(s_ut, 2 * FT)
                    for n in (m - 1, m):
                        j = J_FT[n]
                        claim(pe, j)
                        for c in range(0, ft_width(n), P):
                            last = tr(flat(j)[0:10, c:c + P], UT[:, KT * n + c // P, :], P)
                        last.then_inc(psum_full[j % 4], 1)
            for n in range(5):
                j = J_Y + n
                w = P if n < 4 else NS
                claim(pe, j)
                for k in range(KT):
                    if n == 0:
                        pe.wait_ge(s_x2, k + 1)
                    last = tr(flat(j)[0:w, P * k:P * k + P], xT[:, k, P * n:P * n + w], P)
                last.then_inc(psum_full[j % 4], 1)

        @block.scalar
        def _(act):
            A = nc.scalar.activation
            st = Steps(act, s_act)
            epsc = small[:, 0:1]

            def rstd(j, width, rows=(0, P), lap=0, dst=None):
                full(act, j, lap)
                dst = rs[rows[0]:rows[1], :] if dst is None else dst
                A(two(dst), halves(j, rows), ACT.Ln, bias=epsc[rows[0]:rows[1], :], scale=1.0 / width).then_inc(psum_free[j % 4], 1)
                act.wait_ge(psum_free[j % 4], free_value(j, lap))
                return A(dst, dst, ACT.Exp, scale=-0.5)

            act.wait_ge(s_parz, 1)

            def load_rows(name, src, part=0):
                n = src.shape[0]
                act.dma_start(par_rows[ROWS[name]:ROWS[name] + n, part, 0:src.shape[1]], src).then_inc(s_par, 16)

            for name in ("b_ada", "norm1_g", "lru_conv_b", "lru_b_a", "lru_b_x", "lru_lambda",
                         "q_lora_norm_g", "kv_lora_norm_g", "lru_out_norm_g", "mla_out_norm_g", "norm2_g"):
                load_rows(name, t[name].rearrange("l (r p) -> (l r) p", p=P))
            act.wait_ge(s_c, 32)
            A(c_th, c_tok, ACT.Tanh, scale=0.5).then_inc(s_silu, 1)
            load_rows("lru_conv_w", t["lru_conv_w"].rearrange("l w (r p) -> (l w r) p", p=P))
            for name, a, b in (("gq", "q_nope_norm_g", "q_rope_norm_g"), ("gk", "k_nope_norm_g", "k_rope_norm_g")):
                r = ROWS[name]
                act.dma_start(par_rows[r:r + 1, 0, 0:NOPE], t[a]).then_inc(s_par, 16)
                act.dma_start(par_rows[r:r + 1, 0, NOPE:QK], t[b]).then_inc(s_par, 16)
            fw = t["ffn_conv_w"].rearrange("l w (r p) -> (l w r) p", p=P)
            act.dma_start(par_rows[0:4 * FT, 1, :], fw[0:4 * FT, :]).then_inc(s_par, 16)
            act.dma_start(par_rows[0:2 * FT, 2, :], fw[4 * FT:6 * FT, :]).then_inc(s_par, 16)
            act.dma_start(par_rows[2 * FT:4 * FT, 2, :],
                         t["ffn_conv_b"].rearrange("l (r p) -> (l r) p", p=P)).then_inc(s_par, 16)
            act.dma_start(st_tok, t["state_lru_conv"].rearrange("l b r w -> (l b r) w")).then_inc(s_par, 16)
            act.dma_start(h0_tok, t["state_lru_h"].rearrange("l b w -> (l b) w")).then_inc(s_par, 16)
            for r in range(4):
                act.dma_start(page_of[r:P:4, :], t["page_table"].rearrange("b n -> n b"), allow_slow_non_contiguous=True).then_inc(s_pt, 16)
            for k in range(KT):
                j = J_XT + k
                act.wait_ge(psum_free[j % 4], free_value(j))
                A(sq[:, k, :], xT[:, k, :], ACT.Square).then_inc(s_sq, 1)
            act.wait_ge(s_sp, 1)
            A(small[:, 8:12], small[:, 4:8], ACT.Exp, scale=-1.0).then_inc(s_sp, 1)

            def in_high(n):
                act.wait_ge(s_win[n % 3], 16 * (n // 3 + 1))
                if n >= 2:
                    full(act, J_WIN[WIN_ORDER[n - 2]])
                A(wiH[:, n % 2, :, :], RA[:, n % 3, :, :], ACT.Copy).then_inc(s_wihi, 1)

            rstd(J_N1, D).then_inc(s_rs, 1)
            in_high(0)
            in_high(1)
            act.wait_ge(s_gain, 1)
            for k in range(KT):
                act.wait_ge(s_hp, k + 1)
                A(h1[:, k, 0:NP], h1[:, k, 0:NP], ACT.Identity, bias=modT[:, k, 0:1], scale=gmod[:, k, 0:1]).then_inc(s_h, 1)
            for n in range(2, 6):
                in_high(n)
            for m, dst in ((8, qlT[:, 0, :]), (9, qlT[:, 1, :]), (10, kvT[:, :]), (11, krT[NOPE:QK, :])):
                j = J_WIN[m]
                rows = (0, P) if m < 11 else (NOPE, QK)
                full(act, j)
                A(two(dst), halves(j, rows), ACT.Copy).then_inc(psum_free[j % 4], 1)
                act.wait_ge(psum_free[j % 4], free_value(j))
                A(sq[rows[0]:rows[1], m - 8, :], dst, ACT.Square).then_inc(s_sq, 1)
                if m != 9:
                    in_high({8: 6, 10: 8, 11: 9}[m])
            act.wait_ge(s_sp, 3)
            for g, dst in ((0, TA), (1, TI)):
                for k in range(LT):
                    j = J_GATE + g * LT + k
                    full(act, j)
                    A(two(dst[:, k, :]), halves(j), ACT.Tanh, bias=small[:, 20 + 4 * g + k:21 + 4 * g + k],
                      scale=0.5).then_inc(psum_free[j % 4], 1)
            for k in range(LT):
                act.wait_ge(psum_free[(J_GATE + k) % 4], free_value(J_GATE + k))
            for k in range(LT):
                v = st.did(A(AA[:, k, :], TA[:, k, :], ACT.Exp, bias=small[:, 32 + k:33 + k], scale=small[:, 32 + k:33 + k]))
            st.need(v)
            for k in range(LT):
                A(TA[:, k, :], TA[:, k, :], ACT.Tanh, bias=small[:, 28 + k:29 + k], scale=small[:, 28 + k:29 + k]).then_inc(s_ta, 1)

            def gate_branch(k):
                j = J_WIN[LT + k]
                full(act, j)
                A(two(GG[:, k, :]), halves(j), ACT.Copy).then_inc(psum_free[j % 4], 1)

            nc.scalar.preload_act_table_set("natural_log_exp_and_others")
            gate_branch(0)
            in_high(10)
            act.wait_ge(s_tiny, 1)
            st.did(A(sq[:, 4:8, :], TA[:, :, :], ACT.Ln, bias=1.0))
            st.seq(A(TA[:, :, :], TA[:, :, :], ACT.Ln))
            act.sem_inc(s_lru, 1)
            gate_branch(1)
            in_high(11)
            act.wait_ge(s_tiny, 2)
            A(TA[:, :, :], TA[:, :, :], ACT.Exp, scale=0.5).then_inc(s_lru, 1)
            rstd(J_NQ, QL, dst=sq[:, 0, :]).then_inc(s_rs, 1)
            rstd(J_NKV, KV, dst=sq[:, 1, :]).then_inc(s_rs, 1)
            rstd(J_KR[0], 1, (NOPE, QK), dst=sq[NOPE:QK, 2, :]).then_inc(s_rs, 1)
            gate_branch(2)
            gate_branch(3)
            for k in range(LT):
                act.wait_ge(psum_free[J_WIN[LT + k] % 4], free_value(J_WIN[LT + k]))
            A(GG[:, :, :], GG[:, :, :], ACT.Gelu_apprx_tanh).then_inc(s_g, 1)
            nc.scalar.preload_act_table_set("natural_log_exp_and_others")
            act.wait_ge(s_lrud, 2)
            for k in range(LT):
                A(sq[:, 4 + k, :], XC[:, k, :], ACT.Square).then_inc(s_sq, 1)
            rstd(J_NLRU, LW).then_inc(s_rs, 1)

            def copy_out(j, dst, src, lap=0):
                full(act, j, lap)
                A(dst, src, ACT.Copy).then_inc(psum_free[j % 4], 1)
                act.wait_ge(psum_free[j % 4], free_value(j, lap))

            def projected(J, e, lap):
                q, k = hb[e]["q"][0:QK, :], hb[e]["k"][0:NOPE, :]
                copy_out(J.q[e], two(q), halves(J.q[e], (0, QK)), lap)
                A(sq[0:QK, 2 * e, :], q, ACT.Square).then_inc(s_qsq, 1)
                full(act, J.kn[e], lap)
                A(hb[e]["wt"][0:NOPE, :], flat(J.kn[e])[0:NOPE, 512:512 + P], ACT.Copy).then_inc(s_wt, 1)
                A(k, flat(J.kn[e])[0:NOPE, 0:NP], ACT.Copy).then_inc(psum_free[J.kn[e] % 4], 1)
                act.wait_ge(psum_free[J.kn[e] % 4], free_value(J.kn[e], lap))
                A(sq[0:NOPE, 4 + 2 * e, 0:NP], k, ACT.Square).then_inc(s_ksq, 1)

            def head_rstd(J, e, lap):
                rstd(J.qms[e], 1, (0, QK), lap, sq[0:QK, 2 * e + 1, :]).then_inc(s_qrs, 1)
                r = sq[0:NOPE, 5 + 2 * e, 0:NP]
                full(act, J.kms[e], lap)
                A(r, flat(J.kms[e])[0:NOPE, 0:NP], ACT.Ln, bias=epsc[0:NOPE, :]).then_inc(psum_free[J.kms[e] % 4], 1)
                act.wait_ge(psum_free[J.kms[e] % 4], free_value(J.kms[e], lap))
                A(r, r, ACT.Exp, scale=-0.5).then_inc(s_krs, 1)

            def head_probs(J, e, pair):
                for n in range(4):
                    j = J.s[e][n]
                    act.wait_ge(s_nm, 8 * pair + 4 * e + n + 1)
                    A(hb[e]["p"][:, POFF[n]:POFF[n] + P * (n + 1)], flat(j)[:, 0:P * (n + 1)], ACT.Exp,
                      bias=hb[e]["nm"][:, n:n + 1], scale=SCALE, accum_out=hb[e]["l"][:, n:n + 1]).then_inc(psum_free[j % 4], 1)

            for e in range(2):
                projected(HEAD_FIRST, e, 0)
            def mixed(J, e, pair, lap):
                j = J.pv[e]
                full(act, j, lap)
                A(hT[VD * e:VD * e + VD, bass.ds(LT + pair, 1), 0:NP].rearrange("p o n -> p (o n)"),
                  flat(j)[VD * e:VD * e + VD, 0:NP], ACT.Copy).then_inc(psum_free[j % 4], 1)

            def values(J, e, lap):
                j = J.vw[e]
                full(act, j, lap)
                A(hb[e]["v"], flat(j)[:, 0:4 * VD], ACT.Copy).then_inc(psum_free[j % 4], 1)

            for e in range(2):
                head_rstd(HEAD_FIRST, e, 0)
            for e in range(2):
                values(HEAD_FIRST, e, 0)
            with act.Fori(0, HEAD_LAPS) as i:
                nc.scalar.preload_act_table_set("natural_log_exp_and_others")
                lap = HEAD_LAP.count // 4 * i
                for e in range(2):
                    head_probs(HEAD_LAP, e, i)
                for e in range(2):
                    projected(HEAD_LAP, e, lap)
                for e in range(2):
                    head_rstd(HEAD_LAP, e, lap)
                for e in range(2):
                    mixed(HEAD_LAP, e, i, lap)
                for e in range(2):
                    values(HEAD_LAP, e, lap)
            nc.scalar.preload_act_table_set("natural_log_exp_and_others")
            for e in range(2):
                head_probs(HEAD_LAST, e, HEAD_LAPS)
            for e in range(2):
                mixed(HEAD_LAST, e, HEAD_LAPS, 0)

            def rstd_keys(e, v):
                act.wait_ge(s_sqr, KTILES * v)
                A(ssd[e], ssd[e], ACT.Ln, bias=epsc, scale=1.0 / NOPE).then_inc(s_act2, 1)
                act.wait_ge(s_act2, v)
                A(ssd[e], ssd[e], ACT.Exp, scale=-0.5).then_inc(s_drs, 1)

            def probs(e, v):
                act.wait_ge(s_sh, v)
                A(snd[e], snd[e], ACT.Exp, scale=SCALE).then_inc(s_dp, 1)

            def latents(j, lap, g):
                full(act, j, lap)
                n = GT[g] * P
                A(turned[:, g % 3, 4 * P - n:5 * P], flat(j)[:, 4 * P - n:5 * P], ACT.Copy).then_inc(s_tT, 1)
                A(latH[:, g % 3, 4 * P - n:4 * P], flat(j)[:, 4 * P - n:4 * P], ACT.Copy).then_inc(psum_free[j % 4], 1)

            def unit(base, lap, e, v):
                for g in range(NG):
                    if g + 2 < NG:
                        latents(unit_job(base, "t", g + 2), lap, g + 2)
                    elif base != J_LAST:
                        latents(unit_job(base, "tn", g + 2 - NG), lap, g + 2 - NG)
                    for n in range(GT[g]):
                        c = 4 * g + n
                        j = unit_job(base, "k", c)
                        if base != J_DEC or c >= 3:
                            act.wait_ge(s_sqr, KTILES * (v - 1) + c - 2)
                        full(act, j, lap)
                        A(sqd[c % 3].rearrange("p (h n) -> p h n", h=2), ps[j % 4][:, :, 0:4 * NOPE], ACT.Square).then_inc(s_sqd, 1)
                    if base != J_DEC and g == 0:
                        rstd_keys(1 - e, v - 1)
                    if base != J_DEC and g == 2:
                        probs(1 - e, v - 1)

            for g in range(2):
                latents(J_FIRST_T + g, 0, g)
            unit(J_DEC, 0, 0, 1)
            with act.Fori(0, 3) as i:
                nc.scalar.preload_act_table_set("natural_log_exp_and_others")
                unit(J_UNIT1, 2 * UNIT // 4 * i, 1, 2 * i + 2)
                unit(J_UNIT1 + UNIT, 2 * UNIT // 4 * i, 0, 2 * i + 3)
            unit(J_LAST, 0, 1, 8)
            rstd_keys(1, NS)
            probs(1, NS)

            def out_high(m):
                act.wait_ge(s_wo[m % 3], 16 * (m // 3 + 1))
                if m >= 2:
                    full(act, J_WO[m - 2])
                A(woH[:, m % 2, :, :], woR[:, m % 3, :, :], ACT.Copy).then_inc(s_wohi, 1)

            act.wait_ge(s_mix, LT)
            for k in range(LT):
                A(mixed_high[k], hT[:, k, :], ACT.Copy).then_inc(s_mhi, 1)
            full(act, J_LAST + UJ["pv", 0])
            out_high(0)
            out_high(1)
            act.wait_ge(psum_free[J_VP % 4], free_value(J_VP))
            for k in range(LT):
                A(sq[:, k, :], hT[:, LT + k, :], ACT.Square).then_inc(s_sq, 1)

            act.wait_ge(s_mix, LT)
            rstd(J_NMLA, LW).then_inc(s_rs, 1)
            for k in range(LT, KT):
                act.wait_ge(s_mix, k + 1)
                A(mixed_high[k], hT[:, k, :], ACT.Copy).then_inc(s_mhi, 1)

            def up_high(c, g, loads, before=None, lap=0):
                act.wait_ge(s_wup[c], 32 * loads)
                if before is not None:
                    full(act, before, lap)
                A(wuH[:, KT * g:KT * g + KT, :], wup[:, c, KT * g:KT * g + KT, :], ACT.Copy).then_inc(s_whi, 1)

            for k in range(KT):
                if k + 2 < KT:
                    out_high(k + 2)
                act.wait_ge(s_x1, k + 1)
                A(sq[:, k, :], xT[:, k, :], ACT.Square).then_inc(s_sq, 1)
                if k == 3:
                    full(act, J_PVLAST + 1)
                    up_high(0, 0, 1)
                    up_high(0, 1, 1)
            act.wait_ge(s_mix, 2 * LT)
            rstd(J_N2, D).then_inc(s_rs, 1)
            for k in range(KT):
                if k < KT // 2:
                    act.wait_ge(s_hp, KT + k + 1)
                else:
                    act.wait_ge(s_hq, k + 1 - KT // 2)
                A(h2[:, k, 0:NP], h2[:, k, 0:NP], ACT.Identity, bias=modT[:, 3 * KT + k, 0:1], scale=gmod[:, k, 0:1]).then_inc(s_h, 1)
            act.wait_ge(s_pads, 2)

            def evacuate(m, i, e, g):
                act.wait_ge(s_cvfree, m + 1)
                j = J_UP + 2 * e + g
                full(act, j, i)
                A(two(UU[e % 2][:, g, 2:UW]), halves(j), ACT.Copy).then_inc(psum_free[j % 4], 1)

            def down_high(m):
                act.wait_ge(s_wdn[m % 2], 16 * (m // 2 + 1))
                full(act, J_UP + 2 * FT - 1 if m < 2 else J_DOWN[m - 2])
                if m == 1:
                    act.wait_ge(s_hid, FT)
                    act.wait_ge(s_ut, 2 * FT)
                for a, b in PIECES:
                    A(wdH[m % 2][:, a:b, :], wdn[:, m % 2, a:b, :], ACT.Copy).then_inc(s_whi, 1)

            def mlp(i, e, left):
                m = 2 * i + e
                if left >= 1:
                    up_high(1 - e, 1, i + 1 + e, J_UP + 2 * e + 1, i)
                else:
                    down_high(0)
                evacuate(m, i, e, 1)
                if left >= 2:
                    up_high(e, 0, i + 2, J_UP + 2 * e + 2, i)
                if left >= 1:
                    evacuate(m + 1, i, e + 1, 0)
                act.wait_ge(s_cv, m + 1)
                A(GE, CV[1], ACT.Gelu_apprx_tanh).then_inc(s_ge, 1)

            up_high(1, 0, 1, J_UP)
            evacuate(0, 0, 0, 0)
            with act.Fori(0, FT // 2 - 1) as i:
                mlp(i, 0, 2)
                mlp(i, 1, 2)
            mlp(FT // 2 - 1, 0, 1)
            mlp(FT // 2 - 1, 1, 0)
            for m in range(1, KT):
                down_high(m)
                if m >= 3 and m % 2 == 1:
                    if m > 3:
                        act.wait_ge(s_kept, 16 * (m - 3))
                    for n in (m - 3, m - 2):
                        j, w = J_FT[n], ft_width(n)
                        full(act, j)
                        A(ft_tok[:, D * (n % 2):D * (n % 2) + w], flat(j)[0:10, 0:w], ACT.Copy).then_inc(psum_free[j % 4], 1)
            for n in (1, 3):
                j = J_Y + n
                full(act, j)
                A(y_tok[n], flat(j), ACT.Copy).then_inc(psum_free[j % 4], 1)

        @block.vector
        def _(dve):
            V = nc.vector
            st = Steps(dve, s_dve)
            MUL, ADD, SUB = ALU.mult, ALU.add, ALU.subtract

            def copy_out(j, dst, src, ready=None):
                full(dve, j)
                V.tensor_copy(dst, src).then_inc(psum_free[j % 4], 1)
                dve.wait_ge(psum_free[j % 4], free_value(j))

            def mod_rows(n):
                full(dve, J_ROW[n])
                V.tensor_copy(rows9(n), flat(J_ROW[n])[0:9, :]).then_inc(psum_free[J_ROW[n] % 4], 1)

            def mod_columns(n):
                j, m = J_COL[n], 8 * n
                full(dve, j)
                V.tensor_tensor(modT[:, m:m + 8, :], flat(j)[:, 0:72].rearrange("p (m n) -> p m n", n=9),
                                pr("b_ada", m, 8).unsqueeze(2).to_broadcast([P, 8, 9]), ADD).then_inc(psum_free[j % 4], 1)

            st.did(V.memset(small[:, 0:1], EPS))
            st.did(V.memset(small[:, 1:2], 0.0))
            for k in range(KT):
                j = J_XT + k
                full(dve, j)
                V.tensor_copy(xT[:, k, :], flat(j)[:, 0:T]).then_inc(psum_free[j % 4], 1)
                if k == 3:
                    dve.wait_ge(s_silu, 1)
                    V.scalar_tensor_tensor(c_tok, c_th, 1.0, c_tok, ADD, MUL).then_inc(s_silu, 1)
            full(dve, J_C)
            V.tensor_scalar(cT[:, :, :], flat(J_C)[:, 0:72].rearrange("p (k n) -> p k n", n=9), 0.5, None, MUL).then_inc(psum_free[J_C % 4], 1)
            mod_rows(0)
            copy_out(J_PAR, par[:, :], flat(J_PAR)[:, 0:NROWS])
            copy_out(J_FPAR, fpar[:, :], flat(J_FPAR)[:, 0:8 * FT])
            full(dve, J_STATE)
            st.did(V.tensor_copy(stT[:, :], flat(J_STATE)[:, 0:96]))
            V.tensor_copy(h0T[:, :], flat(J_STATE)[:, 96:128]).then_inc(psum_free[J_STATE % 4], 1)
            dve.wait_ge(s_cst, 16)
            dve.wait_ge(s_pt, 64)
            V.tensor_scalar(row_of[:, :], page_of[:, :], 4.0, C("quarter", 1), MUL, ADD).then_inc(s_row, 1)
            dve.wait_ge(s_row, 1)
            for n in range(2):
                V.tensor_scalar(half_of[:, n, :], row_of[:, :], 2.0, float(n), MUL, ADD).then_inc(s_row, 1)
            lam = pr("lru_lambda", 0, 4)
            st.seq(V.tensor_scalar(small[:, 36:40], lam, -1.0, None, MUL))
            V.tensor_tensor(small[:, 4:8], small[:, 36:40], lam, ALU.max).then_inc(s_sp, 1)
            dve.wait_ge(s_sp, 2)
            u, z, acc, z2 = small[:, 8:12], small[:, 12:16], small[:, 16:20], small[:, 40:44]
            st.seq(V.tensor_scalar(acc, u, 2.0, None, ADD))
            st.seq(V.reciprocal(acc, acc))
            st.seq(V.tensor_tensor(z, u, acc, MUL))
            st.seq(V.tensor_tensor(z2, z, z, MUL))
            st.seq(V.tensor_scalar(acc, z2, 2.0 / 17, 2.0 / 15, MUL, ADD))
            for n in range(6, -1, -1):
                st.seq(V.tensor_tensor(acc, acc, z2, MUL))
                st.seq(V.tensor_scalar(acc, acc, 2.0 / (2 * n + 1), None, ADD))
            st.seq(V.tensor_tensor(acc, acc, z, MUL))
            st.seq(V.tensor_scalar(small[:, 36:40], small[:, 36:40], 0.0, None, ALU.max))
            st.seq(V.tensor_tensor(acc, acc, small[:, 36:40], ADD))
            st.did(V.tensor_scalar(small[:, 28:32], acc, 4.0, None, MUL))
            st.did(V.tensor_scalar(small[:, 32:36], acc, -4.0, None, MUL))
            v = st.did(V.tensor_scalar(small[:, 20:24], pr("lru_b_a", 0, 4), 0.5, None, MUL))
            st.need(v)
            V.tensor_scalar(small[:, 24:28], pr("lru_b_x", 0, 4), 0.5, None, MUL).then_inc(s_sp, 1)

            dve.wait_ge(s_rs, 1)
            for k in range(KT):
                V.tensor_tensor(h1[:, k, 0:NP], xT[:, k, 0:NP], rs[:, 0:NP], MUL).then_inc(s_hp, 1)
            mod_rows(1)
            mod_columns(0)
            mod_columns(1)
            for n in range(2):
                dve.wait_ge(psum_free[J_COL[n] % 4], free_value(J_COL[n]))
            st.seq(V.tensor_scalar(gmod[:, :, :], modT[:, KT:2 * KT, :], 1.0, None, ADD))
            V.tensor_tensor(gmod[:, :, :], gmod[:, :, :], pr("norm1_g", 0, KT).unsqueeze(2).to_broadcast([P, KT, 9]), MUL).then_inc(s_gain, 1)
            dve.wait_ge(s_gain, 1)
            dec = h1[:, :, NP:T]
            st.seq(V.tensor_tensor(dec, xT[:, :, NP:T], rs[:, NP:T].unsqueeze(1).to_broadcast([P, KT, NS]), MUL))
            st.seq(V.tensor_tensor(dec, dec, gmod[:, :, 1:9], MUL))
            st.seq(V.tensor_tensor(dec, dec, modT[:, 0:KT, 1:9], ADD))

            def split_normed(whole, low, base):
                for k in range(KT):
                    dve.wait_ge(s_h, base + k + 1)
                    V.tensor_copy(hH[:, k, :], whole[:, k, :]).then_inc(s_hhi, 1)
                    dve.wait_ge(s_hhi, base + k + 1)
                    V.tensor_tensor(low[:, k, :], whole[:, k, :], hH[:, k, :].bitcast(F32), SUB).then_inc(s_hlo, 1)

            split_normed(h1, h1L, 0)

            full(dve, J_WIN[0])
            v = st.did(V.memset(XX[:, :, 0:3], 0.0))
            for k in range(LT):
                j = J_WIN[k]
                full(dve, j)
                V.tensor_copy(two(XX[:, k, 3:3 + T]), halves(j)).then_inc(psum_free[j % 4], 1)
            st.need(v)
            for tap in range(4):
                for k in range(LT):
                    w = pr("lru_conv_w", 4 * tap + k)
                    x = XX[:, k, tap:tap + NP]
                    if tap == 0:
                        dve.wait_ge(psum_free[J_WIN[k] % 4], free_value(J_WIN[k]))
                        v = st.did(V.tensor_scalar(XC[:, k, 0:NP], x, w, pr("lru_conv_b", k), MUL, ADD))
                    else:
                        v = st.did(V.scalar_tensor_tensor(XC[:, k, 0:NP], x, w, XC[:, k, 0:NP], MUL, ADD))
                st.need(v)
            dec, tmp = XC[:, :, NP:T], AA[:, :, 0:NS]
            for tap in range(4):
                w = pr("lru_conv_w", 4 * tap, 4).unsqueeze(2).to_broadcast([P, LT, NS])
                x = st4[:, :, :, tap] if tap < 3 else XX[:, :, 3 + NP:3 + T]
                st.seq(V.tensor_tensor(tmp, x, w, MUL))
                other = pr("lru_conv_b", 0, 4).unsqueeze(2).to_broadcast([P, LT, NS]) if tap == 0 else dec
                ins = V.tensor_tensor(dec, tmp, other, ADD)
                if tap < 3:
                    st.seq(ins)
                else:
                    ins.then_inc(s_xc, 4)
            for k in range(LT):
                j = J_GATE + LT + k
                dve.wait_ge(psum_free[j % 4], free_value(j))
            dve.wait_ge(s_xc, 4)
            v = st.did(V.scalar_tensor_tensor(TI[:, :, :], TI[:, :, :], 1.0, XC[:, :, :], ADD, MUL))
            dve.wait_ge(s_ta, 4)
            V.tensor_scalar(TA[:, :, :], TA[:, :, :], 1e-18, None, ALU.max).then_inc(s_tiny, 1)
            dve.wait_ge(s_lru, 1)
            V.scalar_tensor_tensor(TA[:, :, :], TA[:, :, :], LN2, sq[:, 4:8, :], ADD, SUB).then_inc(s_tiny, 1)
            dve.wait_ge(s_lru, 2)
            st.seq(V.memset(TA[:, :, 0:1], 1.0))
            st.seq(V.scalar_tensor_tensor(TI[:, :, :], TI[:, :, :], 0.5, TA[:, :, :], MUL, MUL))
            for k in range(LT):
                v = st.did(V.tensor_tensor_scan(TA[:, k, 0:NP], AA[:, k, 0:NP], TI[:, k, 0:NP], 0.0, MUL, ADD))
            v = st.did(V.tensor_tensor(TA[:, :, NP:T], AA[:, :, NP:T], h04, MUL))
            st.need(v)
            V.tensor_tensor(TA[:, :, NP:T], TA[:, :, NP:T], TI[:, :, NP:T], ADD).then_inc(s_lrud, 1)
            dve.wait_ge(s_lrud, 1)
            dve.wait_ge(s_rs, 2)
            for k in range(2):
                V.scalar_tensor_tensor(qlT[:, k, :], qlT[:, k, :], pr("q_lora_norm_g", k), sq[:, 0, :], MUL, MUL).then_inc(s_ql, 1)
            dve.wait_ge(s_rs, 3)
            V.scalar_tensor_tensor(kvT[:, :], kvT[:, :], pr("kv_lora_norm_g"), sq[:, 1, :], MUL, MUL).then_inc(s_kvn, 1)
            dve.wait_ge(s_rs, 4)
            R = (NOPE, QK)
            kr = krT[NOPE:QK, :]
            V.scalar_tensor_tensor(kr, kr, pr("gk", 0, 1, R), sq[NOPE:QK, 2, :], MUL, MUL).then_inc(s_kr, 1)
            dve.wait_ge(s_kr, 1)
            j = J_KR[1]
            full(dve, j)
            V.tensor_tensor(two(qrot[NOPE:QK, :]), halves(j, R), two(C("sin", T, R)), MUL).then_inc(psum_free[j % 4], 1)
            st.seq(V.tensor_tensor(kr, kr, C("cos", T, R), MUL))
            dve.wait_ge(psum_free[j % 4], free_value(j))
            V.tensor_tensor(kr, kr, qrot[NOPE:QK, :], ADD).then_inc(s_kr, 1)
            dve.wait_ge(s_g, 1)
            V.tensor_tensor(XC[:, :, :], TA[:, :, :], GG[:, :, :], MUL).then_inc(s_lrud, 1)
            mod_rows(2)
            mod_rows(3)
            mod_columns(2)
            dve.wait_ge(s_rs, 5)
            for k in range(LT):
                V.scalar_tensor_tensor(hT[:, k, :], XC[:, k, :], pr("lru_out_norm_g", k), rs[:, :], MUL, MUL).then_inc(s_mix, 1)
            mod_rows(4)
            mod_columns(3)
            for a in range(5):
                j = J_LOUT + a
                n = P if a < 4 else NS
                full(dve, j)
                V.tensor_copy(otok[0:n, a, :], flat(j)[0:n, 0:KV + ROPE]).then_inc(psum_free[j % 4], 1)
            for n, w in enumerate((9, 11)):
                j = J_LOUT + 5 + n
                full(dve, j)
                V.tensor_copy(lout[0:w, n, :], flat(j)[0:w, 0:LW]).then_inc(psum_free[j % 4], 1)

            mod_rows(5)
            mod_columns(4)
            mod_columns(5)
            for e in range(2):
                V.tensor_copy(hb[e]["k"][NOPE:QK, :], krT[NOPE:QK, 0:NP]).then_inc(s_krk, 1)
            N0 = (0, NOPE)

            def normed(e, pair):
                q, k = hb[e]["q"][0:QK, :], hb[e]["k"][0:NOPE, :]
                nth = 2 * pair + e + 1
                dve.wait_ge(s_qrs, nth)
                V.scalar_tensor_tensor(q, q, pr("gq", 0, 1, (0, QK)), sq[0:QK, 2 * e + 1, :], MUL, MUL).then_inc(s_qn, 1)
                dve.wait_ge(s_krs, nth)
                V.scalar_tensor_tensor(k, k, pr("gk", 0, 1, N0), sq[0:NOPE, 5 + 2 * e, 0:NP], MUL, MUL).then_inc(s_kn, 1)
                dve.wait_ge(s_qn, nth)
                V.tensor_scalar(hb[e]["gq"][0:NOPE, :], hb[e]["q"][0:NOPE, NP:T], pr("gk", 0, 1, N0), None, MUL).then_inc(s_gq, 1)

            def rotated(J, e, pair, lap):
                qr = hb[e]["q"][NOPE:QK, :]
                j = J.qrot[e]
                full(dve, j, lap)
                V.tensor_tensor(two(qrot[NOPE:QK, :]), halves(j, R), two(C("sin", T, R)), MUL).then_inc(psum_free[j % 4], 1)
                st.seq(V.tensor_tensor(qr, qr, C("cos", T, R), MUL))
                dve.wait_ge(psum_free[j % 4], free_value(j, lap))
                st.seq(V.tensor_tensor(qr, qr, qrot[NOPE:QK, :], ADD))
                V.tensor_copy(QRS[NOPE:QK, :, bass.ds(2 * pair + e, 1)], hb[e]["q"][NOPE:QK, NP:T].unsqueeze(2)).then_inc(s_qr, 1)

            def through_keys(J, e, pair, lap):
                j = J.qa[e]
                full(dve, j, lap)
                V.tensor_copy(QA[:, :, bass.ds(2 * pair + e, 1)], flat(j)[:, 0:NS].unsqueeze(2)).then_inc(psum_free[j % 4], 1)

            def row_max(J, e, pair, lap):
                b = hb[e]
                for n in range(4):
                    j = J.s[e][n]
                    full(dve, j, lap)
                    d = flat(j)[:, P * n:P * n + P]
                    V.tensor_tensor(d, d, C("mask"), ADD).then_inc(s_msk, 1)
                    dve.wait_ge(s_msk, 8 * pair + 4 * e + n + 1)
                    st.seq(V.tensor_reduce(b["rl"][:, n:n + 1], flat(j)[:, 0:P * (n + 1)], AX.X, ALU.max))
                    V.tensor_scalar(b["nm"][:, n:n + 1], b["rl"][:, n:n + 1], -SCALE, None, MUL).then_inc(s_nm, 1)

            def norm_probs(J, e, lap):
                b = hb[e]
                for n in range(4):
                    dve.wait_ge(psum_free[J.s[e][n] % 4], free_value(J.s[e][n], lap))
                st.seq(V.reciprocal(b["rl"], b["l"]))
                for n in range(4):
                    p = b["p"][:, POFF[n]:POFF[n] + P * (n + 1)]
                    V.tensor_scalar(p, p, b["rl"][:, n:n + 1], None, MUL).then_inc(s_pn, 1)

            def turned_probs(J, e, lap):
                for n in range(4):
                    j = J.p[e][n]
                    full(dve, j, lap)
                    V.tensor_copy(hb[e]["pt"][:, 0:n + 1, P * n:P * n + P],
                                  flat(j)[:, 0:P * (n + 1)].rearrange("p (a n) -> p a n", n=P)).then_inc(psum_free[j % 4], 1)

            J = HEAD_FIRST
            for e in range(2):
                normed(e, 0)
            for e in range(2):
                rotated(J, e, 0, 0)
            for e in range(2):
                through_keys(J, e, 0, 0)
            with dve.Fori(0, HEAD_LAPS) as i:
                J, lap = HEAD_LAP, HEAD_LAP.count // 4 * i
                st.enter(i, 14)
                for e in range(2):
                    row_max(J, e, i, lap)
                for e in range(2):
                    norm_probs(J, e, lap)
                turned_probs(J, 0, lap)
                for e in range(2):
                    normed(e, i + 1)
                turned_probs(J, 1, lap)
                for e in range(2):
                    rotated(J, e, i + 1, lap)
                for e in range(2):
                    through_keys(J, e, i + 1, lap)
            st.leave(HEAD_LAPS)
            J = HEAD_LAST
            for e in range(2):
                row_max(J, e, HEAD_LAPS, 0)
            for e in range(2):
                norm_probs(J, e, 0)
            for e in range(2):
                turned_probs(J, e, 0)

            full(dve, J_SPREAD)
            dve.wait_ge(s_bdz, 2)
            src = flat(J_SPREAD)[:, 0:NS * HEADS].rearrange("p (b h) -> p b h", b=NS)
            for n in range(4):
                rows = slice(ROPE * n, ROPE * n + ROPE)
                ins = V.tensor_copy(QBD[rows, :, n, :], src[rows, :, :])
                st.did(ins) if n < 3 else ins.then_inc(psum_free[J_SPREAD % 4], 1)
            st.need(st.n)
            dve.wait_ge(psum_free[J_SPREAD % 4], free_value(J_SPREAD))
            dve.sem_inc(s_qbd, 1)

            def by_key(x):
                return x.rearrange("p (c h) -> p c h", h=HEADS)

            def scores_max(e, v):
                dve.wait_ge(s_drs, v)
                dve.wait_ge(s_snc, NG * v)
                V.tensor_tensor(snd[e], snd[e], ssd[e], MUL).then_inc(s_sm, 1)
                dve.wait_ge(s_sm, 3 * v - 2)
                V.tensor_tensor(snd[e], snd[e], srd[e], ADD).then_inc(s_sm, 1)
                dve.wait_ge(s_sm, 3 * v - 1)
                last = snd[e][:, HEADS * PAGES:HEADS * KTILES]
                V.tensor_scalar(last, last, C("tail", 1), None, ADD).then_inc(s_sm, 1)
                dve.wait_ge(s_sm, 3 * v)
                V.tensor_reduce(mx[e], snd[e].rearrange("p (c h) -> p h c", h=HEADS), AX.X, ALU.max).then_inc(s_mx, 1)

            def shift(e, v):
                dve.wait_ge(s_am, v)
                V.tensor_tensor(by_key(snd[e]), by_key(snd[e]), mx[e].unsqueeze(1).to_broadcast([P, KTILES, HEADS]), SUB).then_inc(s_sh, 1)

            def prob_sums(e, v):
                dve.wait_ge(s_dp, v)
                V.tensor_reduce(pd[e], snd[e].rearrange("p (c h) -> p h c", h=HEADS), AX.X, ADD).then_inc(s_pd, 1)

            def finish(j, lap, s):
                full(dve, j, lap)
                full(dve, j + 1, lap)
                V.reciprocal(rden, flat(j + 1)[0:HEADS, 0:1]).then_inc(psum_free[(j + 1) % 4], 1)
                dve.wait_ge(psum_free[(j + 1) % 4], free_value(j + 1, lap))
                row = OLR[:, bass.ds(s, 1), :].rearrange("p o d -> p (o d)")
                V.tensor_scalar(row, flat(j)[0:HEADS, 0:KV], rden, None, MUL).then_inc(psum_free[j % 4], 1)

            def split_queries(e, s, v):
                q = QA[:, bass.ds(s, 1), :].rearrange("p o h -> p (o h)").rearrange("p (g h) -> p g h", g=2)
                V.tensor_copy(kwH[:, e, :, 4 * NOPE:KWW], q).then_inc(s_kwq, 1)
                dve.wait_ge(s_kwq, 2 * v - 1)
                V.tensor_tensor(kwL[:, e, :, 4 * NOPE:KWW], q, kwH[:, e, :, 4 * NOPE:KWW].bitcast(F32), SUB).then_inc(s_kwq, 1)

            def unit(base, lap, e, s_before, s_next, v):
                for g in range(NG):
                    for n in range(GT[g]):
                        c = 4 * g + n
                        j = unit_job(base, "k", c)
                        dve.wait_ge(s_sqd, KTILES * (v - 1) + c + 1)
                        if n == 0:
                            w = HEADS * GT[g]
                            V.tensor_copy(srd[e][:, HEADS * c:HEADS * c + w], flat(j)[:, KWW:KWW + w]).then_inc(s_snc, 1)
                        V.tensor_copy(snd[e][:, HEADS * c:HEADS * c + HEADS].rearrange("p (g h) -> p g h", g=2),
                                      ps[j % 4][:, :, 4 * NOPE:KWW]).then_inc(psum_free[j % 4], 1)
                        V.tensor_reduce(ssd[e][:, HEADS * c:HEADS * c + HEADS], sqd[c % 3].rearrange("p (m d) -> p m d", d=NOPE),
                                        AX.X, ADD).then_inc(s_sqr, 1)
                        if base != J_DEC and (g, n) == (1, 1):
                            scores_max(1 - e, v - 1)
                        if base != J_DEC and (g, n) == (2, 1):
                            shift(1 - e, v - 1)
                    if base != J_DEC:
                        if g == 3:
                            prob_sums(1 - e, v - 1)
                        if g == PV_AT:
                            finish(unit_job(base, "pv", 0), lap, s_before)
                    if g == 6 and s_next is not None:
                        split_queries(1 - e, s_next, v + 1)
                dve.wait_ge(psum_free[j % 4], free_value(j, lap))

            dve.wait_ge(s_wkn, 16)
            wk2 = wkn[:, :].rearrange("p (g n) -> p g n", g=2)
            for e in range(2):
                V.tensor_copy(kwH[:, e, :, 0:4 * NOPE], wk2).then_inc(s_kw, 1)
            dve.wait_ge(s_kw, 2)
            for e in range(2):
                V.tensor_tensor(kwL[:, e, :, 0:4 * NOPE], wk2, kwH[:, e, :, 0:4 * NOPE].bitcast(F32), SUB).then_inc(s_kw, 1)
            split_queries(0, 0, 1)
            unit(J_DEC, 0, 0, None, 1, 1)
            with dve.Fori(0, 3) as i:
                unit(J_UNIT1, 2 * UNIT // 4 * i, 1, 2 * i, 2 * i + 2, 2 * i + 2)
                unit(J_UNIT1 + UNIT, 2 * UNIT // 4 * i, 0, 2 * i + 1, 2 * i + 3, 2 * i + 3)
            unit(J_LAST, 0, 1, 6, None, 8)
            scores_max(1, NS)
            shift(1, NS)
            prob_sums(1, NS)
            def low_part(k):
                dve.wait_ge(s_mhi, k + 1)
                V.tensor_tensor(mixed_low[k], hT[:, k, :], mixed_high[k].bitcast(F32), SUB).then_inc(s_mlo, 1)

            def out_low(m):
                dve.wait_ge(s_wohi, m + 1)
                V.tensor_tensor(woL[:, m % 2, :, :], woR[:, m % 3, :, :], woH[:, m % 2, :, :].bitcast(F32), SUB).then_inc(s_wolo, 1)

            dve.wait_ge(s_out, 16 * 10)
            for k in range(LT):
                low_part(k)
            out_low(0)
            out_low(1)
            finish(J_PVLAST, 0, NS - 1)
            full(dve, J_OL)
            V.tensor_copy(OL[:, :, :].rearrange("p b h -> p (b h)"), flat(J_OL)[:, 0:NS * HEADS]).then_inc(psum_free[J_OL % 4], 1)
            full(dve, J_VP)
            V.tensor_copy(hT[:, LT:KT, NP:T], flat(J_VP)[:, 0:LT * NS].rearrange("p (k n) -> p k n", n=NS)).then_inc(psum_free[J_VP % 4], 1)

            dve.wait_ge(s_rs, 6)
            for k in range(LT + 1):
                if k < LT:
                    V.scalar_tensor_tensor(hT[:, LT + k, :], hT[:, LT + k, :], pr("mla_out_norm_g", k), rs[:, :], MUL, MUL).then_inc(s_mix, 1)
                if k > 0:
                    low_part(LT + k - 1)

            def residual(j, m, gate, done, nth):
                g = modT[:, gate + m, 0:1]
                full(dve, j)
                b0, b1 = ps[j % 4][:, 0, 0:H], ps[j % 4][:, 1, 0:NP - H]
                V.tensor_tensor(d8[:, m, :], ps[j % 4][:, 1, NP - H:H], modT[:, gate + m, 1:9], MUL).then_inc(s_d8, 1)
                v = st.did(V.scalar_tensor_tensor(xT[:, m, 0:H], b0, g, xT[:, m, 0:H], MUL, ADD))
                V.scalar_tensor_tensor(xT[:, m, H:NP], b1, g, xT[:, m, H:NP], MUL, ADD).then_inc(psum_free[j % 4], 1)
                dve.wait_ge(s_d8, nth)
                st.need(v)
                dve.wait_ge(psum_free[j % 4], free_value(j))
                V.tensor_tensor(xT[:, m, NP:T], xT[:, m, NP:T], d8[:, m, :], ADD).then_inc(done, 1)

            def up_low(c, g, nth):
                dve.wait_ge(s_whi, nth)
                V.tensor_tensor(wuL[:, KT * g:KT * g + KT, :], wup[:, c, KT * g:KT * g + KT, :],
                                wuH[:, KT * g:KT * g + KT, :].bitcast(F32), SUB).then_inc(s_wlo, 1)

            for m in range(KT):
                residual(J_WO[m], m, 2 * KT, s_x1, m + 1)
                if m + 2 < KT:
                    out_low(m + 2)
                if m == 4:
                    up_low(0, 0, 1)
                    up_low(0, 1, 2)
            st.seq(V.tensor_scalar(gmod[:, :, :], modT[:, 4 * KT:5 * KT, :], 1.0, None, ADD))
            st.seq(V.tensor_tensor(gmod[:, :, :], gmod[:, :, :], pr("norm2_g", 0, KT).unsqueeze(2).to_broadcast([P, KT, 9]), MUL))
            dve.wait_ge(s_rs, 7)
            dec = h2[:, :, NP:T]
            for k in range(KT // 2):
                V.tensor_tensor(h2[:, k, 0:NP], xT[:, k, 0:NP], rs[:, 0:NP], MUL).then_inc(s_hp, 1)
                if k > 0:
                    st.need(st.n)
                if k == 0:
                    st.did(V.tensor_tensor(dec, xT[:, :, NP:T], rs[:, NP:T].unsqueeze(1).to_broadcast([P, KT, NS]), MUL))
                elif k == 1:
                    st.did(V.tensor_tensor(dec, dec, gmod[:, :, 1:9], MUL))
                elif k == 2:
                    st.seq(V.tensor_tensor(dec, dec, modT[:, 3 * KT:4 * KT, 1:9], ADD))
            split_normed(h2, hL, KT)
            full(dve, J_FST)
            V.tensor_copy(FS[:, :, :].rearrange("p m n -> p (m n)"), flat(J_FST)[:, 0:4 * FT * NS]).then_inc(psum_free[J_FST % 4], 1)
            dve.wait_ge(psum_free[J_FST % 4], free_value(J_FST))
            for e in range(2):
                V.memset(UU[e][:, :, 0:2], 0.0).then_inc(s_pads, 1)
            dve.sem_inc(s_cvfree, 2)

            def down_low(m):
                for n, (a, b) in enumerate(PIECES):
                    dve.wait_ge(s_whi, 2 * FT + 3 * m + n + 1)
                    V.tensor_tensor(wdL[m % 2][:, a:b, :], wdn[:, m % 2, a:b, :],
                                    wdH[m % 2][:, a:b, :].bitcast(F32), SUB).then_inc(s_wlo, 1)

            def mlp(i, e, left):
                m = 2 * i + e
                if left >= 1:
                    up_low(1 - e, 1, 2 * m + 4)
                else:
                    down_low(0)
                for g in range(2):
                    j = J_UP + 2 * e + g
                    dve.wait_ge(psum_free[j % 4], free_value(j, i))
                    u, cv = UU[e][:, g, :], CV[g]
                    w = [fpar[:, bass.ds(2 * FT * n + FT * g + m, 1)] for n in range(4)]
                    fs = FS[:, bass.ds(FT * g + m, 1), :].rearrange("p o (b r) -> p (o b) r", r=2)
                    st.did(V.tensor_scalar(cv[:, 0:NP], u[:, 0:NP], w[0], w[3], MUL, ADD))
                    st.seq(V.tensor_scalar(cv[:, NP:T], fs[:, :, 0], w[0], w[3], MUL, ADD))
                    st.did(V.scalar_tensor_tensor(cv[:, 0:NP], u[:, 1:1 + NP], w[1], cv[:, 0:NP], MUL, ADD))
                    st.seq(V.scalar_tensor_tensor(cv[:, NP:T], fs[:, :, 1], w[1], cv[:, NP:T], MUL, ADD))
                    st.seq(V.scalar_tensor_tensor(cv[:, :], u[:, 2:2 + T], w[2], cv[:, :], MUL, ADD))
                dve.sem_inc(s_cv, 1)
                if left >= 2:
                    up_low(e, 0, 2 * m + 5)
                dve.wait_ge(s_ge, m + 1)
                st.seq(V.tensor_tensor(CV[0], CV[0], GE, MUL))
                hi, lo = [x[:, bass.ds(m, 1), :].rearrange("p o n -> p (o n)") for x in (actH, actL)]
                st.seq(V.tensor_copy(hi, CV[0]))
                V.tensor_tensor(lo, CV[0], hi.bitcast(F32), SUB).then_inc(s_hid, 1)
                dve.wait_ge(s_hid, m + 1)
                dve.wait_ge(s_ut, 2 * m + 2)
                dve.sem_inc(s_cvfree, 1)

            up_low(1, 0, 3)
            with dve.Fori(0, FT // 2 - 1) as i:
                st.enter(i, 24)
                mlp(i, 0, 2)
                mlp(i, 1, 2)
            st.leave(FT // 2 - 1)
            mlp(FT // 2 - 1, 0, 1)
            mlp(FT // 2 - 1, 1, 0)

            down_low(1)
            for m in range(KT):
                residual(J_DOWN[m], m, 5 * KT, s_x2, KT + m + 1)
                if m + 2 < KT:
                    down_low(m + 2)
            for n in (0, 2, 4):
                j = J_Y + n
                w = P if n < 4 else NS
                full(dve, j)
                V.tensor_copy(y_tok[n][0:w, :], flat(j)[0:w, :]).then_inc(psum_free[j % 4], 1)


_INS = ["x_prompt", "x_sample", "cache_kv_latent", "cache_k_rope", "state_lru_h", "state_lru_conv", "state_ffn_conv",
        "page_table", "c_prompt", "c_sample", "w_ada", "b_ada", "norm1_g", "w_in", "lru_conv_w", "lru_conv_b", "lru_w_a",
        "lru_b_a", "lru_w_x", "lru_b_x", "lru_lambda", "q_lora_norm_g", "w_uq", "q_nope_norm_g", "q_rope_norm_g",
        "kv_lora_norm_g", "k_rope_norm_g", "w_ukv", "k_nope_norm_g", "lru_out_norm_g", "mla_out_norm_g", "w_o", "norm2_g",
        "w_up", "ffn_conv_w", "ffn_conv_b", "w_down"]
_OUTS = [("o_y_p", (1, NP, D)), ("o_y_s", (NS, 1, D)), ("o_kv_p", (1, 1, NP, KV)), ("o_kr_p", (1, 1, NP, ROPE)),
         ("o_lru_h_p", (1, 1, LW)), ("o_lru_conv_p", (1, 1, 3, LW)), ("o_ffn_conv_p", (1, 1, 2, 2 * FF)),
         ("o_kv_s", (1, NS, 1, KV)), ("o_kr_s", (1, NS, 1, ROPE)), ("o_lru_h_s", (1, NS, LW)),
         ("o_lru_conv_s", (1, NS, 3, LW)), ("o_ffn_conv_s", (1, NS, 2, 2 * FF))]


def kernel(**inputs):
    import numpy as np
    import concourse.bacc as bacc
    from concourse.bass_utils import run_bass_kernel_spmd as run

    nc = bacc.Bacc("TRN2", target_bir_lowering=False, num_devices=1)
    arrays, t = {}, {}
    for name in _INS:
        arrays[name] = np.ascontiguousarray(inputs[name])
    arrays["consts"] = constants()
    for name, a in arrays.items():
        t[name] = nc.dram_tensor(name, a.shape, mybir.dt.from_np(a.dtype), kind="ExternalInput").ap()
    for name, shape in _OUTS:
        t[name] = nc.dram_tensor(name, shape, F32, kind="ExternalOutput").ap()
    build(nc, t)
    r = run(nc, [arrays], core_ids=[0])
    return tuple(r.results[0][name] for name, _ in _OUTS)
```
